# Optimizing a Trainium2 kernel written in Bass

```python
import jax, jax.numpy as jnp
from jax import lax
import numpy as np

D_MODEL = 1024
BATCH = 1
SEQ = 1024
DEPTH = 2
DEC_BATCH = 8
DEC_SEQ = 8
PAST_LEN = 4096
PAGE_SIZE = 128

N_A = DEPTH // 2
N_B = DEPTH - N_A
H_RET = 6
DK_RET = 64
DV_RET = 128
H_FOX = 12
DH = 64
H_MEM = 4
N_MEM = 256
D_RET_QK = H_RET * DK_RET
D_RET_V = H_RET * DV_RET
D_FOX = H_FOX * DH
D_MEMQ = H_MEM * DH
D_IN_A = 2 * D_RET_QK + 2 * D_RET_V + D_MEMQ
D_IN_B = D_FOX + D_MEMQ
D_CAT_A = D_RET_V + D_MEMQ
D_CAT_B = D_FOX + D_MEMQ
D_KV_SH = 2 * D_FOX + H_FOX
D_FF = 2816
CONV_W = 3
RET_CHUNK = 128
Q_BLOCK = 128
ROPE_BASE = 10000.0
EPS = 1e-6

kernel_name = 'yoco_retention_fox_convffn_memory_step'

def rmsnorm(x, g):
    xf = x.astype(jnp.float32)
    y = xf * lax.rsqrt(jnp.mean(xf * xf, axis=-1, keepdims=True) + EPS)
    return (y * g.astype(jnp.float32)).astype(x.dtype)

def head_norm(o):
    c = o - jnp.mean(o, axis=-1, keepdims=True)
    return c * lax.rsqrt(jnp.mean(c * c, axis=-1, keepdims=True) + EPS)

def rotary(x, pos):
    half = x.shape[-1] // 2
    inv = ROPE_BASE ** (-jnp.arange(half, dtype=jnp.float32) / half)
    ang = pos.astype(jnp.float32)[:, None] * inv[None, :]
    cos = jnp.cos(ang)[None, :, None, :]
    sin = jnp.sin(ang)[None, :, None, :]
    xf = x.astype(jnp.float32)
    x1, x2 = xf[..., :half], xf[..., half:]
    return jnp.concatenate([x1 * cos - x2 * sin, x1 * sin + x2 * cos], axis=-1).astype(x.dtype)

def retention(q, k, v, S0):
    B, L, H, _ = q.shape
    Dv = v.shape[-1]
    C = RET_CHUNK if L % RET_CHUNK == 0 else L
    n = L // C
    log_gamma = jnp.log1p(-(2.0 ** (-5.0 - jnp.arange(H, dtype=jnp.float32))))
    idx = jnp.arange(C, dtype=jnp.float32)
    rel = idx[:, None] - idx[None, :]
    dmask = jnp.where(rel >= 0, jnp.exp(log_gamma[:, None, None] * jnp.maximum(rel, 0.0)), 0.0)
    qdec = jnp.exp(log_gamma[None, :] * (idx[:, None] + 1.0))
    kdec = jnp.exp(log_gamma[None, :] * (C - 1.0 - idx[:, None]))
    sdec = jnp.exp(log_gamma * C)

    def to_chunks(t):
        return t.astype(jnp.float32).reshape(B, n, C, H, t.shape[-1]).transpose(1, 0, 2, 3, 4)

    def step(S, qkv):
        qc, kc, vc = qkv
        inner = jnp.einsum('bihd,bjhd->bhij', qc, kc) * dmask[None]
        o = (jnp.einsum('bhij,bjhe->bihe', inner, vc)
             + jnp.einsum('bihd,bhde->bihe', qc * qdec[None, :, :, None], S))
        S = sdec[None, :, None, None] * S + jnp.einsum('bjhd,bjhe->bhde', kc * kdec[None, :, :, None], vc)
        return S, o

    S, o = lax.scan(step, S0.astype(jnp.float32), (to_chunks(q), to_chunks(k), to_chunks(v)))
    o = o.transpose(1, 0, 2, 3, 4).reshape(B, L, H, Dv)
    return o, S

def mem_attend(qm, mk, mv):
    B, L, _ = qm.shape
    q = qm.reshape(B, L, H_MEM, DH)
    s = jnp.einsum('blhd,bmhd->bhlm', q, mk.astype(q.dtype)).astype(jnp.float32) * (DH ** -0.5)
    p = jax.nn.softmax(s, axis=-1).astype(q.dtype)
    return jnp.einsum('bhlm,bmhd->blhd', p, mv.astype(q.dtype)).reshape(B, L, D_MEMQ)

def fox_attention(q, k, v, Fq, Fk, q_pos, k_pos):
    B, Lq, H, Dh = q.shape
    FkT = jnp.transpose(Fk.astype(jnp.float32), (0, 2, 1))

    def block(args):
        qb, Fqb, qpb = args
        s = jnp.einsum('bqhd,bkhd->bhqk', qb, k).astype(jnp.float32) * (Dh ** -0.5)
        s = s + jnp.transpose(Fqb.astype(jnp.float32), (0, 2, 1))[..., :, None] - FkT[:, :, None, :]
        s = jnp.where((k_pos[None, :] <= qpb[:, None])[None, None], s, -jnp.inf)
        p = jax.nn.softmax(s, axis=-1).astype(v.dtype)
        return jnp.einsum('bhqk,bkhd->bqhd', p, v)

    Qb = Q_BLOCK if Lq % Q_BLOCK == 0 else Lq
    nb = Lq // Qb
    qs = q.reshape(B, nb, Qb, H, Dh).transpose(1, 0, 2, 3, 4)
    Fqs = Fq.reshape(B, nb, Qb, H).transpose(1, 0, 2, 3)
    qps = q_pos.reshape(nb, Qb)
    out = lax.map(block, (qs, Fqs, qps))
    return out.transpose(1, 0, 2, 3, 4).reshape(B, Lq, H, Dh)

def retention_mixer(a, w_in, w_out, mk, mv, S0, pos):
    B, L, _ = a.shape
    z = a @ w_in
    o1 = D_RET_QK
    o2 = 2 * D_RET_QK
    o3 = o2 + D_RET_V
    o4 = o3 + D_RET_V
    q = rotary(z[..., :o1].reshape(B, L, H_RET, DK_RET), pos)
    k = rotary(z[..., o1:o2].reshape(B, L, H_RET, DK_RET), pos) * (DK_RET ** -0.5)
    v = z[..., o2:o3].reshape(B, L, H_RET, DV_RET)
    g = z[..., o3:o4]
    r, S = retention(q, k, v, S0)
    r = (jax.nn.silu(g.astype(jnp.float32)) * head_norm(r).reshape(B, L, D_RET_V)).astype(a.dtype)
    m = mem_attend(z[..., o4:], mk, mv)
    return jnp.concatenate([r, m], axis=-1) @ w_out, S

def fox_mixer(a, w_in, w_out, keys, vals, Fq, Fk, q_pos, k_pos, mk, mv):
    B, L, _ = a.shape
    z = a @ w_in
    qf = z[..., :D_FOX].reshape(B, L, H_FOX, DH)
    o = fox_attention(qf, keys.astype(qf.dtype), vals.astype(qf.dtype), Fq, Fk, q_pos, k_pos).reshape(B, L, D_FOX)
    m = mem_attend(z[..., D_FOX:], mk, mv)
    return jnp.concatenate([o, m], axis=-1) @ w_out

def shared_kv(h, g_kv, w_kv, b_f):
    B, L, _ = h.shape
    z = rmsnorm(h, g_kv) @ w_kv
    k = z[..., :D_FOX].reshape(B, L, H_FOX, DH)
    v = z[..., D_FOX:2 * D_FOX].reshape(B, L, H_FOX, DH)
    logf = jax.nn.log_sigmoid((z[..., 2 * D_FOX:] + b_f).astype(jnp.float32))
    return k, v, logf

def conv_ffn(a, w_up, cw, cb, w_down, buf):
    L = a.shape[1]
    u = a @ w_up
    ext = jnp.concatenate([buf.astype(u.dtype), u], axis=1)
    c = cb
    for i in range(CONV_W):
        c = c + cw[i] * ext[:, i:i + L]
    gate, val = c[..., :D_FF], c[..., D_FF:]
    y = (jax.nn.gelu(gate, approximate=True) * val) @ w_down
    return y, ext[:, L:]

def trunk(x, pos, mem_k, mem_v, ret_state, conv_state, past_k, past_v, past_logf, p):
    L = x.shape[1]
    h = x
    new_ret, new_conv = [], []
    k_sh = v_sh = logf_sh = None
    keys = vals = F = Fq = k_pos = None
    for layer in range(DEPTH):
        a = rmsnorm(h, p['g_mix_pre'][layer])
        if layer < N_A:
            o, S = retention_mixer(a, p['w_in_a'][layer], p['w_out_a'][layer], mem_k[layer], mem_v[layer],
                                   ret_state[layer], pos)
            new_ret.append(S.astype(x.dtype))
        else:
            if layer == N_A:
                k_sh, v_sh, logf_sh = shared_kv(h, p['g_kv'], p['w_kv_shared'], p['b_f'])
                if past_k is None:
                    keys, vals, logf_all, k_pos = k_sh, v_sh, logf_sh, pos
                else:
                    past_len = past_k.shape[1]
                    keys = jnp.concatenate([past_k.astype(k_sh.dtype), k_sh], axis=1)
                    vals = jnp.concatenate([past_v.astype(v_sh.dtype), v_sh], axis=1)
                    logf_all = jnp.concatenate([past_logf.astype(jnp.float32), logf_sh], axis=1)
                    k_pos = jnp.arange(past_len + L, dtype=jnp.int32)
                F = jnp.cumsum(logf_all, axis=1)
                F = F - F[:, -1:]
                Fq = F[:, -L:]
            j = layer - N_A
            o = fox_mixer(a, p['w_in_b'][j], p['w_out_b'][j], keys, vals, Fq, F, pos, k_pos,
                          mem_k[layer], mem_v[layer])
        h = h + rmsnorm(o, p['g_mix_post'][layer])
        f, buf = conv_ffn(rmsnorm(h, p['g_ffn_pre'][layer]), p['w_ffn_up'][layer], p['conv_w'][layer],
                          p['conv_b'][layer], p['w_ffn_down'][layer], conv_state[layer])
        new_conv.append(buf)
        h = h + rmsnorm(f, p['g_ffn_post'][layer])
    return h, k_sh, v_sh, logf_sh, jnp.stack(new_ret), jnp.stack(new_conv)

def setup_inputs(seed: int = 0) -> dict:
    key = jax.random.key(seed)
    ks = jax.random.split(key, 32)
    n_pages = PAST_LEN // PAGE_SIZE
    n_phys = (DEC_BATCH * n_pages * 5) // 4

    def nrm(k, shape, scale=1.0):
        return scale * jax.random.normal(k, shape, jnp.float32)

    fox_bias_base = jnp.linspace(1.0, 6.0, H_FOX, dtype=jnp.float32)
    x_prompt = nrm(ks[0], (BATCH, SEQ, D_MODEL))
    x_sample = nrm(ks[1], (DEC_BATCH, DEC_SEQ, D_MODEL))
    mem_prompt = nrm(ks[2], (BATCH, N_MEM, D_MODEL))
    cache_k = nrm(ks[3], (n_phys, PAGE_SIZE, H_FOX, DH))
    cache_v = nrm(ks[4], (n_phys, PAGE_SIZE, H_FOX, DH))
    cache_logf = jax.nn.log_sigmoid(fox_bias_base + nrm(ks[5], (n_phys, PAGE_SIZE, H_FOX)))
    page_table = jax.random.permutation(ks[6], n_phys)[:DEC_BATCH * n_pages].reshape(
        DEC_BATCH, n_pages).astype(jnp.int32)
    cache_mem_k = nrm(ks[7], (DEPTH, DEC_BATCH, N_MEM, H_MEM, DH))
    cache_mem_v = nrm(ks[8], (DEPTH, DEC_BATCH, N_MEM, H_MEM, DH))
    state_ret = nrm(ks[9], (N_A, DEC_BATCH, H_RET, DK_RET, DV_RET))
    state_conv = nrm(ks[10], (DEPTH, DEC_BATCH, CONV_W - 1, 2 * D_FF))
    g_mix_pre = 1.0 + nrm(ks[11], (DEPTH, D_MODEL), 0.05)
    g_mix_post = 1.0 + nrm(ks[12], (DEPTH, D_MODEL), 0.05)
    g_ffn_pre = 1.0 + nrm(ks[13], (DEPTH, D_MODEL), 0.05)
    g_ffn_post = 1.0 + nrm(ks[14], (DEPTH, D_MODEL), 0.05)
    w_in_a = nrm(ks[15], (N_A, D_MODEL, D_IN_A), D_MODEL ** -0.5)
    w_out_a = nrm(ks[16], (N_A, D_CAT_A, D_MODEL), D_CAT_A ** -0.5)
    w_in_b = nrm(ks[17], (N_B, D_MODEL, D_IN_B), D_MODEL ** -0.5)
    w_out_b = nrm(ks[18], (N_B, D_CAT_B, D_MODEL), D_CAT_B ** -0.5)
    w_mem_kv = nrm(ks[19], (DEPTH, D_MODEL, 2 * D_MEMQ), D_MODEL ** -0.5)
    g_kv = 1.0 + nrm(ks[20], (D_MODEL,), 0.05)
    w_kv_shared = nrm(ks[21], (D_MODEL, D_KV_SH), D_MODEL ** -0.5)
    b_f = fox_bias_base + nrm(ks[22], (H_FOX,), 0.1)
    w_ffn_up = nrm(ks[23], (DEPTH, D_MODEL, 2 * D_FF), D_MODEL ** -0.5)
    conv_w = nrm(ks[24], (DEPTH, CONV_W, 2 * D_FF), CONV_W ** -0.5)
    conv_b = nrm(ks[25], (DEPTH, 2 * D_FF), 0.02)
    w_ffn_down = nrm(ks[26], (DEPTH, D_FF, D_MODEL), D_FF ** -0.5)
    return {'x_prompt': x_prompt, 'x_sample': x_sample, 'mem_prompt': mem_prompt,
            'cache_k': cache_k, 'cache_v': cache_v, 'cache_logf': cache_logf, 'page_table': page_table,
            'cache_mem_k': cache_mem_k, 'cache_mem_v': cache_mem_v,
            'state_ret': state_ret, 'state_conv': state_conv,
            'g_mix_pre': g_mix_pre, 'g_mix_post': g_mix_post, 'g_ffn_pre': g_ffn_pre, 'g_ffn_post': g_ffn_post,
            'w_in_a': w_in_a, 'w_out_a': w_out_a, 'w_in_b': w_in_b, 'w_out_b': w_out_b,
            'w_mem_kv': w_mem_kv, 'g_kv': g_kv, 'w_kv_shared': w_kv_shared, 'b_f': b_f,
            'w_ffn_up': w_ffn_up, 'conv_w': conv_w, 'conv_b': conv_b, 'w_ffn_down': w_ffn_down}

def reference(x_prompt, x_sample, mem_prompt, cache_k, cache_v, cache_logf, page_table,
              cache_mem_k, cache_mem_v, state_ret, state_conv,
              g_mix_pre, g_mix_post, g_ffn_pre, g_ffn_post, w_in_a, w_out_a, w_in_b, w_out_b,
              w_mem_kv, g_kv, w_kv_shared, b_f, w_ffn_up, conv_w, conv_b, w_ffn_down):
    p = {'g_mix_pre': g_mix_pre, 'g_mix_post': g_mix_post, 'g_ffn_pre': g_ffn_pre, 'g_ffn_post': g_ffn_post,
         'w_in_a': w_in_a, 'w_out_a': w_out_a, 'w_in_b': w_in_b, 'w_out_b': w_out_b,
         'g_kv': g_kv, 'w_kv_shared': w_kv_shared, 'b_f': b_f,
         'w_ffn_up': w_ffn_up, 'conv_w': conv_w, 'conv_b': conv_b, 'w_ffn_down': w_ffn_down}

    B, L, _ = x_prompt.shape
    M = mem_prompt.shape[1]
    mkv = jnp.einsum('bmd,lde->lbme', mem_prompt, w_mem_kv)
    mem_k_p = mkv[..., :D_MEMQ].reshape(DEPTH, B, M, H_MEM, DH)
    mem_v_p = mkv[..., D_MEMQ:].reshape(DEPTH, B, M, H_MEM, DH)
    ret0 = jnp.zeros((N_A, B, H_RET, DK_RET, DV_RET), jnp.float32)
    conv0 = jnp.zeros((DEPTH, B, CONV_W - 1, 2 * D_FF), x_prompt.dtype)
    pos_p = jnp.arange(L, dtype=jnp.int32)
    y_prompt, k_p, v_p, logf_p, ret_p, conv_p = trunk(
        x_prompt, pos_p, mem_k_p, mem_v_p, ret0, conv0, None, None, None, p)

    DB, Ls, _ = x_sample.shape
    n_pages = page_table.shape[1]
    past_len = n_pages * cache_k.shape[1]
    past_k = cache_k[page_table].reshape(DB, past_len, H_FOX, DH)
    past_v = cache_v[page_table].reshape(DB, past_len, H_FOX, DH)
    past_logf = cache_logf[page_table].reshape(DB, past_len, H_FOX)
    pos_s = past_len + jnp.arange(Ls, dtype=jnp.int32)
    y_sample, k_s, v_s, logf_s, ret_s, conv_s = trunk(
        x_sample, pos_s, cache_mem_k, cache_mem_v, state_ret, state_conv, past_k, past_v, past_logf, p)

    return (y_prompt, y_sample, k_p, v_p, logf_p, k_s, v_s, logf_s,
            mem_k_p, mem_v_p, ret_p, ret_s, conv_p, conv_s)


_drawn_inputs = setup_inputs


def setup_inputs(seed=0):
    import zlib

    import numpy as np

    out = dict(_drawn_inputs(seed))
    spreads = {}
    factors = {}
    for name, (base, spread) in spreads.items():
        noise = np.random.default_rng([zlib.crc32(name.encode()), seed]).standard_normal(out[name].shape)
        drawn = base * np.exp(spread * noise) if base else spread * noise
        out[name] = __import__('jax').numpy.asarray(drawn.astype(out[name].dtype))
    for name, factor in factors.items():
        out[name] = (out[name] * factor).astype(out[name].dtype)
    return out
```

```python
from contextlib import ExitStack

import concourse.bass as bass
from concourse import mybir

F32 = mybir.dt.float32
F32R = mybir.dt.float32r
I32 = mybir.dt.int32
ACT = mybir.ActivationFunctionType
ALU = mybir.AluOpType
AX = mybir.AxisListType

P = 128
D = 1024
KD = D // P
SEQ = 1024
PT = SEQ // P
DB, DS = 8, 8
NS = DB * DS
TILES = PT + 1
ROWS = TILES * P
TOK = SEQ + NS
NC = 512
EPS = 1e-6
NEG = -1e30

H_RET, DK, DV = 6, 64, 128
NQ = H_RET * DK
NV = H_RET * DV
Z_V, Z_G, Z_M = 2 * NQ, 2 * NQ + NV, 2 * NQ + 2 * NV
NZ = Z_M + 256
H_FOX, DH = 12, 64
NF = H_FOX * DH
HP = H_FOX // 2
H_MEM, N_MEM = 4, 256
MT = N_MEM // P
DFF = 2816
KF = DFF // P
CW = 3
DEPTH = 2
PAGE = 128
PAGES = 32


class Counter:

    def __init__(self, sem):
        self.sem, self.base, self.added = sem, 0, 0

    def wait_all(self, eng, total):
        self.added = total
        eng.wait_ge(self.sem, self.base + total)


def never(value):
    return isinstance(value, int) and value <= 0


def need(eng, sem, value):
    if never(value):
        return
    if isinstance(sem, Counter):
        sem, value = sem.sem, sem.base + value
    eng.wait_ge(sem, value)


def need_all(eng, *waits):
    waits = [(w.sem, w.base + v) if isinstance(w, Counter) else (w, v) for w, v in waits if not never(v)]
    waits = [(sem, v if isinstance(v, int) else eng.compute_val(v)) for sem, v in waits]
    for sem, v in waits:
        eng.wait_ge(sem, v)


def repeat(eng, n, body):
    body(0)
    if n == 2:
        body(1)
    elif n > 2:
        with eng.Fori(1, n) as i:
            body(i)


def repeat_ahead(eng, n, body):
    body(0)
    if n > 2:
        with eng.Fori(1, n - 1) as i:
            body(i)
    body(n - 1)


def first(i):
    return isinstance(i, int) and i == 0


def last_of(i, n):
    return isinstance(i, int) and i == n - 1


def at(ap, i):
    if isinstance(i, int):
        return ap[i]
    names = " ".join(f"d{j}" for j in range(len(ap.shape) - 1))
    return ap[bass.ds(i, 1)].rearrange(f"o d0 {names[3:]} -> (o d0) {names[3:]}")


def bc(ap, axis, n):
    a = ap.unsqueeze(axis)
    shape = list(a.shape)
    shape[axis] = n
    return a.broadcast_to(shape)


class Program:

    def __init__(self, nc, ctx):
        self.nc, self.ctx = nc, ctx
        self.n = 0
        self.kept = []
        self.old = None
        self.old_sems = []
        self.ps = ctx.enter_context(nc.psum_tensor("ps", [P, 8, 512], F32))

    def open(self, name):
        self.n += 1
        self.name = f"{name}{self.n}"
        self.mem = ExitStack()
        self.sems = ExitStack()
        self.live = []
        self.pool_sems = 0

    def sb(self, name, shape, dt=F32):
        return self.mem.enter_context(self.nc.sbuf_tensor(f"{self.name}_{name}", shape, dt))

    def sem(self, name):
        s = self.sems.enter_context(self.nc.semaphore(f"{self.name}_{name}"))
        self.live.append(s)
        return s

    def pool_sem(self, name):
        if self.pool_sems == len(self.kept):
            self.kept.append(Counter(self.ctx.enter_context(self.nc.semaphore(f"pool_dma{self.pool_sems}_{name}"))))
        self.pool_sems += 1
        return self.kept[self.pool_sems - 1]

    def clear_old(self, eng):
        for s in self.old_sems:
            eng.sem_clear(s)

    def close(self):
        self.mem.close()
        for counter in self.kept:
            counter.base, counter.added = counter.base + counter.added, 0
        if self.old is not None:
            self.old.close()
        self.old, self.old_sems = self.sems, self.live


def project(g, a, w, n_chunks, tiles, outs, silu=(), tail=None):
    nc = g.nc
    g.open("project")
    a_hi, a_lo = a
    S = 3 if tiles == TILES else tiles
    US = tiles // S
    raw = g.sb("raw", [P, 2, 4, NC])
    w_hi, w_lo = g.sb("w_hi", [P, KD, NC], F32R), g.sb("w_lo", [P, KD, NC], F32R)
    z = g.sb("z", [P, S, NC])
    loaded = [g.sem("half0_loaded"), g.sem("half1_loaded")]
    hi_done, lo_done, w_used = g.sem("w_hi_done"), g.sem("w_lo_done"), g.sem("w_used")
    z_done, z_out = g.sem("z_done"), g.sem("z_copied")
    stored = [g.pool_sem(f"stored{s}") for s in range(S)]
    stores = len(outs(0, 0))
    T1 = tiles - 1

    def bank(t):
        return 4 if t == 8 else t

    with nc.Block() as block:
        @block.sync
        def _(sp):
            g.clear_old(sp)

            def body(n):
                for half in range(2):
                    need(sp, lo_done, (n - 1) * KD + half * 4 + 4)
                    sp.dma_start(raw[:, half], at(w, n)[:, half * 4:half * 4 + 4, :]).then_inc(loaded[half], 16)
            repeat(sp, n_chunks, body)

        @block.scalar
        def _(act):
            def split(n):
                for k in range(KD):
                    if k % 4 == 0:
                        act.wait_ge(loaded[k // 4], 16 * n + 16)
                    need(act, w_used, (n - 1) * KD + k + 1)
                    nc.scalar.activation(w_hi[:, k], raw[:, k // 4, k % 4], ACT.Copy).then_inc(hi_done, 1)

            def evac(n, t):
                if t < T1:
                    act.wait_ge(z_done, n * T1 + t + 1)
                else:
                    act.wait_ge(w_used, n * KD + KD)
                need(act, stored[t % S], (n * US + t // S) * 16 * stores)
                cut = silu[n] if isinstance(n, int) and n < len(silu) else 0
                if cut:
                    nc.scalar.activation(z[:, t % S, :cut], g.ps[:, bank(t), :cut], ACT.Silu).then_inc(z_out, 1)
                if cut < NC:
                    nc.scalar.activation(z[:, t % S, cut:], g.ps[:, bank(t), cut:], ACT.Copy).then_inc(z_out, 1)
                elif silu:
                    pass

            def body(n):
                split(n)
                if not first(n):
                    evac(n - 1, T1)
                for t in range(T1):
                    evac(n, t)
            if silu:
                for n in range(n_chunks):
                    body(n)
            else:
                repeat(act, n_chunks, body)
            evac(n_chunks - 1, T1)

        def copies(n, t):
            if not silu:
                return n * tiles + t + 1
            before = sum(tiles * (2 if 0 < silu[m] < NC else 1) for m in range(n))
            return before + (t + 1) * (2 if 0 < silu[n] < NC else 1)

        @block.vector
        def _(dve):
            def body(n):
                for k in range(KD):
                    dve.wait_ge(hi_done, n * KD + k + 1)
                    nc.vector.tensor_tensor(w_lo[:, k], raw[:, k // 4, k % 4], w_hi[:, k].bitcast(F32),
                                            ALU.subtract).then_inc(lo_done, 1)
            repeat(dve, n_chunks, body)

        @block.tensor
        def _(pe):
            def body(n):
                for t in range(tiles):
                    m, s = (n - 1, t) if t < 8 else (n, 4)
                    if t == 4 and tiles == 9:
                        s = 8
                    if not first(n) or t == 8:
                        need(pe, z_out, copies(m, s))
                    for k in range(KD):
                        if t == 0:
                            pe.wait_ge(lo_done, n * KD + k + 1)
                        ah, al = a_hi[:, k, t * P:t * P + P], a_lo[:, k, t * P:t * P + P]
                        o = g.ps[:, bank(t)]
                        nc.tensor.matmul(o, al, w_hi[:, k], start=(k == 0), stop=False)
                        nc.tensor.matmul(o, ah, w_hi[:, k], start=False, stop=False)
                        last = nc.tensor.matmul(o, ah, w_lo[:, k], start=False, stop=(k == KD - 1))
                        if t == T1:
                            last.then_inc(w_used, 1)
                    if t < T1:
                        last.then_inc(z_done, 1)
            if silu:
                for n in range(n_chunks):
                    body(n)
            else:
                repeat(pe, n_chunks, body)

        @block.gpsimd
        def _(pool):
            def body(n):
                for t in range(tiles):
                    pool.wait_ge(z_out, copies(n, t))
                    for dst, c0, c1 in outs(n, t):
                        pool.dma_start(dst, z[:, t % S, c0:c1]).then_inc(stored[t % S].sem, 16)
            if silu:
                for n in range(n_chunks):
                    body(n)
            else:
                repeat(pool, n_chunks, body)
            for s in range(S):
                stored[s].wait_all(pool, n_chunks * US * 16 * stores)
    g.close()


def columns(z, tiles):
    v = z.rearrange("(t p) (n c) -> n t p c", p=P, c=NC)

    def outs(n, t):
        return [(at(v[:, t], n), 0, NC)]
    return outs


def normalise(g, a, src, gain=None, residual=None, h_out=None, plain=False):
    nc = g.nc
    g.open("normalise")
    x = g.sb("x", [P, TILES, D])
    y = g.sb("y", [P, TILES, D]) if not plain else None
    square = g.sb("square", [P, D])
    stat = g.sb("stat", [P, TILES, 8])
    eps = g.sb("eps", [P, 1])
    post = g.sb("post", [P, D]) if residual else None
    pre = g.sb("pre", [P, D]) if gain is not None else None
    x_in = [g.sem(f"x_in{t}") for t in range(TILES)]
    o_in = [g.sem(f"o_in{t}") for t in range(TILES)] if residual else None
    h_stored = g.pool_sem("h_stored")
    post_in, pre_in, eps_set = g.sem("post_in"), g.sem("pre_in"), g.sem("eps_set")
    o_sum, o_std, o_rstd, o_normed, h_done = (g.sem(s) for s in ("o_sum", "o_std", "o_rstd", "o_normed", "h_done"))
    h_sum, h_std, h_rstd, n_done = (g.sem(s) for s in ("h_sum", "h_std", "h_rstd", "n_done"))
    turned, hi_done, lo_done = g.sem("turned"), g.sem("hi_done"), g.sem("lo_done")
    a_hi, a_lo = a if a else (None, None)
    rows = x if plain else y
    AHEAD_H, AHEAD_O = (0, 0) if plain else (1, 2)

    def skewed(stages):
        for i in range(-max(s for s, _ in stages), TILES):
            for s, step in stages:
                if 0 <= i + s < TILES:
                    step(i + s)

    def bank(t, j):
        return (2 * t + j) % 8

    with nc.Block() as block:
        @block.sync
        def _(sp):
            g.clear_old(sp)
            for t in range(TILES):
                if residual:
                    sp.dma_start(y[:, t], residual[0][t]).then_inc(o_in[t], 16)
                sp.dma_start(x[:, t], src[t]).then_inc(x_in[t], 16)
                if t == 0 and residual:
                    sp.dma_start(post[:], residual[1].broadcast_to([P, D])).then_inc(post_in, 16)
                if t == 0 and gain is not None:
                    sp.dma_start(pre[:], gain.broadcast_to([P, D])).then_inc(pre_in, 16)

        @block.scalar
        def _(act):
            act.wait_ge(eps_set, 1)

            def stat_o(t):
                act.wait_ge(o_in[t], 16)
                nc.scalar.activation(square[:], y[:, t], ACT.Square, accum_out=stat[:, t, 0:1]).then_inc(o_sum, 1)
                act.wait_ge(o_sum, t + 1)
                nc.scalar.activation(stat[:, t, 1:2], stat[:, t, 0:1], ACT.Sqrt, scale=1.0 / D,
                                     bias=eps[:]).then_inc(o_std, 1)

            def stat_h(t):
                if residual:
                    act.wait_ge(h_done, t + 1)
                else:
                    act.wait_ge(x_in[t], 16)
                nc.scalar.activation(square[:], x[:, t], ACT.Square, accum_out=stat[:, t, 4:5]).then_inc(h_sum, 1)
                act.wait_ge(h_sum, t + 1)
                nc.scalar.activation(stat[:, t, 5:6], stat[:, t, 4:5], ACT.Sqrt, scale=1.0 / D,
                                     bias=eps[:]).then_inc(h_std, 1)

            def hi(t):
                for j in range(2):
                    act.wait_ge(turned, 2 * t + j + 1)
                    nc.scalar.activation(a_hi[:, 4 * j:4 * j + 4, t * P:t * P + P], g.ps[:, bank(t, j), :].rearrange(
                        "p (k r) -> p k r", k=4), ACT.Copy).then_inc(hi_done, 1)
            skewed([(AHEAD_O, stat_o)] * bool(residual) + [(AHEAD_H, stat_h)] * bool(a and not plain) +
                   [(0, hi)] * bool(a))

        @block.vector
        def _(dve):
            nc.vector.memset(eps[:], EPS).then_inc(eps_set, 1)
            if residual:
                dve.wait_ge(post_in, 16)
            if gain is not None:
                dve.wait_ge(pre_in, 16)

            def norm_o(t):
                dve.wait_ge(o_std, t + 1)
                nc.vector.reciprocal(stat[:, t, 2:3], stat[:, t, 1:2]).then_inc(o_rstd, 1)
                dve.wait_ge(o_rstd, t + 1)
                nc.vector.scalar_tensor_tensor(out=y[:, t], in0=y[:, t], scalar=stat[:, t, 2:3], in1=post[:],
                                               op0=ALU.mult, op1=ALU.mult).then_inc(o_normed, 1)
                dve.wait_ge(o_normed, t + 1)
                dve.wait_ge(x_in[t], 16)
                nc.vector.tensor_tensor(x[:, t], x[:, t], y[:, t], ALU.add).then_inc(h_done, 1)

            def norm_h(t):
                dve.wait_ge(h_std, t + 1)
                nc.vector.reciprocal(stat[:, t, 6:7], stat[:, t, 5:6]).then_inc(h_rstd, 1)
                dve.wait_ge(h_rstd, t + 1)
                nc.vector.scalar_tensor_tensor(out=y[:, t], in0=x[:, t], scalar=stat[:, t, 6:7], in1=pre[:],
                                               op0=ALU.mult, op1=ALU.mult).then_inc(n_done, 1)

            def lo(t):
                for j in range(2):
                    dve.wait_ge(hi_done, 2 * t + j + 1)
                    nc.vector.tensor_tensor(
                        a_lo[:, 4 * j:4 * j + 4, t * P:t * P + P],
                        g.ps[:, bank(t, j), :].rearrange("p (k r) -> p k r", k=4),
                        a_hi[:, 4 * j:4 * j + 4, t * P:t * P + P].bitcast(F32), ALU.subtract).then_inc(lo_done, 1)
            skewed([(AHEAD_O, norm_o)] * bool(residual) + [(AHEAD_H, norm_h)] * bool(a and not plain) +
                   [(0, lo)] * bool(a))

        if a:
            @block.tensor
            def _(pe):
                for t in range(TILES):
                    if plain:
                        pe.wait_ge(x_in[t], 16)
                    else:
                        pe.wait_ge(n_done, t + 1)
                    for j in range(2):
                        need(pe, lo_done, 2 * t + j - 7)
                        for k in range(4 * j, 4 * j + 4):
                            last = nc.tensor.transpose(g.ps[:, bank(t, j), (k % 4) * P:(k % 4) * P + P],
                                                       rows[:, t, k * P:k * P + P], g.ident[:])
                        last.then_inc(turned, 1)

        if h_out is not None:
            @block.gpsimd
            def _(pool):
                for t in range(TILES):
                    pool.wait_ge(h_done, t + 1)
                    pool.dma_start(h_out[t], x[:, t]).then_inc(h_stored.sem, 16)
                h_stored.wait_all(pool, 16 * TILES)
    g.close()


def retention(g, z, t_in, cat, state_in, state_out, sample):
    nc = g.nc
    g.open("retention")
    R = NS if sample else P
    B = DB if sample else 1
    n_tiles = 1 if sample else PT
    U = 1 if sample else 2
    steps = n_tiles // U
    zt = g.sb("zt", [P, U, Z_M])
    rope = g.sb("rope", [P, U, 64])
    zcos, zsin = g.sb("zcos", [P, 2 * NQ]), g.sb("zsin", [P, 2 * NQ])
    rot = g.sb("rot", [P, 2 * NQ])
    q_t, k_t = g.sb("q_t", [P, 3, R]), g.sb("k_t", [P, 3, R])
    qd, kd = g.sb("qd", [P, B, 3, R]), g.sb("kd", [P, B, H_RET, DK])
    inner = g.sb("inner", [P, H_RET, R])
    o = g.sb("o", [P, H_RET, DV])
    square = g.sb("square", [P, H_RET, DV])
    r = g.sb("r", [P, U, NV])
    st = g.sb("st", [P, 5, H_RET])
    S = g.sb("S", [P, B, 3, DV])
    dmask, qdec = g.sb("dmask", [P, H_RET, R]), g.sb("qdec", [P, B, 3, R])
    kdec, sdec = g.sb("kdec", [P, B, H_RET]), g.sb("sdec", [P, 3])
    eps = g.sb("eps", [P, 1])
    z_in = [g.sem(f"z_in{u}") for u in range(U)]
    r_stored = [g.pool_sem(f"r_stored{u}") for u in range(U)]
    tables_in, s_stored = g.sem("tables_in"), g.pool_sem("s_stored")
    (s_set, cos_done, sin_done, rot_done, qk_turned, q_ready, k_ready, qd_done, kd_done, inner_in, inner_done,
     o_in, s_in, s_done, o_copied, mean_done, center_done, square_done, var_done, std_done, rstd_done, norm_done,
     r_done) = (g.sem(x) for x in (
         "s_set cos_done sin_done rot_done qk_turned q_ready k_ready qd_done kd_done inner_in inner_done o_in s_in "
         "s_done o_copied mean_done center_done square_done var_done std_done rstd_done norm_done r_done").split())
    inner_bank = lambda h: g.ps[0:R, 2 + h % 2, (h // 2) * R:(h // 2) * R + R]
    o_bank = lambda h: g.ps[0:R, 4 + h % 2, (h // 2) * DV:(h // 2) * DV + DV]
    heads = lambda x, f: x.rearrange("p (c f) r -> p f c r", f=2)[:, f]

    with nc.Block() as block:
        @block.sync
        def _(sp):
            g.clear_old(sp)
            for dst, src in ((dmask[0:R], t_in["dmask"]), (qdec[:], t_in["qdec"]), (kdec[0:R], t_in["kdec"]),
                             (sdec[:], t_in["sdec"])):
                sp.dma_start(dst, src).then_inc(tables_in, 16)
            if sample:
                for half in range(2):
                    for c in range(3):
                        sp.dma_start(S[half * DK:half * DK + DK, :, c],
                                     state_in[:, 2 * c + half].rearrange("b d e -> d b e")).then_inc(tables_in, 16)

            def body(i):
                for u in range(U):
                    t = i * U + u
                    need_all(sp, (r_done, t - U + 1), (s_in, (t - U + 1) * B))
                    tt = PT if sample else t
                    sp.dma_start(zt[:, u], at(z, tt)[:, 0:Z_M]).then_inc(z_in[u], 16)
                    sp.dma_start(rope[0:R, u], at(t_in["rope"], tt)[0:R]).then_inc(z_in[u], 16)
            repeat(sp, steps, body)

        @block.scalar
        def _(act):
            act.wait_ge(s_set, 2)

            def body(i):
                for u in range(U):
                    t = i * U + u
                    act.wait_ge(qk_turned, 2 * t + 1)
                    need(act, inner_in, t)
                    need(act, o_in, t)
                    need(act, qd_done, t)
                    nc.scalar.activation(q_t[:], g.ps[:, 0, 0:3 * R].rearrange("p (c r) -> p c r", c=3),
                                         ACT.Copy).then_inc(q_ready, 1)
                    act.wait_ge(qk_turned, 2 * t + 2)
                    nc.scalar.activation(k_t[:], g.ps[:, 1, 0:3 * R].rearrange("p (c r) -> p c r", c=3),
                                         ACT.Copy, scale=DK ** -0.5).then_inc(k_ready, 1)
                    act.wait_ge(o_in, t + 1)
                    need(act, norm_done, t)
                    for f in range(2):
                        last = nc.scalar.activation(heads(o[0:R], f), g.ps[0:R, 4 + f, 0:3 * DV].rearrange(
                            "p (c e) -> p c e", c=3), ACT.Copy)
                    last.then_inc(o_copied, 1)
                    act.wait_ge(center_done, t + 1)
                    nc.scalar.activation(square[0:R], o[0:R], ACT.Square).then_inc(square_done, 1)
                    act.wait_ge(var_done, t + 1)
                    nc.scalar.activation(st[0:R, 3], st[0:R, 2], ACT.Sqrt, scale=1.0 / DV, bias=eps[0:R]).then_inc(
                        std_done, 1)
            repeat(act, steps, body)

        @block.vector
        def _(dve):
            nc.vector.memset(eps[:], EPS).then_inc(s_set, 1)
            if sample:
                nc.vector.memset(inner[:], 0.0).then_inc(s_set, 1)
            else:
                nc.vector.memset(S[:], 0.0).then_inc(s_set, 1)
            dve.wait_ge(s_set, 2)
            dve.wait_ge(tables_in, 16 * (10 if sample else 4))

            def body(i):
                for u in range(U):
                    t = i * U + u
                    dve.wait_ge(z_in[u], 32 * i + 32)
                    qk = zt[0:R, u, 0:2 * NQ].rearrange("p (h d) -> p h d", d=32)
                    C = zcos[0:R].rearrange("p (h f d) -> p h f d", f=2, d=32)
                    Sn = zsin[0:R].rearrange("p (h f d) -> p h f d", f=2, d=32)
                    need(dve, rot_done, 2 * t)
                    nc.vector.tensor_tensor(zcos[0:R].rearrange("p (h d) -> p h d", d=32), qk,
                                            bc(rope[0:R, u, 0:32], 1, 24), ALU.mult).then_inc(cos_done, 1)
                    nc.vector.tensor_tensor(zsin[0:R].rearrange("p (h d) -> p h d", d=32), qk,
                                            bc(rope[0:R, u, 32:64], 1, 24), ALU.mult).then_inc(sin_done, 1)
                    dve.wait_ge(cos_done, t + 1)
                    dve.wait_ge(sin_done, t + 1)
                    need(dve, qk_turned, 2 * t)
                    need(dve, kd_done, t)
                    rv = rot[0:R].rearrange("p (h f d) -> p h f d", f=2, d=32)
                    nc.vector.tensor_tensor(rv[:, :, 0], C[:, :, 0], Sn[:, :, 1], ALU.subtract).then_inc(rot_done, 1)
                    nc.vector.tensor_tensor(rv[:, :, 1], Sn[:, :, 0], C[:, :, 1], ALU.add).then_inc(rot_done, 1)
                    dve.wait_ge(rot_done, 2 * t + 2)
                    need(dve, s_in, t)
                    for b in range(B):
                        last = nc.vector.tensor_tensor(kd[0:R, b], rot[0:R, NQ:].rearrange("p (h d) -> p h d", d=DK),
                                                       bc(kdec[0:R, b], 2, DK), ALU.mult)
                    last.then_inc(kd_done, 1)
                    dve.wait_ge(q_ready, t + 1)
                    for b in range(B):
                        last = nc.vector.tensor_tensor(qd[:, b], q_t[:], qdec[:, b], ALU.mult)
                    last.then_inc(qd_done, 1)
                    dve.wait_ge(inner_in, t + 1)
                    for f in range(2):
                        last = nc.vector.tensor_tensor(
                            heads(inner[0:R], f), g.ps[0:R, 2 + f, 0:3 * R].rearrange("p (c r) -> p c r", c=3),
                            heads(dmask[0:R], f), ALU.mult)
                    last.then_inc(inner_done, 1)
                    for b in range(B):
                        dve.wait_ge(s_in, t * B + b + 1)
                        if b == 0:
                            dve.wait_ge(o_in, t + 1)
                        for c in range(3):
                            last = nc.vector.scalar_tensor_tensor(
                                out=S[:, b, c], in0=S[:, b, c], scalar=sdec[:, c:c + 1],
                                in1=g.ps[:, 6 + b % 2, c * DV:c * DV + DV], op0=ALU.mult, op1=ALU.add)
                        last.then_inc(s_done, 1)
                    dve.wait_ge(o_copied, t + 1)
                    need(dve, rstd_done, t)
                    nc.vector.tensor_reduce(st[0:R, 0], o[0:R], AX.X, ALU.add).then_inc(mean_done, 1)
                    dve.wait_ge(mean_done, 2 * t + 1)
                    nc.vector.tensor_scalar(st[0:R, 1], st[0:R, 0], -1.0 / DV, None, ALU.mult).then_inc(mean_done, 1)
                    dve.wait_ge(mean_done, 2 * t + 2)
                    nc.vector.tensor_tensor(o[0:R], o[0:R], bc(st[0:R, 1], 2, DV), ALU.add).then_inc(center_done, 1)
                    dve.wait_ge(square_done, t + 1)
                    nc.vector.tensor_reduce(st[0:R, 2], square[0:R], AX.X, ALU.add).then_inc(var_done, 1)
                    dve.wait_ge(std_done, t + 1)
                    nc.vector.reciprocal(st[0:R, 4], st[0:R, 3]).then_inc(rstd_done, 1)
                    dve.wait_ge(rstd_done, t + 1)
                    dve.wait_ge(center_done, t + 1)
                    need(dve, r_stored[u], 16 * i)
                    nc.vector.tensor_tensor(r[0:R, u].rearrange("p (h e) -> p h e", h=H_RET), o[0:R],
                                            bc(st[0:R, 4], 2, DV), ALU.mult).then_inc(norm_done, 1)
                    dve.wait_ge(norm_done, t + 1)
                    nc.vector.tensor_tensor(r[0:R, u], r[0:R, u], zt[0:R, u, Z_G:Z_M], ALU.mult).then_inc(r_done, 1)
            repeat(dve, steps, body)

        @block.tensor
        def _(pe):
            pe.wait_ge(s_set, 2)
            if sample:
                pe.wait_ge(tables_in, 160)

            def body(i):
                for u in range(U):
                    t = i * U + u
                    pe.wait_ge(rot_done, 2 * t + 2)
                    need(pe, q_ready, t)
                    need(pe, k_ready, t)
                    for x in range(2):
                        for c in range(3):
                            last = nc.tensor.transpose(g.ps[:, x, c * R:c * R + R],
                                                       rot[0:R, x * NQ + c * P:x * NQ + c * P + P],
                                                       g.ident[0:R, 0:R])
                        last.then_inc(qk_turned, 1)
                    pe.wait_ge(q_ready, t + 1)
                    pe.wait_ge(k_ready, t + 1)
                    need(pe, inner_done, t)
                    for h in range(H_RET):
                        half = slice((h % 2) * DK, (h % 2) * DK + DK)
                        last = nc.tensor.matmul(inner_bank(h), k_t[half, h // 2], q_t[half, h // 2],
                                                start=True, stop=True)
                    last.then_inc(inner_in, 1)
                    pe.wait_ge(inner_done, t + 1)
                    pe.wait_ge(qd_done, t + 1)
                    need(pe, s_done, t * B)
                    need(pe, o_copied, t)
                    for h in range(H_RET):
                        half = slice((h % 2) * DK, (h % 2) * DK + DK)
                        nc.tensor.matmul(o_bank(h), inner[:, h], zt[:, u, Z_V + h * DV:Z_V + h * DV + DV],
                                         start=True, stop=False)
                        for b in range(B):
                            last = nc.tensor.matmul(o_bank(h), qd[half, b, h // 2], S[half, b, h // 2], start=False,
                                                    stop=(b == B - 1))
                    last.then_inc(o_in, 1)
                    pe.wait_ge(kd_done, t + 1)
                    for b in range(B):
                        need(pe, s_done, t * B + b - 1)
                        for h in range(H_RET):
                            half = slice((h % 2) * DK, (h % 2) * DK + DK)
                            v = zt[0:R, u, Z_V + h * DV:Z_V + h * DV + DV]
                            last = nc.tensor.matmul(g.ps[half, 6 + b % 2, (h // 2) * DV:(h // 2) * DV + DV],
                                                    kd[0:R, b, h], v, start=True, stop=True)
                        last.then_inc(s_in, 1)
            repeat(pe, steps, body)

        @block.gpsimd
        def _(pool):
            def body(i):
                for u in range(U):
                    t = i * U + u
                    pool.wait_ge(r_done, t + 1)
                    pool.dma_start(at(cat, PT if sample else t)[0:R, 0:NV], r[0:R, u]).then_inc(r_stored[u].sem, 16)
            repeat(pool, steps, body)
            pool.wait_ge(s_done, n_tiles * B)
            for half in range(2):
                for c in range(3):
                    pool.dma_start(state_out[:, 2 * c + half].rearrange("b d e -> d b e"),
                                   S[half * DK:half * DK + DK, :, c]).then_inc(s_stored.sem, 16)
            s_stored.wait_all(pool, 6 * 16)
            for u in range(U):
                r_stored[u].wait_all(pool, 16 * steps)
    g.close()


def mem_prompt(g, z, q0, mem_k, mem_v, cat):
    nc = g.nc
    g.open("mem_prompt")
    U = 2
    steps = PT // U
    mk = g.sb("mk", [P, MT, N_MEM])
    mv = g.sb("mv", [P, MT, N_MEM])
    mk_t = g.sb("mk_t", [P, 2, N_MEM])
    q = g.sb("q", [P, U, N_MEM])
    q_t = g.sb("q_t", [P, 2, P])
    p = g.sb("p", [P, H_MEM, N_MEM])
    p_t = g.sb("p_t", [P, H_MEM * MT, P])
    st = g.sb("st", [P, 3, H_MEM])
    o = g.sb("o", [P, U, H_MEM, DH])
    q_in = [g.sem(f"q_in{u}") for u in range(U)]
    o_stored = [g.pool_sem(f"o_stored{u}") for u in range(U)]
    (mem_in, k_turned, k_ready, q_turned, q_ready, scores_in, max_done, exp_done, p_turned, p_ready, o_in, rsum_done,
     o_done) = (g.sem(x) for x in ("mem_in k_turned k_ready q_turned q_ready scores_in max_done exp_done p_turned "
                                   "p_ready o_in rsum_done o_done").split())
    with nc.Block() as block:
        @block.sync
        def _(sp):
            g.clear_old(sp)
            sp.dma_start(mk[:], mem_k.rearrange("(m p) c -> p m c", p=P)).then_inc(mem_in, 16)
            sp.dma_start(mv[:], mem_v.rearrange("(m p) c -> p m c", p=P)).then_inc(mem_in, 16)

            def body(i):
                for u in range(U):
                    need(sp, q_turned, i * U + u - U + 1)
                    sp.dma_start(q[:, u], at(z, i * U + u)[:, q0:q0 + N_MEM]).then_inc(q_in[u], 16)
            repeat(sp, steps, body)

        @block.tensor
        def _(pe):
            pe.wait_ge(mem_in, 32)
            for c in range(2):
                for m in range(MT):
                    last = nc.tensor.transpose(g.ps[:, 0, (c * MT + m) * P:(c * MT + m) * P + P],
                                               mk[:, m, c * P:c * P + P], g.ident[:])
            last.then_inc(k_turned, 1)
            pe.wait_ge(k_ready, 1)

            def body(i):
                for u in range(U):
                    t = i * U + u
                    pe.wait_ge(q_in[u], 16 * i + 16)
                    need(pe, q_ready, t)
                    for c in range(2):
                        last = nc.tensor.transpose(g.ps[:, 0, c * P:c * P + P], q[:, u, c * P:c * P + P], g.ident[:])
                    last.then_inc(q_turned, 1)
                    pe.wait_ge(q_ready, t + 1)
                    need(pe, exp_done, t * H_MEM)
                    for h in range(H_MEM):
                        half = slice((h % 2) * DH, (h % 2) * DH + DH)
                        last = nc.tensor.matmul(g.ps[:, 1 + h % 2, (h // 2) * N_MEM:(h // 2) * N_MEM + N_MEM],
                                                q_t[half, h // 2], mk_t[half, h // 2], start=True, stop=True)
                    last.then_inc(scores_in, 1)
                    for j in range(2):
                        need(pe, p_ready, 2 * (t - 1) + j + 1)
                        for x in range(4):
                            h, m = (4 * j + x) // MT, x % MT
                            pe.wait_ge(exp_done, t * H_MEM + h + 1)
                            last = nc.tensor.transpose(g.ps[:, 3 + j, x * P:x * P + P], p[:, h, m * P:m * P + P],
                                                       g.ident[:])
                        last.then_inc(p_turned, 1)
                    need(pe, o_done, t)
                    for h in range(H_MEM):
                        pe.wait_ge(p_ready, 2 * t + h // 2 + 1)
                        for m in range(MT):
                            last = nc.tensor.matmul(g.ps[:, 7, h * DH:h * DH + DH], p_t[:, h * MT + m],
                                                    mv[:, m, h * DH:h * DH + DH], start=(m == 0), stop=(m == MT - 1))
                    last.then_inc(o_in, 1)
            repeat(pe, steps, body)

        @block.scalar
        def _(act):
            act.wait_ge(k_turned, 1)
            nc.scalar.activation(mk_t[:], g.ps[:, 0, :].rearrange("p (c m) -> p c m", c=2), ACT.Copy).then_inc(
                k_ready, 1)

            def body(i):
                for u in range(U):
                    t = i * U + u
                    act.wait_ge(q_turned, t + 1)
                    need(act, scores_in, t)
                    nc.scalar.activation(q_t[:], g.ps[:, 0, 0:2 * P].rearrange("p (c m) -> p c m", c=2), ACT.Copy,
                                         scale=DH ** -0.5).then_inc(q_ready, 1)
                    act.wait_ge(max_done, t + 1)
                    need(act, p_turned, 2 * t)
                    need(act, rsum_done, t)
                    for h in range(H_MEM):
                        nc.scalar.activation(p[:, h], g.ps[:, 1 + h % 2, (h // 2) * N_MEM:(h // 2) * N_MEM + N_MEM],
                                             ACT.Exp, bias=st[:, 0, h:h + 1], accum_out=st[:, 1, h:h + 1]).then_inc(
                                                 exp_done, 1)
            repeat(act, steps, body)

        @block.vector
        def _(dve):
            def body(i):
                for u in range(U):
                    t = i * U + u
                    dve.wait_ge(scores_in, t + 1)
                    need(dve, exp_done, t * H_MEM)
                    nc.vector.tensor_reduce(st[:, 0].rearrange("p (c f) -> p f c", f=2),
                                            g.ps[:, 1:3, :].rearrange("p f (c m) -> p f c m", m=N_MEM),
                                            AX.X, ALU.max, negate=True).then_inc(max_done, 1)
                    for j in range(2):
                        dve.wait_ge(p_turned, 2 * t + j + 1)
                        need(dve, o_in, t)
                        nc.vector.tensor_copy(p_t[:, 4 * j:4 * j + 4],
                                              g.ps[:, 3 + j, :].rearrange("p (x r) -> p x r", x=4)).then_inc(
                                                  p_ready, 1)
                    dve.wait_ge(exp_done, t * H_MEM + H_MEM)
                    need(dve, o_done, t)
                    nc.vector.reciprocal(st[:, 2], st[:, 1]).then_inc(rsum_done, 1)
                    dve.wait_ge(rsum_done, t + 1)
                    dve.wait_ge(o_in, t + 1)
                    need(dve, o_stored[u], 16 * i)
                    nc.vector.tensor_tensor(o[:, u], g.ps[:, 7, 0:N_MEM].rearrange("p (h d) -> p h d", d=DH),
                                            bc(st[:, 2], 2, DH), ALU.mult).then_inc(o_done, 1)
            repeat(dve, steps, body)

        @block.gpsimd
        def _(pool):
            def body(i):
                for u in range(U):
                    pool.wait_ge(o_done, i * U + u + 1)
                    pool.dma_start(at(cat, i * U + u)[:, NV:D], o[:, u].rearrange("p h d -> p (h d)")).then_inc(o_stored[u].sem, 16)
            repeat(pool, steps, body)
            for u in range(U):
                o_stored[u].wait_all(pool, 16 * steps)
    g.close()


def mem_sample(g, z, q0, mem_kt, mem_v, cat):
    nc = g.nc
    g.open("mem_sample")
    HT = H_MEM * DS
    mk_t = g.sb("mk_t", [P, DB, 2, N_MEM])
    mv = g.sb("mv", [P, DB, MT, N_MEM])
    q = g.sb("q", [P, N_MEM])
    qb = g.sb("qb", [P, 2, DB, H_MEM, DS])
    p = g.sb("p", [HT, 2, N_MEM])
    p_t = g.sb("p_t", [P, 2, MT, HT])
    st = g.sb("st", [HT, 2, 3])
    o = g.sb("o", [HT, DB, N_MEM])
    (mem_in, q_in, zeroed, q_turned, q_ready, scores_in, max_done, exp_done, p_turned, p_ready, o_in, rsum_done,
     o_done) = (g.sem(x) for x in (
         "mem_in q_in zeroed q_turned q_ready scores_in max_done exp_done p_turned p_ready o_in rsum_done "
         "o_done").split())
    o_stored = g.pool_sem("o_stored")
    with nc.Block() as block:
        @block.sync
        def _(sp):
            g.clear_old(sp)
            sp.dma_start(q[0:NS], at(z, PT)[0:NS, q0:q0 + N_MEM]).then_inc(q_in, 16)
            sp.dma_start(mk_t[:], mem_kt.rearrange("b p c m -> p b c m")).then_inc(mem_in, 16)
            sp.dma_start(mv[:], mem_v.rearrange("b (m p) c -> p b m c", p=P)).then_inc(mem_in, 16)

        @block.tensor
        def _(pe):
            pe.wait_ge(q_in, 16)
            for c in range(2):
                last = nc.tensor.transpose(g.ps[:, 0, c * NS:c * NS + NS], q[0:NS, c * P:c * P + P],
                                           g.ident[0:NS, 0:NS])
            last.then_inc(q_turned, 1)
            pe.wait_ge(q_ready, 1)
            pe.wait_ge(mem_in, 32)

            def scores(b):
                need(pe, exp_done, b - 1)
                for c in range(2):
                    last = nc.tensor.matmul(g.ps[0:HT, 1 + b % 2, 0:N_MEM], qb[:, c, b], mk_t[:, b, c],
                                            start=(c == 0), stop=(c == 1))
                last.then_inc(scores_in, 1)

            scores(0)
            for b in range(DB):
                if b + 1 < DB:
                    scores(b + 1)
                pe.wait_ge(exp_done, b + 1)
                need(pe, p_ready, b - 1)
                for m in range(MT):
                    last = nc.tensor.transpose(g.ps[:, 3 + b % 2, m * HT:m * HT + HT], p[:, b % 2, m * P:m * P + P],
                                               g.ident[0:HT, 0:HT])
                last.then_inc(p_turned, 1)
                pe.wait_ge(p_ready, b + 1)
                need(pe, o_done, b - 1)
                for m in range(MT):
                    last = nc.tensor.matmul(g.ps[0:HT, 5 + b % 2, 0:N_MEM], p_t[:, b % 2, m], mv[:, b, m],
                                            start=(m == 0), stop=(m == MT - 1))
                last.then_inc(o_in, 1)

        @block.scalar
        def _(act):
            act.wait_ge(q_turned, 1)
            act.wait_ge(zeroed, 1)
            for h in range(H_MEM):
                half = slice((h % 2) * DH, (h % 2) * DH + DH)
                last = nc.scalar.activation(
                    qb[half, h // 2, :, h], g.ps[half, 0, (h // 2) * NS:(h // 2) * NS + NS].rearrange(
                        "p (b t) -> p b t", b=DB), ACT.Copy, scale=DH ** -0.5)
            last.then_inc(q_ready, 1)
            for b in range(DB):
                act.wait_ge(max_done, b + 1)
                need(act, p_turned, b - 1)
                need(act, rsum_done, b - 1)
                nc.scalar.activation(p[:, b % 2], g.ps[0:HT, 1 + b % 2, 0:N_MEM], ACT.Exp, bias=st[:, b % 2, 0:1],
                                     accum_out=st[:, b % 2, 1:2]).then_inc(exp_done, 1)

        @block.vector
        def _(dve):
            nc.vector.memset(qb[:], 0.0).then_inc(zeroed, 1)

            def row_max(b):
                dve.wait_ge(scores_in, b + 1)
                need(dve, exp_done, b - 1)
                nc.vector.tensor_reduce(st[:, b % 2, 0:1], g.ps[0:HT, 1 + b % 2, 0:N_MEM], AX.X, ALU.max,
                                        negate=True).then_inc(max_done, 1)

            row_max(0)
            for b in range(DB):
                if b + 1 < DB:
                    row_max(b + 1)
                dve.wait_ge(p_turned, b + 1)
                need(dve, o_in, b - 1)
                nc.vector.tensor_copy(p_t[:, b % 2], g.ps[:, 3 + b % 2, 0:MT * HT].rearrange(
                    "p (m r) -> p m r", m=MT)).then_inc(p_ready, 1)
                dve.wait_ge(exp_done, b + 1)
                need(dve, o_done, b - 1)
                nc.vector.reciprocal(st[:, b % 2, 2:3], st[:, b % 2, 1:2]).then_inc(rsum_done, 1)
                dve.wait_ge(rsum_done, b + 1)
                dve.wait_ge(o_in, b + 1)
                nc.vector.tensor_scalar(o[:, b], g.ps[0:HT, 5 + b % 2, 0:N_MEM], st[:, b % 2, 2:3], None,
                                        ALU.mult).then_inc(o_done, 1)

        @block.gpsimd
        def _(pool):
            pool.wait_ge(o_done, DB)
            for h in range(H_MEM):
                pool.dma_start(at(cat, PT)[0:NS, NV + h * DH:NV + h * DH + DH].rearrange("(b t) d -> t b d", b=DB),
                               o[h * DS:h * DS + DS, :, h * DH:h * DH + DH]).then_inc(o_stored.sem, 16)
            o_stored.wait_all(pool, 16 * H_MEM)
    g.close()


def ffn_up(g, a, w_up, taps, state_in, y_t, state_out):
    nc = g.nc
    g.open("ffn_up")
    U = 2
    steps = KF // U
    raw = g.sb("raw", [P, U, 2, KD * P])
    w_hi, w_lo = g.sb("w_hi", [P, U, 2, KD * P], F32R), g.sb("w_lo", [P, U, 2, KD * P], F32R)
    up = g.sb("up", [P, 2, SEQ + CW - 1])
    us = g.sb("us", [P, 2, DB, DS + CW - 1])
    cp = g.sb("cp", [P, 2, TOK])
    y = g.sb("y", [P, U, TOK])
    tp = g.sb("tp", [P, 2 * KF, 4])
    s_in = g.sb("s_in", [P, 2 * KF, DB, 2])
    s_new = g.sb("s_new", [P, 2 * KF, 2 + 2 * DB])
    a_hi, a_lo = a
    w_in = [g.sem(f"w_in{u}") for u in range(U)]
    y_stored = [g.pool_sem(f"y_stored{u}") for u in range(U)]
    (tables_in, zeroed, hi_done, lo_done, u_in, u_copied, state_set, tap0, tap1, tap2, gelu_done, y_done, state_kept,
     ) = (g.sem(x) for x in ("tables_in zeroed w_hi_done w_lo_done u_in u_copied state_set tap0 tap1 tap2 "
                                         "gelu_done y_done state_kept").split())
    state_stored = g.pool_sem("state_stored")
    SPANS = [(0, 364), (364, 364), (728, TOK - 728)]
    sample = lambda x: x[:, SEQ:TOK].rearrange("p (b t) -> p b t", b=DB)

    with nc.Block() as block:
        @block.sync
        def _(sp):
            g.clear_old(sp)
            sp.dma_start(tp[:], taps).then_inc(tables_in, 16)
            sp.dma_start(s_in[:], state_in).then_inc(tables_in, 16)

            def body(i):
                for u in range(U):
                    need(sp, lo_done, i * U + u - U + 1)
                    sp.dma_start(raw[:, u], at(w_up, i * U + u)).then_inc(w_in[u], 16)
            repeat(sp, steps, body)

        @block.scalar
        def _(act):
            act.wait_ge(zeroed, 1)

            def split(f, i, u):
                act.wait_ge(w_in[u], 16 * i + 16)
                need(act, u_in, 2 * (f - U) + 2)
                nc.scalar.activation(w_hi[:, u], raw[:, u], ACT.Copy).then_inc(hi_done, 1)

            def body(i):
                for u in range(U):
                    f = i * U + u
                    if first(f):
                        split(f, i, u)
                    if not last_of(f, KF):
                        split(f + 1, i + u, 1 - u)
                    for x in range(2):
                        act.wait_ge(u_in, 2 * f + x + 1)
                        need(act, tap2, 4 * (f - 1) + 2 * x + 2)
                        need(act, state_kept, 4 * (f - 1) + 2 * x + 2)
                        for j, (c0, cn) in enumerate(SPANS):
                            cn = min(cn, SEQ - c0)
                            nc.scalar.activation(up[:, x, CW - 1 + c0:CW - 1 + c0 + cn],
                                                 g.ps[:, 3 * x + j, 0:cn], ACT.Copy).then_inc(u_copied, 1)
                        nc.scalar.activation(us[:, x, :, CW - 1:], g.ps[:, 3 * x + 2, cn:cn + NS].rearrange(
                            "p (b t) -> p b t", b=DB), ACT.Copy).then_inc(u_copied, 1)
                    act.wait_ge(tap2, 4 * f + 2)
                    nc.scalar.activation(cp[:, 0], cp[:, 0], ACT.Gelu_apprx_tanh).then_inc(gelu_done, 1)
            repeat_ahead(act, steps, body)

        @block.vector
        def _(dve):
            nc.vector.memset(up[:, :, 0:CW - 1], 0.0).then_inc(zeroed, 1)
            dve.wait_ge(zeroed, 1)
            dve.wait_ge(tables_in, 32)

            def split(f, u):
                dve.wait_ge(hi_done, f + 1)
                nc.vector.tensor_tensor(w_lo[:, u], raw[:, u], w_hi[:, u].bitcast(F32), ALU.subtract).then_inc(
                    lo_done, 1)

            def body(i):
                for u in range(U):
                    f = i * U + u
                    if first(f):
                        split(f, u)
                    if not last_of(f, KF):
                        split(f + 1, 1 - u)
                    for x in range(2):
                        ch = f + x * KF
                        tap = lambda j: tp[:, bass.ds(ch, 1), j]
                        dve.wait_ge(u_copied, 8 * f + 4 * x + 4)
                        dve.wait_ge(state_set, 2 * f + x + 1)
                        if x == 0:
                            need(dve, y_done, f)
                        parts = ((cp[:, x, 0:SEQ], lambda j: up[:, x, j:j + SEQ]),
                                 (sample(cp[:, x]), lambda j: us[:, x, :, j:j + DS]))
                        for out, src in parts:
                            nc.vector.tensor_scalar(out, src(0), tap(0), tap(3), ALU.mult, ALU.add).then_inc(tap0, 1)
                        for j, prev, done in ((1, tap0, tap1), (2, tap1, tap2)):
                            for s, (out, src) in enumerate(parts):
                                dve.wait_ge(prev, 4 * f + 2 * x + s + 1)
                                nc.vector.scalar_tensor_tensor(out=out, in0=src(j), scalar=tap(j), in1=out,
                                                               op0=ALU.mult, op1=ALU.add).then_inc(done, 1)
                    dve.wait_ge(gelu_done, f + 1)
                    dve.wait_ge(tap2, 4 * f + 4)
                    need(dve, y_stored[u], 16 * i)
                    nc.vector.tensor_tensor(y[:, u], cp[:, 0], cp[:, 1], ALU.mult).then_inc(y_done, 1)
            repeat_ahead(dve, steps, body)

        @block.tensor
        def _(pe):
            def body(i):
                for u in range(U):
                    f = i * U + u
                    pe.wait_ge(lo_done, f + 1)
                    for x in range(2):
                        need(pe, u_copied, 8 * (f - 1) + 4 * x + 4)
                        for k in range(KD):
                            wh, wl = (w[:, u, x, k * P:k * P + P] for w in (w_hi, w_lo))
                            for n, (w, m) in enumerate(((wh, a_lo), (wh, a_hi), (wl, a_hi))):
                                for j, (c0, cn) in enumerate(SPANS):
                                    last = nc.tensor.matmul(g.ps[:, 3 * x + j, 0:cn], w, m[:, k, c0:c0 + cn],
                                                            start=(k == 0 and n == 0), stop=(k == KD - 1 and n == 2))
                        last.then_inc(u_in, 1)
            repeat(pe, steps, body)

        @block.gpsimd
        def _(pool):
            pool.wait_ge(tables_in, 32)

            def body(i):
                for u in range(U):
                    f = i * U + u
                    for x in range(2):
                        ch = bass.ds(f + x * KF, 1)
                        need(pool, tap2, 4 * (f - 1) + 2 * x + 2)
                        need(pool, state_kept, 4 * (f - 1) + 2 * x + 2)
                        nc.gpsimd.tensor_copy(us[:, x, :, 0:2],
                                              s_in[:, ch].rearrange("p o b j -> p (o b) j")).then_inc(state_set, 1)
                    for x in range(2):
                        ch = bass.ds(f + x * KF, 1)
                        pool.wait_ge(u_copied, 8 * f + 4 * x + 4)
                        nc.gpsimd.tensor_copy(s_new[:, ch, 0:2].rearrange("p o j -> p (o j)"),
                                              up[:, x, SEQ:SEQ + 2]).then_inc(state_kept, 1)
                        nc.gpsimd.tensor_copy(s_new[:, ch, 2:].rearrange("p o (b j) -> p (o b) j", j=2),
                                              us[:, x, :, DS:DS + 2]).then_inc(state_kept, 1)
                    pool.wait_ge(y_done, f + 1)
                    pool.dma_start(at(y_t, f)[:, 0:TOK], y[:, u]).then_inc(y_stored[u].sem, 16)
            repeat(pool, steps, body)
            pool.wait_ge(state_kept, 4 * KF)
            pool.dma_start(state_out, s_new[:]).then_inc(state_stored.sem, 16)
            state_stored.wait_all(pool, 16)
            for u in range(U):
                y_stored[u].wait_all(pool, 16 * steps)
    g.close()


def ffn_down(g, y_t, w_down, outs):
    nc = g.nc
    g.open("ffn_down")
    N = D // NC
    K2 = 2
    W = KF // K2
    raw = g.sb("raw", [P, 2, K2, NC])
    w_hi, w_lo = g.sb("w_hi", [P, KF, NC], F32R), g.sb("w_lo", [P, KF, NC], F32R)
    yr = g.sb("yr", [P, 2, KF, P])
    y_hi, y_lo = g.sb("y_hi", [P, 2, KF, P], F32R), g.sb("y_lo", [P, 2, KF, P], F32R)
    z = g.sb("z", [P, 2, NC])
    w_in = [g.sem(f"w_in{s}") for s in range(2)]
    y_in = [g.sem(f"y_in{s}") for s in range(2)]
    stored = [g.pool_sem(f"stored{s}") for s in range(2)]
    w_hi_done, w_lo_done, w_used = g.sem("w_hi_done"), g.sem("w_lo_done"), g.sem("w_used")
    y_hi_done, y_lo_done, z_done, z_out = g.sem("y_hi_done"), g.sem("y_lo_done"), g.sem("z_done"), g.sem("z_copied")
    T1 = TILES - 1
    items = [(n, t) for n in range(N) for t in range(TILES)]

    def used(x):
        n, t = items[x]
        return (z_done, n * T1 + t + 1) if t < T1 else (w_used, (n + 1) * KF)

    with nc.Block() as block:
        @block.sync
        def _(sp):
            g.clear_old(sp)

            def load_w(n, j):
                x = n * W + j
                if x >= 2:
                    sp.wait_ge(w_lo_done, (x - 1) * K2)
                sp.dma_start(raw[:, x % 2], w_down[n, :, j * K2:j * K2 + K2, :]).then_inc(w_in[x % 2], 16)

            def load_y(x):
                if x >= 2:
                    sp.wait_ge(y_lo_done, x - 1)
                sp.dma_start(yr[:, x % 2], y_t[:, :, items[x][1] * P:items[x][1] * P + P].rearrange(
                    "k p c -> p k c")).then_inc(y_in[x % 2], 16)

            load_y(0)
            for j in range(W):
                load_w(0, j)
            for x in range(1, len(items)):
                load_y(x)
                if items[x][1] == T1 and items[x][0] + 1 < N:
                    for j in range(2):
                        load_w(items[x][0] + 1, j)
                if items[x][1] == 0:
                    for j in range(2, W):
                        load_w(items[x][0], j)

        @block.scalar
        def _(act):
            def split_w(n):
                for k in range(KF):
                    x = n * W + k // K2
                    act.wait_ge(w_in[x % 2], 16 * (x // 2 + 1))
                    need(act, w_used, (n - 1) * KF + k + 1)
                    nc.scalar.activation(w_hi[:, k], raw[:, x % 2, k % K2], ACT.Copy).then_inc(w_hi_done, 1)

            def split_y(x):
                act.wait_ge(y_in[x % 2], 16 * (x // 2 + 1))
                if x >= 2:
                    act.wait_ge(*used(x - 2))
                nc.scalar.activation(y_hi[:, x % 2], yr[:, x % 2], ACT.Copy).then_inc(y_hi_done, 1)

            def evac(x):
                act.wait_ge(*used(x))
                need(act, stored[x % 2], 16 * (x // 2))
                nc.scalar.activation(z[:, x % 2], g.ps[:, x % 8], ACT.Copy).then_inc(z_out, 1)

            split_y(0)
            split_w(0)
            for x in range(len(items)):
                if x + 1 < len(items):
                    split_y(x + 1)
                    if items[x + 1][1] == 0:
                        split_w(items[x + 1][0])
                evac(x)

        @block.vector
        def _(dve):
            def split_w(n):
                for k in range(KF):
                    x = n * W + k // K2
                    dve.wait_ge(w_hi_done, n * KF + k + 1)
                    nc.vector.tensor_tensor(w_lo[:, k], raw[:, x % 2, k % K2], w_hi[:, k].bitcast(F32),
                                            ALU.subtract).then_inc(w_lo_done, 1)

            def split_y(x):
                dve.wait_ge(y_hi_done, x + 1)
                nc.vector.tensor_tensor(y_lo[:, x % 2], yr[:, x % 2], y_hi[:, x % 2].bitcast(F32),
                                        ALU.subtract).then_inc(y_lo_done, 1)

            split_y(0)
            split_w(0)
            for x in range(1, len(items)):
                split_y(x)
                if items[x][1] == 0:
                    split_w(items[x][0])

        @block.tensor
        def _(pe):
            for x, (n, t) in enumerate(items):
                pe.wait_ge(y_lo_done, x + 1)
                need(pe, z_out, x - 7)
                for k in range(KF):
                    if t == 0:
                        pe.wait_ge(w_lo_done, n * KF + k + 1)
                    o = g.ps[:, x % 8]
                    yh, yl = y_hi[:, x % 2, k], y_lo[:, x % 2, k]
                    nc.tensor.matmul(o, yl, w_hi[:, k], start=(k == 0), stop=False)
                    nc.tensor.matmul(o, yh, w_hi[:, k], start=False, stop=False)
                    last = nc.tensor.matmul(o, yh, w_lo[:, k], start=False, stop=(k == KF - 1))
                    if t == T1:
                        last.then_inc(w_used, 1)
                if t < T1:
                    last.then_inc(z_done, 1)

        @block.gpsimd
        def _(pool):
            for x, (n, t) in enumerate(items):
                pool.wait_ge(z_out, x + 1)
                pool.dma_start(outs(n, t)[0][0], z[:, x % 2]).then_inc(stored[x % 2].sem, 16)
            for s in range(2):
                stored[s].wait_all(pool, 16 * len(items) // 2)
    g.close()


def gates(g, a, w_f, b_f, logf_out, fgt):
    nc = g.nc
    g.open("gates")
    a_hi, a_lo = a
    wf = g.sb("wf", [P, KD, H_FOX])
    wh, wl = g.sb("wh", [P, KD, H_FOX], F32R), g.sb("wl", [P, KD, H_FOX], F32R)
    bias = g.sb("bias", [P, H_FOX])
    x, ax, e, up, ln, d, one, q, mn, lf, tot = (g.sb(n, [P, TILES, H_FOX]) for n in (
        "x", "ax", "e", "up", "ln", "d", "one", "q", "mn", "lf", "tot"))
    rest = g.sb("rest", [P, PT, H_FOX])
    w_in, hi_done, lo_done, z_done, x_done, abs_done, exp_done, up_done, ln_done, step, lf_done, sums_in, tot_done, \
        rest_done = (g.sem(s) for s in (
            "w_in hi_done lo_done z_done x_done abs_done exp_done up_done ln_done dve_step lf_done sums_in tot_done "
            "rest_done").split())
    stored = g.pool_sem("stored")
    with nc.Block() as block:
        @block.sync
        def _(sp):
            g.clear_old(sp)
            sp.dma_start(wf[:], w_f).then_inc(w_in, 16)
            sp.dma_start(bias[:], b_f).then_inc(w_in, 16)

        @block.scalar
        def _(act):
            act.wait_ge(w_in, 32)
            nc.scalar.activation(wh[:], wf[:], ACT.Copy).then_inc(hi_done, 1)
            act.wait_ge(x_done, 1)
            nc.scalar.activation(ax[:], x[:], ACT.Abs).then_inc(abs_done, 1)
            act.wait_ge(abs_done, 1)
            nc.scalar.activation(e[:], ax[:], ACT.Exp, scale=-1.0).then_inc(exp_done, 1)
            act.wait_ge(up_done, 1)
            nc.scalar.activation(ln[:], up[:], ACT.Ln).then_inc(ln_done, 1)

        @block.tensor
        def _(pe):
            pe.wait_ge(lo_done, 1)
            for t in range(TILES):
                for k in range(KD):
                    ah, al = a_hi[:, k, t * P:t * P + P], a_lo[:, k, t * P:t * P + P]
                    o = g.ps[:, 0, t * H_FOX:t * H_FOX + H_FOX]
                    nc.tensor.matmul(o, al, wh[:, k], start=(k == 0), stop=False)
                    nc.tensor.matmul(o, ah, wh[:, k], start=False, stop=False)
                    last = nc.tensor.matmul(o, ah, wl[:, k], start=False, stop=(k == KD - 1))
            last.then_inc(z_done, 1)
            pe.wait_ge(lf_done, 1)
            flat = lf[:, 0:PT].rearrange("p t h -> p (t h)")
            nc.tensor.matmul(g.ps[:, 1, 0:PT * H_FOX], g.later[:], flat, start=True, stop=True).then_inc(sums_in, 1)
            nc.tensor.matmul(g.ps[:, 2, 0:PT * H_FOX], g.ones[:], flat, start=True, stop=True).then_inc(sums_in, 1)

        @block.vector
        def _(dve):
            V = nc.vector
            dve.wait_ge(hi_done, 1)
            V.tensor_tensor(wl[:], wf[:], wh[:].bitcast(F32), ALU.subtract).then_inc(lo_done, 1)
            dve.wait_ge(z_done, 1)
            V.tensor_tensor(x[:], g.ps[:, 0, 0:TILES * H_FOX].rearrange("p (t h) -> p t h", h=H_FOX),
                            bc(bias[:], 1, TILES), ALU.add).then_inc(x_done, 1)
            dve.wait_ge(exp_done, 1)
            V.tensor_scalar(up[:], e[:], 1.0, None, ALU.add).then_inc(up_done, 1)
            dve.wait_ge(up_done, 1)
            V.tensor_scalar(d[:], up[:], -1.0, 1e-30, ALU.add, ALU.max).then_inc(step, 1)
            V.tensor_scalar(one[:], up[:], 1.0, None, ALU.is_equal).then_inc(step, 1)
            V.tensor_scalar(mn[:], x[:], 0.0, None, ALU.min).then_inc(step, 1)
            dve.wait_ge(step, 3)
            V.reciprocal(q[:], d[:]).then_inc(step, 1)
            dve.wait_ge(ln_done, 1)
            dve.wait_ge(step, 4)
            V.tensor_tensor(q[:], q[:], ln[:], ALU.mult).then_inc(step, 1)
            dve.wait_ge(step, 5)
            V.tensor_tensor(q[:], q[:], one[:], ALU.add).then_inc(step, 1)
            dve.wait_ge(step, 6)
            V.tensor_tensor(q[:], q[:], e[:], ALU.mult).then_inc(step, 1)
            dve.wait_ge(step, 7)
            V.tensor_tensor(lf[:], mn[:], q[:], ALU.subtract).then_inc(lf_done, 1)
            dve.wait_ge(sums_in, 2)
            V.tensor_copy(tot[:, 0:PT], g.ps[:, 2, 0:PT * H_FOX].rearrange("p (t h) -> p t h", h=H_FOX)).then_inc(
                tot_done, 1)
            V.memset(rest[:, PT - 1], 0.0).then_inc(rest_done, 1)
            dve.wait_ge(tot_done, 1)
            for t in range(PT - 2, -1, -1):
                dve.wait_ge(rest_done, PT - 1 - t)
                V.tensor_tensor(rest[:, t], rest[:, t + 1], tot[:, t + 1], ALU.add).then_inc(rest_done, 1)
            dve.wait_ge(rest_done, PT)
            V.tensor_tensor(fgt[:], g.ps[:, 1, 0:PT * H_FOX].rearrange("p (t h) -> p t h", h=H_FOX), rest[:],
                            ALU.add).then_inc(step, 1)

        @block.gpsimd
        def _(pool):
            pool.wait_ge(lf_done, 1)
            pool.dma_start(logf_out.rearrange("(t p) h -> p t h", p=P), lf[:]).then_inc(stored.sem, 16)
            stored.wait_all(pool, 16)
    g.close()


def fox_prompt(g, z, kv, fgt, cat):
    nc = g.nc
    g.open("fox_prompt")
    E = DH + 2
    q, k, v = (g.sb(n, [P, 2, PT, P]) for n in "qkv")
    qa, ka = g.sb("qa", [P, 2, PT, E]), g.sb("ka", [P, 2, PT, E])
    q_t, k_t = g.sb("q_t", [E, 2, SEQ]), g.sb("k_t", [E, 2, SEQ])
    mask = g.causal
    p = g.sb("p", [P, 2, SEQ])
    p_t = g.sb("p_t", [P, 2, PT, P])
    st = g.sb("st", [P, 2, 3])
    o = g.sb("o", [P, 2, PT, DH])
    qkv_in = [g.sem(f"qkv_in{s}") for s in range(2)]
    o_stored = [g.pool_sem(f"o_stored{s}") for s in range(2)]
    (ones_set, aug_done, turned, t_ready, scores_in, masked, max_done, exp_done, p_turned, p_ready, o_in, rsum_done,
     o_done) = (g.sem(x) for x in ("ones_set aug_done turned t_ready scores_in masked max_done exp_done p_turned "
                                   "p_ready o_in rsum_done o_done").split())
    groups = [(i + 4) // 4 for i in range(PT)]
    before = [sum(groups[:i]) for i in range(PT)]
    G8 = sum(groups)
    CP = 2
    steps = HP // CP
    LAST = (H_FOX * PT - 1, PT - 1, 1, H_FOX - 1, HP - 1, (HP - 1) % CP)

    with nc.Block() as block:
        @block.sync
        def _(sp):
            g.clear_old(sp)

            def body(i):
                for cc in range(CP):
                    c = i * CP + cc
                    need(sp, o_in, (c - CP + 1) * 2 * PT)
                    for dst, src, c0 in ((q, z, 0), (k, kv, 0), (v, kv, NF)):
                        sp.dma_start(dst[:, cc], at(src[0:SEQ, c0:c0 + NF].rearrange(
                            "(t p) (c d) -> c p t d", p=P, d=P), c)).then_inc(qkv_in[cc], 16)
            repeat(sp, steps, body)

        def setup_pe(pe, h, s):
            for r in range(4):
                pe.wait_ge(aug_done, 2 * h + r // 2 + 1)
                need(pe, t_ready, 4 * h + r)
                rows = (qa, ka)[r // 2]
                for x in range(4):
                    last = nc.tensor.transpose(g.ps[0:E, 0, x * P:x * P + P], rows[:, s, 4 * (r % 2) + x], g.ident[:])
                last.then_inc(turned, 1)

        def before_that(n, b, s, h, c, cc):
            return (n - 1, b - 1, s, h, c, cc) if b else (n - 1, PT - 1, 1 - s, h - 1, c if s else c - 1,
                                                          cc if s else 1 - cc)

        def turned_at(b, h):
            return (h * G8 if b >= 0 else (h - 1) * G8) + before[b % PT] + groups[b % PT]

        def walk(eng, body_of_item, ahead, at_mid, at_start=None):
            def body(i):
                for cc in range(CP):
                    for s in range(2):
                        h = (i * CP + cc) * 2 + s
                        for b in range(PT):
                            n = h * PT + b
                            if b == 1 and at_start and not last_of(h, H_FOX):
                                at_start(h + 1, 1 - s, i + (cc + s) // 2, (cc + s) % 2)
                            if b == 3 and not last_of(h, H_FOX):
                                at_mid(h + 1, 1 - s)
                            if not last_of(n, H_FOX * PT):
                                ahead(n + 1, (b + 1) % PT, *((s, h) if b + 1 < PT else (1 - s, h + 1)))
                            body_of_item(n, b, s, h, i * CP + cc, cc)
            repeat_ahead(eng, steps, body)

        @block.tensor
        def _(pe):
            setup_pe(pe, 0, 0)

            def scores(n, b, s, h):
                pe.wait_ge(t_ready, 4 * h + 4)
                need(pe, exp_done, n - 1)
                w = (b + 1) * P
                for c0 in range(0, w, 512):
                    c1 = min(w, c0 + 512)
                    last = nc.tensor.matmul(g.ps[:, 2 + 2 * (b % 2) + c0 // 512, 0:c1 - c0], q_t[:, s, b * P:b * P + P],
                                            k_t[:, s, c0:c1], start=True, stop=True)
                last.then_inc(scores_in, 1)

            scores(0, 0, 0, 0)

            def item(n, b, s, h, c, cc):
                pe.wait_ge(exp_done, n + 1)
                gr = h * G8 + before[b]
                for r in range(groups[b]):
                    need(pe, p_ready, gr + r - 1)
                    bank = 6 + (before[b] + r) % 2
                    for x in range(min(4, b + 1 - 4 * r)):
                        j = 4 * r + x
                        last = nc.tensor.transpose(g.ps[:, bank, x * P:x * P + P], p[:, b % 2, j * P:j * P + P],
                                                   g.ident[:])
                    last.then_inc(p_turned, 1)
                if not first(n):
                    weigh(*before_that(n, b, s, h, c, cc))

            def weigh(n, b, s, h, c, cc):
                need(pe, o_done, n)
                for j in range(b + 1):
                    if j % 4 == 0:
                        pe.wait_ge(p_ready, h * G8 + before[b] + j // 4 + 1)
                    last = nc.tensor.matmul(g.ps[:, 1, 0:DH], p_t[:, b % 2, j], v[:, cc, j, s * DH:s * DH + DH],
                                            start=(j == 0), stop=(j == b))
                last.then_inc(o_in, 1)

            walk(pe, item, scores, lambda h, s: setup_pe(pe, h, s))
            weigh(*LAST)

        @block.scalar
        def _(act):
            act.wait_ge(ones_set, 2)

            def augment(h, s, i, cc):
                need_all(act, (qkv_in[cc], 48 * i + 48), (turned, 4 * (h - 1)))
                half = slice(s * DH, s * DH + DH)
                f = fgt[:, :, bass.ds(h, 1)].rearrange("p t o -> p (t o)")
                nc.scalar.activation(qa[:, s, :, 0:DH], q[:, cc, :, half], ACT.Copy, scale=DH ** -0.5)
                nc.scalar.activation(qa[:, s, :, DH + 1], f, ACT.Copy, scale=-1.0).then_inc(aug_done, 1)
                nc.scalar.activation(ka[:, s, :, 0:DH], k[:, cc, :, half], ACT.Copy)
                nc.scalar.activation(ka[:, s, :, DH], f, ACT.Copy).then_inc(aug_done, 1)

            def setup(h, s):
                for r in range(4):
                    act.wait_ge(turned, 4 * h + r + 1)
                    if r == 0:
                        need(act, scores_in, (h - 1) * PT)
                    dst = (q_t, k_t)[r // 2]
                    nc.scalar.activation(dst[:, s, (r % 2) * 512:(r % 2) * 512 + 512], g.ps[0:E, 0, :],
                                         ACT.Copy).then_inc(t_ready, 1)

            augment(0, 0, 0, 0)
            setup(0, 0)

            def item(n, b, s, h, c, cc):
                act.wait_ge(max_done, n + 1)
                need(act, p_turned, turned_at(b - 2, h))
                need(act, rsum_done, n - 1)
                nc.scalar.activation(p[:, b % 2, 0:(b + 1) * P], g.ps[:, 2 + 2 * (b % 2):4 + 2 * (b % 2), :].rearrange(
                    "p a c -> p (a c)")[:, 0:(b + 1) * P], ACT.Exp, bias=st[:, b % 2, 0:1],
                                     accum_out=st[:, b % 2, 1:2]).then_inc(exp_done, 1)
            walk(act, item, lambda *_: None, setup, augment)

        @block.vector
        def _(dve):
            nc.vector.memset(qa[:, :, :, DH], 1.0).then_inc(ones_set, 1)
            nc.vector.memset(ka[:, :, :, DH + 1], 1.0).then_inc(ones_set, 1)

            def row_max(n, b, s, h):
                dve.wait_ge(scores_in, n + 1)
                flat = g.ps[:, 2 + 2 * (b % 2):4 + 2 * (b % 2), :].rearrange("p a c -> p (a c)")
                diag = flat[:, b * P:b * P + P]
                nc.vector.tensor_tensor(diag, diag, mask[:], ALU.add).then_inc(masked, 1)
                dve.wait_ge(masked, n + 1)
                need(dve, exp_done, n - 1)
                nc.vector.tensor_reduce(st[:, b % 2, 0:1], flat[:, 0:(b + 1) * P], AX.X, ALU.max,
                                        negate=True).then_inc(max_done, 1)

            row_max(0, 0, 0, 0)

            def item(n, b, s, h, c, cc):
                gr = h * G8 + before[b]
                for r in range(groups[b]):
                    dve.wait_ge(p_turned, gr + r + 1)
                    need(dve, o_in, n - 1)
                    m = min(4, b + 1 - 4 * r)
                    nc.vector.tensor_copy(p_t[:, b % 2, 4 * r:4 * r + m], g.ps[:, 6 + (before[b] + r) % 2, 0:m * P].rearrange(
                        "p (x r) -> p x r", x=m)).then_inc(p_ready, 1)
                need(dve, o_done, n - 1)
                nc.vector.reciprocal(st[:, b % 2, 2:3], st[:, b % 2, 1:2]).then_inc(rsum_done, 1)
                if not first(n):
                    divide(*before_that(n, b, s, h, c, cc))

            def divide(n, b, s, h, c, cc):
                dve.wait_ge(rsum_done, n + 1)
                dve.wait_ge(o_in, n + 1)
                if b == 0:
                    need(dve, o_stored[s], 16 * c)
                nc.vector.tensor_scalar(o[:, s, b], g.ps[:, 1, 0:DH], st[:, b % 2, 2:3], None, ALU.mult).then_inc(
                    o_done, 1)
            walk(dve, item, row_max, lambda *_: None)
            divide(*LAST)

        @block.gpsimd
        def _(pool):
            def body(i):
                for cc in range(CP):
                    for s in range(2):
                        h = (i * CP + cc) * 2 + s
                        if not first(h):
                            store(pool, h - 1, 1 - s)

            def store(pool, h, s):
                pool.wait_ge(o_done, (h + 1) * PT)
                pool.dma_start(at(cat[0:SEQ, 0:NF].rearrange("(t p) (h d) -> h p t d", p=P, d=DH), h),
                               o[:, s]).then_inc(o_stored[s].sem, 16)
            repeat(pool, steps, body)
            store(pool, H_FOX - 1, 1)
            for s in range(2):
                o_stored[s].wait_all(pool, 16 * HP)
    g.close()


def page_gates(g, pages, cache_f, logf, t_in, fg_out):
    nc = g.nc
    g.open("page_gates")
    NP = cache_f.shape[1]
    R = DB * PAGES
    ids, idf = g.sb("ids", [P, R], I32), g.sb("idf", [P, R])
    phys = g.sb("phys", [P, NP])
    lp = g.sb("lp", [P, NP, PAGE * H_FOX])
    hot = g.sb("hot", [P, NP, R])
    pp, pt, off = g.sb("pp", [P, NP, H_FOX]), g.sb("pt", [P, 2, H_FOX]), g.sb("off", [P, 2, H_FOX])
    lf, fg = g.sb("lf", [P, H_FOX, R]), g.sb("fg", [P, 2, H_FOX, PAGE])
    lfs = g.sb("lfs", [NS, H_FOX])
    later_pages, batch_sel = g.sb("later_pages", [P, P]), g.sb("batch_sel", [NS, 2, P])
    ids_in, tables_in, pages_in, f_done, hot_done, pp_done, pt_in, pt_done, off_in, off_done, lf_in, lf_done, \
        fg_in, fg_done, stored = (g.sem(n) for n in ("ids_in tables_in pages_in f_done hot_done pp_done pt_in pt_done off_in "
                                             "off_done lf_in lf_done fg_in fg_done stored").split())
    with nc.Block() as block:
        @block.sync
        def _(sp):
            g.clear_old(sp)
            sp.dma_start(ids[:], pages.broadcast_to([P, R])).then_inc(ids_in, 16)
            for dst, src in ((phys, t_in["phys"]), (later_pages, t_in["later_pages"]), (batch_sel, t_in["batch_sel"]),
                             (lfs, logf[SEQ:SEQ + NS])):
                sp.dma_start(dst[:], src).then_inc(tables_in, 16)
            sp.dma_start(lp[:], cache_f).then_inc(pages_in, 16)
            for x in range(2):
                sp.wait_ge(fg_done, 2 * H_FOX - 1 + x)
                sp.dma_start(fg_out.rearrange("h (x b) (g k) -> x (b g) h k", x=2, k=PAGE)[x], fg[:, x]).then_inc(
                    stored, 16)
            sp.wait_ge(stored, 32)

        @block.vector
        def _(dve):
            V = nc.vector
            dve.wait_ge(ids_in, 16)
            V.tensor_copy(idf[:], ids[:]).then_inc(f_done, 1)
            dve.wait_ge(f_done, 1)
            dve.wait_ge(tables_in, 64)
            for x in range(NP):
                V.tensor_scalar(hot[:, x], idf[:], phys[:, x:x + 1], None, ALU.is_equal).then_inc(hot_done, 1)
            dve.wait_ge(pages_in, 16)
            for x in range(NP):
                V.tensor_reduce(pp[:, x], lp[:, x].rearrange("p (k h) -> p h k", h=H_FOX), AX.X,
                                ALU.add).then_inc(pp_done, 1)
            dve.wait_ge(pt_in, 1)
            V.tensor_copy(pt[:], g.ps[:, 0, 0:2 * H_FOX].rearrange("p (a h) -> p a h", a=2)).then_inc(pt_done, 1)
            dve.wait_ge(off_in, 1)
            V.tensor_copy(off[:], g.ps[:, 1, 0:2 * H_FOX].rearrange("p (a h) -> p a h", a=2)).then_inc(off_done, 1)
            dve.wait_ge(off_done, 1)
            for h in range(H_FOX):
                dve.wait_ge(fg_in, h + 1)
                for half in range(2):
                    V.tensor_scalar(fg[:, half, h], g.ps[:, 6 + h % 2, half * P:half * P + P], off[:, half, h:h + 1], None,
                                    ALU.add).then_inc(fg_done, 1)

        @block.scalar
        def _(act):
            for h in range(H_FOX):
                act.wait_ge(lf_in, h + 1)
                nc.scalar.activation(lf[:, h], g.ps[:, 2 + h % 4, 0:R], ACT.Copy).then_inc(lf_done, 1)

        @block.tensor
        def _(pe):
            pe.wait_ge(hot_done, NP)
            pe.wait_ge(pp_done, NP)
            for half in range(2):
                for x in range(NP):
                    last = nc.tensor.matmul(g.ps[:, 0, half * H_FOX:half * H_FOX + H_FOX],
                                            hot[:, x, half * P:half * P + P], pp[:, x], start=(x == 0),
                                            stop=(x == NP - 1))
            last.then_inc(pt_in, 1)

            def gather(h):
                need(pe, lf_done, h - 3)
                for x in range(NP):
                    last = nc.tensor.matmul(g.ps[:, 2 + h % 4, 0:R],
                                            lp[:, x].rearrange("p (k h) -> p h k", h=H_FOX)[:, h], hot[:, x],
                                            start=(x == 0), stop=(x == NP - 1))
                last.then_inc(lf_in, 1)
            gather(0)
            pe.wait_ge(pt_done, 1)
            for half in range(2):
                nc.tensor.matmul(g.ps[:, 1, half * H_FOX:half * H_FOX + H_FOX], later_pages[:], pt[:, half],
                                 start=True, stop=False)
                last = nc.tensor.matmul(g.ps[:, 1, half * H_FOX:half * H_FOX + H_FOX], batch_sel[:, half], lfs[:],
                                        start=False, stop=True)
            last.then_inc(off_in, 1)
            for h in range(H_FOX):
                if h + 1 < H_FOX:
                    gather(h + 1)
                pe.wait_ge(lf_done, h + 1)
                need(pe, fg_done, 2 * (h - 1))
                for half in range(2):
                    last = nc.tensor.matmul(g.ps[:, 6 + h % 2, half * P:half * P + P], lf[:, h, half * P:half * P + P],
                                            g.later[:], start=True, stop=True)
                last.then_inc(fg_in, 1)
    g.close()


def fox_sample(g, z, kv, logf, pages, cache_k, cache_v, fg_in_dram, t_in, cat):
    nc = g.nc
    g.open("fox_sample")
    HT = H_FOX * DS
    KS = 16
    GP = 4
    NG = PAGES // GP
    W = GP * PAGE
    KEYS = PAGES * PAGE
    QW = HT + 2 * DS
    PIECES = ((0, 1), (1, 4), (4, NG))
    ids = g.sb("ids", [1, DB * PAGES], I32)
    kr, vr = g.sb("kr", [P, KS, HP, PAGE]), g.sb("vr", [P, KS, NF])
    fg = g.sb("fg", [HT, 2, KEYS // 2])
    qk = g.sb("qk", [NS, 2 * NF])
    qb = g.sb("qb", [P, DB, HP, 2, DS])
    kn = g.sb("kn", [P, HP, DB, DS])
    vn = g.sb("vn", [DS, DB, NF])
    lfn, lfw = g.sb("lfn", [NS, H_FOX]), g.sb("lfw", [NS, H_FOX, DS])
    later_new, new_mask = g.sb("later_new", [NS, NS]), g.sb("new_mask", [HT, DS])
    fn = g.sb("fn", [HT, DB, DS])
    own, fold = g.sb("own", [HT, NF]), g.sb("fold", [HT, DS])
    qc, kc, vc = g.sb("qc", [P, HP * QW]), g.sb("kc", [P, HP, DS]), g.sb("vc", [DS, NF])
    sc = g.sb("sc", [HT, KEYS + DS])
    gm, nm = g.sb("gm", [HT, NG + 1]), g.sb("nm", [HT, 1])
    sums, sm, rs = g.sb("sums", [HT, len(PIECES)]), g.sb("sm", [HT, 1]), g.sb("rs", [HT, 1])
    pt = g.sb("pt", [P, 2, GP + 1, HT])
    om = g.sb("om", [HT, NF])
    kin = [g.sem(f"k_in{s}") for s in range(KS)]
    vin = [g.sem(f"v_in{s}") for s in range(KS)]
    (ids_in, ids_done, tables_in, rows_in, fg_in, fg_in2, zeroed, turned, q_set, lfw_done, fn_in, fn_done, qk_set, v_set,
     k_used, v_used, new_in, scores_out, new_out, group_max, max_done, exp_done, sm_done, rs_done, p_turned, p_ready,
     o_in, o_done, folded, back) = (g.sem(n) for n in (
         "ids_in ids_done tables_in rows_in fg_in fg_in2 zeroed turned q_set lfw_done fn_in fn_done qk_set v_set k_used "
         "v_used new_in scores_out new_out group_max max_done exp_done sm_done rs_done p_turned p_ready o_in "
         "o_done folded back").split())
    fg_sems = (fg_in, fg_in2)
    stored = g.pool_sem("stored")

    def slot(j):
        return j % KS

    def fills(b, j):
        return b * (PAGES // KS) + j // KS + 1

    def piece_of(x):
        return [x < j1 for _, j1 in PIECES].index(True)

    with nc.Block() as block:
        @block.sync
        def _(sp):
            g.clear_old(sp)
            sp.dma_start(ids[:], pages).then_inc(ids_in, 16)
            sp.dma_start(qk[:, 0:NF], at(z, PT)[0:NS, 0:NF]).then_inc(rows_in, 16)
            sp.dma_start(qk[:, NF:], at(kv, PT)[0:NS, 0:NF]).then_inc(rows_in, 16)
            sp.dma_start(vn[:], at(kv, PT)[0:NS, NF:].rearrange("(b t) c -> t b c", b=DB)).then_inc(rows_in, 16)
            for dst, src in ((lfn, logf[SEQ:SEQ + NS]), (later_new, t_in["later_new"]), (new_mask, t_in["new_mask"]),
                             (own, t_in["own_head"]), (fold, t_in["fold"])):
                sp.dma_start(dst[:], src).then_inc(tables_in, 16)

            def load_fg(b, x):
                need(sp, scores_out, (b - 1) * NG + (x + 1) * NG // 2)
                sp.dma_start(fg[:, x], bc(at(fg_in_dram.rearrange("h b n -> b h n"), b)[
                    :, x * KEYS // 2:(x + 1) * KEYS // 2], 1, DS)).then_inc(fg_sems[x], 16)

            def load(ring, arrived, free, value, cache, b, j):
                page = nc.values_load(ids[0:1, bass.ds(b * PAGES + j, 1)], engines=[sp.engine], min_val=0,
                                      max_val=cache.shape[0] - 1,
                                      skip_runtime_bounds_check_because="DVE has clamped the page numbers")
                need(sp, free, value)
                sp.dma_start(ring[:, slot(j)], at_page(cache, page)).then_inc(arrived[slot(j)], 16)

            def load_k(b, j):
                load(kr, kin, k_used, b * NG + (j - KS) // GP + 1, cache_k, b, j)

            def load_v(b, j):
                load(vr, vin, v_used, b * PAGES + j - KS + 1, cache_v, b, j)

            def body(b):
                for x in range(NG):
                    if not last_of(b, DB):
                        if x % (NG // 2) == 0:
                            load_fg(b + 1, x // (NG // 2))
                        for j in range(x * GP, x * GP + GP):
                            load_k(b + 1, j)
                    for j in range(x * GP, x * GP + GP):
                        load_v(b, j)
            sp.wait_ge(ids_done, 1)
            for x in range(2):
                load_fg(0, x)
            for j in range(PAGES):
                load_k(0, j)
            repeat_ahead(sp, DB, body)

        @block.gpsimd
        def _(pool):
            nc.gpsimd.memset(qc[:], 0.0).then_inc(zeroed, 1)
            nc.gpsimd.memset(qb[:], 0.0).then_inc(zeroed, 1)
            pool.wait_ge(zeroed, 2)
            pool.wait_ge(q_set, 2)
            pool.wait_ge(rows_in, 48)

            def queries(b):
                need(pool, new_in, b)
                nc.gpsimd.tensor_copy(qc[:].rearrange("p (c w) -> p c w", w=QW)[:, :, 0:2 * DS],
                                      qb[:, bass.ds(b, 1)].rearrange("p o c f t -> p (o c) (f t)"))
                nc.gpsimd.tensor_copy(kc[:], kn[:, :, bass.ds(b, 1)].rearrange("p c o t -> p c (o t)")).then_inc(
                    qk_set, 1)

            def body(b):
                need(pool, o_in, b)
                nc.gpsimd.tensor_copy(vc[:], vn[:, bass.ds(b, 1)].rearrange("p o c -> p (o c)")).then_inc(v_set, 1)
                if not last_of(b, DB):
                    queries(b + 1)
            queries(0)
            repeat_ahead(pool, DB, body)
            pool.wait_ge(back, 2 * DB)
            pool.dma_start(at(cat, PT)[0:NS, 0:NF].rearrange("(b t) c -> t b c", b=DB), vn[:]).then_inc(stored.sem, 16)
            stored.wait_all(pool, 16)

        @block.tensor
        def _(pe):
            pe.wait_ge(rows_in, 48)
            for x in range(2):
                for c in range(HP):
                    last = nc.tensor.transpose(g.ps[:, x, c * NS:c * NS + NS], qk[:, x * NF + c * P:x * NF + c * P + P],
                                               g.ident[0:NS, 0:NS])
                last.then_inc(turned, 1)
            pe.wait_ge(lfw_done, 1)
            nc.tensor.matmul(g.ps[0:HT, 6, 0:NS], lfw[:].rearrange("p h t -> p (h t)"), later_new[:], start=True,
                             stop=True).then_inc(fn_in, 1)
            pe.wait_ge(q_set, 2)

            def own_queries(c):
                return qc[:, c * HT:c * HT + HT]

            def score(b, x):
                need(pe, scores_out, b * NG + x - 1)
                for j in range(x * GP, x * GP + GP):
                    pe.wait_ge(kin[slot(j)], 16 * fills(b, j))
                s0 = slot(x * GP)
                for c in range(HP):
                    last = nc.tensor.matmul(g.ps[0:HT, x % 2, :], own_queries(c), kr[:, s0:s0 + GP, c], start=(c == 0),
                                            stop=(c == HP - 1))
                last.then_inc(k_used, 1)

            def score_new(b):
                need(pe, back, 2 * (b - 1))
                if first(b):
                    pe.wait_ge(fn_done, 1)
                for c in range(HP):
                    last = nc.tensor.matmul(g.ps[0:HT, 6, 0:DS], own_queries(c), kc[:, c], start=(c == 0),
                                            stop=(c == HP - 1))
                last.then_inc(new_in, 1)

            def turn(b, x):
                pe.wait_ge(exp_done, len(PIECES) * b + piece_of(x) + 1)
                need(pe, p_ready, b * NG + x - 1)
                for y in range(GP):
                    last = nc.tensor.transpose(g.ps[:, 2 + x % 2, y * HT:y * HT + HT],
                                               sc[:, x * W + y * PAGE:x * W + (y + 1) * PAGE], g.ident[0:HT, 0:HT])
                if x == NG - 1:
                    last = nc.tensor.transpose(g.ps[0:DS, 2 + x % 2, GP * HT:(GP + 1) * HT], sc[:, KEYS:],
                                               g.ident[0:HT, 0:HT])
                last.then_inc(p_turned, 1)

            def weigh(b, x):
                pe.wait_ge(p_ready, b * NG + x + 1)
                if x == 0:
                    need(pe, o_done, 2 * b)
                for y in range(GP):
                    j = x * GP + y
                    pe.wait_ge(vin[slot(j)], 16 * fills(b, j))
                    for bank, c0, c1 in ((4, 0, 512), (5, 512, NF)):
                        last = nc.tensor.matmul(g.ps[0:HT, bank, 0:c1 - c0], pt[:, x % 2, y], vr[:, slot(j), c0:c1],
                                                start=(j == 0), stop=False)
                    last.then_inc(v_used, 1)
                if x == NG - 1:
                    pe.wait_ge(v_set, b + 1)
                    for bank, c0, c1 in ((4, 0, 512), (5, 512, NF)):
                        last = nc.tensor.matmul(g.ps[0:HT, bank, 0:c1 - c0], pt[0:DS, x % 2, GP], vc[:, c0:c1],
                                                start=False, stop=True)
                    last.then_inc(o_in, 1)

            def fold_o(b):
                pe.wait_ge(o_done, 2 * b + 2)
                for bank, c0, c1 in ((6, 0, 512), (7, 512, NF)):
                    last = nc.tensor.matmul(g.ps[0:DS, bank, 0:c1 - c0], fold[:], om[:, c0:c1], start=True, stop=True)
                last.then_inc(folded, 1)

            pe.wait_ge(tables_in, 80)
            pe.wait_ge(qk_set, 1)
            for x in range(NG):
                score(0, x)
            score_new(0)

            def body(b):
                if not last_of(b, DB):
                    pe.wait_ge(qk_set, b + 2)
                for x in range(NG):
                    if not last_of(b, DB):
                        score(b + 1, x)
                    turn(b, x)
                    if x == 0 and not first(b):
                        pe.wait_ge(new_out, b + 1)
                        fold_o(b - 1)
                    if x > 0:
                        weigh(b, x - 1)
                if not last_of(b, DB):
                    score_new(b + 1)
                weigh(b, NG - 1)
            repeat_ahead(pe, DB, body)
            fold_o(DB - 1)

        @block.scalar
        def _(act):
            act.wait_ge(turned, 1)
            act.wait_ge(zeroed, 2)
            for h in range(H_FOX):
                half = slice((h % 2) * DH, (h % 2) * DH + DH)
                last = nc.scalar.activation(
                    qb[half, :, h // 2, h % 2], g.ps[half, 0, (h // 2) * NS:(h // 2) * NS + NS].rearrange(
                        "p (b t) -> p b t", b=DB), ACT.Copy, scale=DH ** -0.5)
            last.then_inc(q_set, 1)
            act.wait_ge(turned, 2)
            nc.scalar.activation(kn[:].rearrange("p c b t -> p c (b t)"), g.ps[:, 1, 0:HP * NS].rearrange(
                "p (c r) -> p c r", c=HP), ACT.Copy).then_inc(q_set, 1)

            def body(b):
                act.wait_ge(max_done, b + 1)
                need(act, sm_done, b)
                for i, (x0, x1) in enumerate(PIECES):
                    cols = sc[:, x0 * W:x1 * W if x1 < NG else KEYS + DS]
                    nc.scalar.activation(cols, cols, ACT.Exp, bias=nm[:], accum_out=sums[:, i:i + 1]).then_inc(
                        exp_done, 1)
                for x in range(NG):
                    act.wait_ge(p_turned, b * NG + x + 1)
                    need(act, v_used, b * PAGES + (x - 1) * GP)
                    if x == 1:
                        need(act, o_in, b)
                    if x == NG - 1:
                        nc.scalar.activation(pt[0:DS, x % 2, GP], g.ps[0:DS, 2 + x % 2, GP * HT:(GP + 1) * HT],
                                             ACT.Copy)
                    nc.scalar.activation(pt[:, x % 2, 0:GP].rearrange("p y r -> p (y r)"),
                                         g.ps[:, 2 + x % 2, 0:GP * HT], ACT.Copy).then_inc(p_ready, 1)
                    if x == 0 and not first(b):
                        output(b - 1)

            def output(b):
                act.wait_ge(folded, b + 1)
                act.wait_ge(v_set, b + 1)
                for bank, c0, c1 in ((6, 0, 512), (7, 512, NF)):
                    nc.scalar.activation(vn[:, bass.ds(b, 1), c0:c1].rearrange("p o c -> p (o c)"),
                                         g.ps[0:DS, bank, 0:c1 - c0], ACT.Copy).then_inc(back, 1)
            repeat(act, DB, body)
            output(DB - 1)

        @block.vector
        def _(dve):
            V = nc.vector
            dve.wait_ge(ids_in, 16)
            V.tensor_scalar(ids[:], ids[:], 0, cache_k.shape[0] - 1, ALU.max, ALU.min).then_inc(ids_done, 1)
            dve.wait_ge(tables_in, 80)
            V.tensor_copy(lfw[:], bc(lfn[:], 2, DS)).then_inc(lfw_done, 1)
            dve.wait_ge(fn_in, 1)
            V.tensor_tensor(fn[:], g.ps[0:HT, 6, 0:NS].rearrange("p (b t) -> p b t", b=DB), bc(new_mask[:], 1, DB),
                            ALU.add).then_inc(fn_done, 1)
            dve.wait_ge(fn_done, 1)

            def softmax(b):
                need(dve, max_done, b)
                for x in range(NG):
                    cols = sc[:, x * W:x * W + W]
                    dve.wait_ge(k_used, b * NG + x + 1)
                    need(dve, p_turned, (b - 1) * NG + x + 1)
                    if x % (NG // 2) == 0:
                        dve.wait_ge(fg_sems[x // (NG // 2)], 16 * b + 16)
                    V.tensor_tensor(cols, g.ps[0:HT, x % 2, :],
                                    fg[:, x // (NG // 2), (x % (NG // 2)) * W:(x % (NG // 2)) * W + W],
                                    ALU.add).then_inc(scores_out, 1)
                    dve.wait_ge(scores_out, b * NG + x + 1)
                    V.tensor_reduce(gm[:, x:x + 1], cols, AX.X, ALU.max).then_inc(group_max, 1)
                dve.wait_ge(new_in, b + 1)
                V.tensor_tensor(sc[:, KEYS:], g.ps[0:HT, 6, 0:DS], fn[:, bass.ds(b, 1)].rearrange("p o t -> p (o t)"),
                                ALU.add).then_inc(new_out, 1)
                dve.wait_ge(new_out, b + 1)
                V.tensor_reduce(gm[:, NG:], sc[:, KEYS:], AX.X, ALU.max).then_inc(group_max, 1)
                dve.wait_ge(group_max, (b + 1) * (NG + 1))
                V.tensor_reduce(nm[:], gm[:], AX.X, ALU.max, negate=True).then_inc(max_done, 1)
                if not first(b):
                    divide(b - 1)
                dve.wait_ge(exp_done, len(PIECES) * (b + 1))
                V.tensor_reduce(sm[:], sums[:], AX.X, ALU.add).then_inc(sm_done, 1)
                dve.wait_ge(sm_done, b + 1)
                need(dve, o_done, 2 * b)
                V.reciprocal(rs[:], sm[:]).then_inc(rs_done, 1)

            def divide(b):
                dve.wait_ge(rs_done, b + 1)
                dve.wait_ge(o_in, b + 1)
                need(dve, folded, b)
                for bank, c0, c1 in ((4, 0, 512), (5, 512, NF)):
                    V.scalar_tensor_tensor(om[:, c0:c1], g.ps[0:HT, bank, 0:c1 - c0], rs[:], own[:, c0:c1], ALU.mult,
                                           ALU.mult).then_inc(o_done, 1)
            repeat(dve, DB, softmax)
            divide(DB - 1)
    g.close()


def at_page(cache, page):
    return cache[bass.ds(page, 1)].rearrange("o p n -> (o p) n")


def build(nc, d):
    def scratch(name, shape):
        return nc.dram_tensor(name, shape, F32, kind="Internal").ap()

    def tiles(ap):
        return ap.rearrange("(t p) c -> t p c", p=P)

    h1, h2, h3 = (tiles(scratch(f"h{i}", [ROWS, D])) for i in (1, 2, 3))
    z_a, z_b = scratch("z_a", [ROWS, NZ]), scratch("z_b", [ROWS, D])
    cat, o, f = scratch("cat", [ROWS, D]), scratch("o", [ROWS, D]), scratch("f", [ROWS, D])
    y_t = scratch("y_t", [KF, P, ROWS])
    with ExitStack() as ctx:
        g = Program(nc, ctx)
        for name in ("ident", "later", "ones", "causal"):
            t = ctx.enter_context(nc.sbuf_tensor(name, [P, P], F32))
            if name == "ident":
                g.ident = t
            elif name == "later":
                g.later = t
            elif name == "ones":
                g.ones = t
            else:
                g.causal = t
        fgt = ctx.enter_context(nc.sbuf_tensor("fgt", [P, PT, H_FOX], F32))

        def operands():
            m = ExitStack()
            a = tuple(m.enter_context(nc.sbuf_tensor(f"a_{x}{g.n}", [P, KD, ROWS], F32R)) for x in ("hi", "lo"))
            return m, a

        m, a = operands()
        g.open("setup")
        mem_t, zero = g.sb("mem_t", [P, KD, N_MEM]), g.sb("zero", [P, D])
        const_in, mem_in, hi_done, lo_done, zeroed, zero_out = (g.sem(s) for s in (
            "const_in mem_in hi_done lo_done zeroed zero_out").split())
        with nc.Block() as block:
            @block.sync
            def _(sp):
                for t, name in ((g.ident, "ident"), (g.later, "later"), (g.ones, "ones"), (g.causal, "causal")):
                    sp.dma_start(t[:], d[name]).then_inc(const_in, 16)
                sp.dma_start(mem_t[:], d["mem_t"]).then_inc(mem_in, 16)
                sp.wait_ge(zeroed, 1)
                sp.dma_start(cat[TOK:], zero[0:ROWS - TOK]).then_inc(zero_out, 16)
                for k in range(KF):
                    sp.dma_start(y_t[k, :, TOK:], zero[:, 0:ROWS - TOK]).then_inc(zero_out, 16)
                sp.wait_ge(zero_out, 16 * (KF + 1))
                sp.wait_ge(const_in, 64)

            @block.vector
            def _(dve):
                nc.vector.memset(zero[:], 0.0).then_inc(zeroed, 1)
                dve.wait_ge(hi_done, 1)
                nc.vector.tensor_tensor(a[1][:, :, 0:N_MEM], mem_t[:], a[0][:, :, 0:N_MEM].bitcast(F32),
                                        ALU.subtract).then_inc(lo_done, 1)

            @block.scalar
            def _(act):
                act.wait_ge(mem_in, 16)
                nc.scalar.activation(a[0][:, :, 0:N_MEM], mem_t[:], ACT.Copy).then_inc(hi_done, 1)
        g.close()
        mk, mv = d["mem_k"], d["mem_v"]

        def mem_outs(n, t):
            return [(at(mk, n)[t * P:t * P + P], 0, N_MEM), (at(mv, n)[t * P:t * P + P], N_MEM, NC)]
        project(g, a, d["w_mem"], DEPTH, MT, mem_outs)

        normalise(g, a, tiles(d["x"]), gain=d["g_pre"][0])
        project(g, a, d["w_in_a"], NZ // NC, TILES, columns(z_a, TILES), silu=(0, 0, 0, NC, NC // 2))
        m.close()
        prompt = {n: d[f"p_{n}"] for n in ("dmask", "qdec", "kdec", "sdec")}
        sample = {n: d[f"s_{n}"] for n in ("dmask", "qdec", "kdec", "sdec")}
        prompt["rope"] = sample["rope"] = tiles(d["rope"])
        retention(g, tiles(z_a), prompt, tiles(cat), None, d["ret_p"], False)
        retention(g, tiles(z_a), sample, tiles(cat), d["state_ret"], d["ret_s"], True)
        mem_prompt(g, tiles(z_a), Z_M, mk[0], mv[0], tiles(cat))
        mem_sample(g, tiles(z_a), Z_M, d["cache_mem_kt"][0], d["cache_mem_v"][0], tiles(cat))
        m, a = operands()
        normalise(g, a, tiles(cat), plain=True)
        project(g, a, d["w_out_a"], D // NC, TILES, columns(o, TILES))

        def ffn(layer, h_in, h_mid, m, a):
            normalise(g, a, h_in, gain=d["g_pre"][2 + layer], residual=(tiles(o), d["g_mix_post"][layer]), h_out=h_mid)
            ffn_up(g, a, d["w_up"][layer], d["taps"][layer], d["state_conv"][layer], y_t, d["conv"][layer])
            m.close()
            ffn_down(g, y_t, d["w_down"][layer], columns(f, TILES))
        ffn(0, tiles(d["x"]), h1, m, a)

        m, a = operands()
        normalise(g, a, h1, gain=d["g_pre"][4], residual=(tiles(f), d["g_ffn_post"][0]), h_out=h2)
        project(g, a, d["w_kv"], 2 * NF // NC, TILES, columns(d["kv"], TILES))
        gates(g, a, d["w_f"], d["b_f"], d["logf"], fgt)
        normalise(g, a, h2, gain=d["g_pre"][1])
        project(g, a, d["w_in_b"], D // NC, TILES, columns(z_b, TILES))
        m.close()
        fg = scratch("fg", [H_FOX, DB, PAGES * PAGE])
        page_gates(g, d["page_table"], d["cache_logf"], d["logf"], d, fg)
        fox_prompt(g, z_b, d["kv"], fgt, cat)
        mem_prompt(g, tiles(z_b), NF, mk[1], mv[1], tiles(cat))
        mem_sample(g, tiles(z_b), NF, d["cache_mem_kt"][1], d["cache_mem_v"][1], tiles(cat))
        fox_sample(g, tiles(z_b), tiles(d["kv"]), d["logf"], d["page_table"], d["cache_kt"], d["cache_v"], fg, d,
                   tiles(cat))
        m, a = operands()
        normalise(g, a, tiles(cat), plain=True)
        project(g, a, d["w_out_b"], D // NC, TILES, columns(o, TILES))
        ffn(1, h2, h3, m, a)
        normalise(g, None, h3, residual=(tiles(f), d["g_ffn_post"][1]), h_out=tiles(d["y"]))


def tables():
    import numpy as np
    f = np.float32
    t = {}
    i = np.arange(P)
    t["ident"] = np.eye(P, dtype=f)
    t["later"] = (i[:, None] > i[None, :]).astype(f)
    t["ones"] = np.ones((P, P), f)
    t["causal"] = np.where(i[None, :] <= i[:, None], 0.0, NEG).astype(f)
    inv = (f(10000.0) ** (-np.arange(32, dtype=f) / f(32))).astype(f)
    pos = np.concatenate([np.arange(SEQ), np.tile(PAGES * PAGE + np.arange(DS), DB), np.zeros(ROWS - TOK)]).astype(f)
    ang = (pos[:, None] * inv[None]).astype(f)
    t["rope"] = np.concatenate([np.cos(ang), np.sin(ang)], axis=1).astype(f)
    lg = np.log1p(-(2.0 ** (-5.0 - np.arange(H_RET))))

    def decay(name, C, B):
        R = C * B
        n, b = np.arange(R) % C, np.arange(R) // C
        same = b[:, None] == b[None, :]
        rel = n[None, :] - n[:, None]
        t[f"{name}_dmask"] = np.stack([np.where(same & (rel >= 0), np.exp(x * np.maximum(rel, 0)), 0.0) for x in lg],
                                      axis=1).astype(f)
        qd = np.zeros((P, B, 3, R))
        kd = np.zeros((R, B, H_RET))
        for h in range(H_RET):
            for x in range(B):
                rows = slice((h % 2) * DK, (h % 2) * DK + DK)
                qd[rows, x, h // 2] = np.where(b == x, np.exp(lg[h] * (n + 1.0)), 0.0)[None]
                kd[:, x, h] = np.where(b == x, np.exp(lg[h] * (C - 1.0 - n)), 0.0) * DK ** -0.5
        t[f"{name}_qdec"], t[f"{name}_kdec"] = qd.astype(f), kd.astype(f)
        t[f"{name}_sdec"] = np.exp(lg.reshape(3, 2)[:, np.arange(P) // DK].T * C).astype(f)
    decay("p", P, 1)
    decay("s", DS, DB)
    b4, pg = i // PAGES, i % PAGES
    t["later_pages"] = ((b4[:, None] == b4[None]) & (pg[:, None] > pg[None])).astype(f)
    t["batch_sel"] = np.stack([(np.arange(NS) // DS)[:, None] == (4 * x + b4)[None] for x in range(2)],
                              axis=1).astype(f)
    rows = np.arange(H_FOX * DS)
    new = np.arange(NS)
    t["later_new"] = ((new[:, None] // DS == new[None] // DS) & (new[:, None] > new[None])).astype(f)
    t["new_mask"] = np.where(np.arange(DS)[None] <= rows[:, None] % DS, 0.0, NEG).astype(f)
    t["own_head"] = (np.arange(NF)[None] // DH == rows[:, None] // DS).astype(f)
    t["fold"] = (np.arange(DS)[None] == rows[:, None] % DS).astype(f)
    return {k: np.ascontiguousarray(v) for k, v in t.items()}


def kernel(x_prompt, x_sample, mem_prompt, cache_k, cache_v, cache_logf, page_table, cache_mem_k, cache_mem_v,
           state_ret, state_conv, g_mix_pre, g_mix_post, g_ffn_pre, g_ffn_post, w_in_a, w_out_a, w_in_b, w_out_b,
           w_mem_kv, g_kv, w_kv_shared, b_f, w_ffn_up, conv_w, conv_b, w_ffn_down):
    import numpy as np
    import concourse.bacc as bacc
    from concourse.bass_utils import run_bass_kernel_spmd as run

    def chunks(w, n=NC):
        return w.reshape(-1, P, w.shape[1] // n, n).transpose(2, 1, 0, 3)

    ins = tables()
    ins["x"] = np.concatenate([x_prompt.reshape(SEQ, D), x_sample.reshape(NS, D),
                               np.zeros((ROWS - TOK, D), x_prompt.dtype)])
    ins["mem_t"] = mem_prompt[0].reshape(N_MEM, KD, P).transpose(2, 1, 0)
    n_phys = cache_k.shape[0]
    ins["cache_kt"] = cache_k.reshape(n_phys, PAGE, HP, P).transpose(0, 3, 2, 1).reshape(n_phys, P, HP * PAGE)
    ins["cache_v"] = cache_v.reshape(n_phys, PAGE, NF)
    phys = -(-n_phys // P)
    padded = np.concatenate([cache_logf.reshape(n_phys, PAGE * H_FOX),
                             np.zeros((phys * P - n_phys, PAGE * H_FOX), cache_logf.dtype)])
    ins["cache_logf"] = padded.reshape(phys, P, PAGE * H_FOX).transpose(1, 0, 2)
    ins["phys"] = (np.arange(P)[:, None] + P * np.arange(phys)[None]).astype(np.float32)
    ins["page_table"] = page_table.reshape(1, DB * PAGES)
    ins["cache_mem_kt"] = cache_mem_k.reshape(DEPTH, DB, N_MEM, 2, P).transpose(0, 1, 4, 3, 2)
    ins["cache_mem_v"] = cache_mem_v.reshape(DEPTH, DB, N_MEM, N_MEM)
    ins["state_ret"] = state_ret[0]
    ins["state_conv"] = state_conv.reshape(DEPTH, DB, 2, 2 * KF, P).transpose(0, 4, 3, 1, 2)
    for name, gain in (("g_mix_post", g_mix_post), ("g_ffn_post", g_ffn_post),
                       ("g_pre", np.concatenate([g_mix_pre, g_ffn_pre, g_kv[None]]))):
        ins[name] = gain[:, None]
    ins["w_in_a"], ins["w_out_a"] = chunks(w_in_a[0]), chunks(w_out_a[0])
    ins["w_in_b"], ins["w_out_b"] = chunks(w_in_b[0]), chunks(w_out_b[0])
    ins["w_mem"] = w_mem_kv.reshape(DEPTH, KD, P, NC).transpose(0, 2, 1, 3)
    ins["w_kv"] = chunks(w_kv_shared[:, :2 * NF])
    ins["w_f"] = w_kv_shared[:, 2 * NF:].reshape(KD, P, H_FOX).transpose(1, 0, 2)
    ins["b_f"] = np.broadcast_to(b_f[None], (P, H_FOX))
    ins["w_up"] = w_ffn_up.reshape(DEPTH, KD, P, 2, KF, P).transpose(0, 4, 2, 3, 1, 5).reshape(
        DEPTH, KF, P, 2, KD * P)
    ins["taps"] = np.concatenate([conv_w, conv_b[:, None]], axis=1).reshape(DEPTH, 4, 2 * KF, P).transpose(0, 3, 2, 1)
    ins["w_down"] = np.stack([chunks(w) for w in w_ffn_down])
    outs = {"y": (ROWS, D), "kv": (ROWS, 2 * NF), "logf": (ROWS, H_FOX), "mem_k": (DEPTH, N_MEM, N_MEM),
            "mem_v": (DEPTH, N_MEM, N_MEM), "ret_p": (1, H_RET, DK, DV), "ret_s": (DB, H_RET, DK, DV),
            "conv": (DEPTH, P, 2 * KF, 2 + 2 * DB)}

    nc = bacc.Bacc("TRN2", target_bir_lowering=False, num_devices=1)
    d, arrays = {}, {}
    for name, v in ins.items():
        arrays[f"in_{name}"] = np.ascontiguousarray(v)
        d[name] = nc.dram_tensor(f"in_{name}", v.shape, mybir.dt.from_np(v.dtype), kind="ExternalInput").ap()
    for name, shape in outs.items():
        d[name] = nc.dram_tensor(f"out_{name}", shape, F32, kind="ExternalOutput").ap()
    build(nc, d)
    r = run(nc, [arrays], core_ids=[0]).results[0]
    r = {name: r[f"out_{name}"] for name in outs}

    def heads(x, c0, *shape):
        return x[:, c0:c0 + NF].reshape(*shape, H_FOX, DH)
    k_p, v_p = (heads(r["kv"][:SEQ], c, 1, SEQ) for c in (0, NF))
    k_s, v_s = (heads(r["kv"][SEQ:TOK], c, DB, DS) for c in (0, NF))
    conv = r["conv"].transpose(0, 3, 2, 1).reshape(DEPTH, 2 + 2 * DB, 2 * DFF)
    return (r["y"][:SEQ].reshape(1, SEQ, D), r["y"][SEQ:TOK].reshape(DB, DS, D), k_p, v_p,
            r["logf"][:SEQ].reshape(1, SEQ, H_FOX), k_s, v_s, r["logf"][SEQ:TOK].reshape(DB, DS, H_FOX),
            r["mem_k"].reshape(DEPTH, 1, N_MEM, H_MEM, DH), r["mem_v"].reshape(DEPTH, 1, N_MEM, H_MEM, DH),
            r["ret_p"].reshape(1, 1, H_RET, DK, DV), r["ret_s"].reshape(1, DB, H_RET, DK, DV),
            conv[:, :2].reshape(DEPTH, 1, 2, 2 * DFF), conv[:, 2:].reshape(DEPTH, DB, 2, 2 * DFF))
```

```python
from contextlib import ExitStack

import concourse.bass as bass
from concourse import mybir

F32 = mybir.dt.float32
F32R = mybir.dt.float32r
I32 = mybir.dt.int32
ACT = mybir.ActivationFunctionType
ALU = mybir.AluOpType
AX = mybir.AxisListType

P = 128
D = 1024
KD = D // P
SEQ = 1024
PT = SEQ // P
DB, DS = 8, 8
NS = DB * DS
TILES = PT + 1
ROWS = TILES * P
TOK = SEQ + NS
NC = 512
EPS = 1e-6
NEG = -1e30

H_RET, DK, DV = 6, 64, 128
NQ = H_RET * DK
NV = H_RET * DV
Z_V, Z_G, Z_M = 2 * NQ, 2 * NQ + NV, 2 * NQ + 2 * NV
NZ = Z_M + 256
H_FOX, DH = 12, 64
NF = H_FOX * DH
HP = H_FOX // 2
H_MEM, N_MEM = 4, 256
MT = N_MEM // P
DFF = 2816
KF = DFF // P
CW = 3
DEPTH = 2
PAGE = 128
PAGES = 32


class Counter:

    def __init__(self, sem):
        self.sem, self.base, self.added = sem, 0, 0

    def wait_all(self, eng, total):
        self.added = total
        eng.wait_ge(self.sem, self.base + total)


def never(value):
    return isinstance(value, int) and value <= 0


def need(eng, sem, value):
    if never(value):
        return
    if isinstance(sem, Counter):
        sem, value = sem.sem, sem.base + value
    eng.wait_ge(sem, value)


def need_all(eng, *waits):
    waits = [(w.sem, w.base + v) if isinstance(w, Counter) else (w, v) for w, v in waits if not never(v)]
    waits = [(sem, v if isinstance(v, int) else eng.compute_val(v)) for sem, v in waits]
    for sem, v in waits:
        eng.wait_ge(sem, v)


def repeat(eng, n, body):
    body(0)
    if n == 2:
        body(1)
    elif n > 2:
        with eng.Fori(1, n) as i:
            body(i)


def repeat_ahead(eng, n, body):
    body(0)
    if n > 2:
        with eng.Fori(1, n - 1) as i:
            body(i)
    body(n - 1)


def first(i):
    return isinstance(i, int) and i == 0


def last_of(i, n):
    return isinstance(i, int) and i == n - 1


def at(ap, i):
    if isinstance(i, int):
        return ap[i]
    names = " ".join(f"d{j}" for j in range(len(ap.shape) - 1))
    return ap[bass.ds(i, 1)].rearrange(f"o d0 {names[3:]} -> (o d0) {names[3:]}")


def bc(ap, axis, n):
    a = ap.unsqueeze(axis)
    shape = list(a.shape)
    shape[axis] = n
    return a.broadcast_to(shape)


class Program:

    def __init__(self, nc, ctx):
        self.nc, self.ctx = nc, ctx
        self.n = 0
        self.kept = []
        self.old = None
        self.old_sems = []
        self.ps = ctx.enter_context(nc.psum_tensor("ps", [P, 8, 512], F32))

    def open(self, name):
        self.n += 1
        self.name = f"{name}{self.n}"
        self.mem = ExitStack()
        self.sems = ExitStack()
        self.live = []
        self.pool_sems = 0

    def sb(self, name, shape, dt=F32):
        return self.mem.enter_context(self.nc.sbuf_tensor(f"{self.name}_{name}", shape, dt))

    def sem(self, name):
        s = self.sems.enter_context(self.nc.semaphore(f"{self.name}_{name}"))
        self.live.append(s)
        return s

    def pool_sem(self, name):
        if self.pool_sems == len(self.kept):
            self.kept.append(Counter(self.ctx.enter_context(self.nc.semaphore(f"pool_dma{self.pool_sems}_{name}"))))
        self.pool_sems += 1
        return self.kept[self.pool_sems - 1]

    def clear_old(self, eng):
        for s in self.old_sems:
            eng.sem_clear(s)

    def close(self):
        self.mem.close()
        for counter in self.kept:
            counter.base, counter.added = counter.base + counter.added, 0
        if self.old is not None:
            self.old.close()
        self.old, self.old_sems = self.sems, self.live


class Rows:

    def __init__(self, g, a, src, gain=None, residual=None, h_out=None, plain=False, bank=None, banks=2,
                 slots=TILES):
        self.g, self.a, self.src, self.gain, self.residual = g, a, src, gain, residual
        self.h_out, self.plain, self.bank, self.banks, self.XS = h_out, plain, bank, banks, slots
        self.YS = 4
        self.xs = g.sb("rows_x", [P, self.XS, D])
        self.y = g.sb("rows_y", [P, self.YS, D]) if residual else self.xs
        self.square = g.sb("square", [P, D])
        self.stat = g.sb("stat", [P, TILES, 8])
        self.eps = g.sb("eps", [P, 1])
        self.post = g.sb("post", [P, D]) if residual else None
        self.pre = g.sb("pre", [P, D]) if gain is not None else None
        self.x_in = [g.sem(f"x_in{t}") for t in range(TILES)]
        self.o_in = [g.sem(f"o_in{t}") for t in range(TILES)] if residual else None
        self.h_stored = [g.sem(f"h_stored{s}") for s in range(self.XS)] if h_out is not None else None
        (self.post_in, self.pre_in, self.eps_set, self.o_sum, self.o_std, self.o_rstd, self.o_normed, self.h_done,
         self.h_sum, self.h_std, self.h_rstd, self.n_done, self.turned, self.rows_hi_done, self.rows_lo_done) = (
             g.sem(name) for name in ("post_in pre_in eps_set o_sum o_std o_rstd o_normed h_done h_sum h_std h_rstd "
                                      "n_done turned rows_hi_done rows_lo_done").split())
        self.ahead = [(2, self.stat_o, self.norm_o)] * bool(residual) + \
            [(1, self.store, None)] * bool(h_out is not None) + \
            [(1, self.stat_h, self.norm_h)] * bool(gain is not None) + [(0, self.hi, self.lo)] * bool(a)
        self.first_step = -max(s for s, _, _ in self.ahead)

    def x(self, t):
        return self.xs[:, t % self.XS]

    def slot(self, t):
        return self.y[:, t % self.YS] if self.residual else self.x(t)

    def load(self, sp, t):
        if self.residual:
            need(sp, self.turned if self.a else self.h_done, (2 if self.a else 1) * (t - self.YS + 1))
            sp.dma_start(self.y[:, t % self.YS], self.residual[0][t]).then_inc(self.o_in[t], 16)
        if t >= self.XS:
            sp.wait_ge(self.n_done, t - self.XS + 1)
            sp.wait_ge(self.h_stored[t % self.XS], 16 * (t // self.XS))
        sp.dma_start(self.x(t), self.src[t]).then_inc(self.x_in[t], 16)
        if t == 0 and self.residual:
            sp.dma_start(self.post[:], self.residual[1].broadcast_to([P, D])).then_inc(self.post_in, 16)
        if t == 0 and self.gain is not None:
            sp.dma_start(self.pre[:], self.gain.broadcast_to([P, D])).then_inc(self.pre_in, 16)

    def act_step(self, act, i):
        for s, step, _ in self.ahead:
            if 0 <= i + s < TILES:
                step(act, i + s)

    def stat_o(self, act, t):
        nc, stat = self.g.nc, self.stat
        act.wait_ge(self.o_in[t], 16)
        nc.scalar.activation(self.square[:], self.y[:, t % self.YS], ACT.Square, accum_out=stat[:, t, 0:1]).then_inc(
            self.o_sum, 1)
        act.wait_ge(self.o_sum, t + 1)
        nc.scalar.activation(stat[:, t, 1:2], stat[:, t, 0:1], ACT.Sqrt, scale=1.0 / D, bias=self.eps[:]).then_inc(
            self.o_std, 1)

    def stat_h(self, act, t):
        nc, stat = self.g.nc, self.stat
        if self.residual:
            act.wait_ge(self.h_done, t + 1)
        else:
            act.wait_ge(self.x_in[t], 16)
        nc.scalar.activation(self.square[:], self.x(t), ACT.Square, accum_out=stat[:, t, 4:5]).then_inc(
            self.h_sum, 1)
        act.wait_ge(self.h_sum, t + 1)
        nc.scalar.activation(stat[:, t, 5:6], stat[:, t, 4:5], ACT.Sqrt, scale=1.0 / D, bias=self.eps[:]).then_inc(
            self.h_std, 1)

    def store(self, act, t):
        act.wait_ge(self.h_done, t + 1)
        act.dma_start(self.h_out[t], self.x(t)).then_inc(self.h_stored[t % self.XS], 16)

    def stored(self, act):
        for s, sem in enumerate(self.h_stored or ()):
            act.wait_ge(sem, 16 * len(range(s, TILES, self.XS)))

    def hi(self, act, t):
        for j in range(2):
            act.wait_ge(self.turned, 2 * t + j + 1)
            self.g.nc.scalar.activation(
                self.a[0][:, 4 * j:4 * j + 4, t * P:t * P + P],
                self.g.ps[:, self.bank(t, j), :].rearrange("p (k r) -> p k r", k=4), ACT.Copy).then_inc(
                    self.rows_hi_done, 1)

    def dve_start(self, dve):
        self.g.nc.vector.memset(self.eps[:], EPS).then_inc(self.eps_set, 1)
        if self.residual:
            dve.wait_ge(self.post_in, 16)
        if self.gain is not None:
            dve.wait_ge(self.pre_in, 16)

    def dve_step(self, dve, i):
        for s, _, step in self.ahead:
            if step and 0 <= i + s < TILES:
                step(dve, i + s)

    def norm_o(self, dve, t):
        nc, stat, y = self.g.nc, self.stat, self.y[:, t % self.YS]
        dve.wait_ge(self.o_std, t + 1)
        nc.vector.reciprocal(stat[:, t, 2:3], stat[:, t, 1:2]).then_inc(self.o_rstd, 1)
        dve.wait_ge(self.o_rstd, t + 1)
        nc.vector.scalar_tensor_tensor(out=y, in0=y, scalar=stat[:, t, 2:3], in1=self.post[:],
                                       op0=ALU.mult, op1=ALU.mult).then_inc(self.o_normed, 1)
        dve.wait_ge(self.o_normed, t + 1)
        dve.wait_ge(self.x_in[t], 16)
        nc.vector.tensor_tensor(self.x(t), self.x(t), y, ALU.add).then_inc(self.h_done, 1)

    def norm_h(self, dve, t):
        nc, stat = self.g.nc, self.stat
        dve.wait_ge(self.h_std, t + 1)
        nc.vector.reciprocal(stat[:, t, 6:7], stat[:, t, 5:6]).then_inc(self.h_rstd, 1)
        dve.wait_ge(self.h_rstd, t + 1)
        if self.residual:
            dve.wait_ge(self.h_done, t + 1)
        nc.vector.scalar_tensor_tensor(out=self.slot(t), in0=self.x(t), scalar=stat[:, t, 6:7], in1=self.pre[:],
                                       op0=ALU.mult, op1=ALU.mult).then_inc(self.n_done, 1)

    def lo(self, dve, t):
        for j in range(2):
            dve.wait_ge(self.rows_hi_done, 2 * t + j + 1)
            self.g.nc.vector.tensor_tensor(
                self.a[1][:, 4 * j:4 * j + 4, t * P:t * P + P],
                self.g.ps[:, self.bank(t, j), :].rearrange("p (k r) -> p k r", k=4),
                self.a[0][:, 4 * j:4 * j + 4, t * P:t * P + P].bitcast(F32), ALU.subtract).then_inc(
                    self.rows_lo_done, 1)

    def turn(self, pe, t):
        if self.plain:
            pe.wait_ge(self.x_in[t], 16)
        else:
            pe.wait_ge(self.n_done, t + 1)
        for j in range(2):
            need(pe, self.rows_lo_done, 2 * t + j - self.banks + 1)
            for k in range(4 * j, 4 * j + 4):
                last = self.g.nc.tensor.transpose(self.g.ps[:, self.bank(t, j), (k % 4) * P:(k % 4) * P + P],
                                                  self.slot(t)[:, k * P:k * P + P], self.g.ident[:])
            last.then_inc(self.turned, 1)


def normalise(g, a, src, **kinds):
    nc = g.nc
    g.open("normalise")
    rows = Rows(g, a, src, bank=lambda t, j: (2 * t + j) % 8, banks=8, **kinds)
    with nc.Block() as block:
        @block.sync
        def _(sp):
            g.clear_old(sp)
            for t in range(TILES):
                rows.load(sp, t)

        @block.scalar
        def _(act):
            act.wait_ge(rows.eps_set, 1)
            for i in range(rows.first_step, TILES):
                rows.act_step(act, i)
            rows.stored(act)

        @block.vector
        def _(dve):
            rows.dve_start(dve)
            for i in range(rows.first_step, TILES):
                rows.dve_step(dve, i)

        if a:
            @block.tensor
            def _(pe):
                for t in range(TILES):
                    rows.turn(pe, t)
    g.close()


def project(g, a, w, n_chunks, tiles, outs, silu=(), rows=None):
    nc = g.nc
    g.open("project")
    a_hi, a_lo = a
    S = 3 if tiles == TILES else tiles
    US = tiles // S
    raw = g.sb("raw", [P, 2, 4, NC])
    w_hi, w_lo = g.sb("w_hi", [P, KD, NC], F32R), g.sb("w_lo", [P, KD, NC], F32R)
    z = g.sb("z", [P, S, NC])
    loaded = [g.sem("half0_loaded"), g.sem("half1_loaded")]
    hi_done, lo_done, w_used = g.sem("w_hi_done"), g.sem("w_lo_done"), g.sem("w_used")
    z_done, z_out = g.sem("z_done"), g.sem("z_copied")
    stored = [g.pool_sem(f"stored{s}") for s in range(S)]
    stores = len(outs(0, 0))
    T1 = tiles - 1

    def bank(t):
        return 4 if t == 8 else t

    made = Rows(g, a, bank=lambda t, j: 6 + j if t < 6 else j, **rows) if rows else None

    with nc.Block() as block:
        @block.sync
        def _(sp):
            g.clear_old(sp)

            for t in range(3 if made else 0):
                made.load(sp, t)

            def body(n):
                for half in range(2):
                    need(sp, lo_done, (n - 1) * KD + half * 4 + 4)
                    sp.dma_start(raw[:, half], at(w, n)[:, half * 4:half * 4 + 4, :]).then_inc(loaded[half], 16)
                if made and first(n):
                    for t in range(3, tiles):
                        made.load(sp, t)
            repeat(sp, n_chunks, body)

        @block.scalar
        def _(act):
            def split(n):
                for k in range(KD):
                    if k % 4 == 0:
                        act.wait_ge(loaded[k // 4], 16 * n + 16)
                    need(act, w_used, (n - 1) * KD + k + 1)
                    nc.scalar.activation(w_hi[:, k], raw[:, k // 4, k % 4], ACT.Copy).then_inc(hi_done, 1)

            def evac(n, t):
                if t < T1:
                    act.wait_ge(z_done, n * T1 + t + 1)
                else:
                    act.wait_ge(w_used, n * KD + KD)
                need(act, stored[t % S], (n * US + t // S) * 16 * stores)
                cut = silu[n] if isinstance(n, int) and n < len(silu) else 0
                if cut:
                    nc.scalar.activation(z[:, t % S, :cut], g.ps[:, bank(t), :cut], ACT.Silu).then_inc(z_out, 1)
                if cut < NC:
                    nc.scalar.activation(z[:, t % S, cut:], g.ps[:, bank(t), cut:], ACT.Copy).then_inc(z_out, 1)

            def body(n):
                split(n)
                if not first(n):
                    evac(n - 1, T1)
                for t in range(T1):
                    if made and first(n):
                        made.act_step(act, t + 1)
                    evac(n, t)
            if made:
                act.wait_ge(made.eps_set, 1)
                for i in range(made.first_step, 1):
                    made.act_step(act, i)
            if silu:
                for n in range(n_chunks):
                    body(n)
            else:
                repeat(act, n_chunks, body)
            evac(n_chunks - 1, T1)
            if made:
                made.stored(act)

        def copies(n, t):
            if not silu:
                return n * tiles + t + 1
            before = sum(tiles * (2 if 0 < silu[m] < NC else 1) for m in range(n))
            return before + (t + 1) * (2 if 0 < silu[n] < NC else 1)

        @block.vector
        def _(dve):
            def body(n):
                for k in range(KD):
                    dve.wait_ge(hi_done, n * KD + k + 1)
                    nc.vector.tensor_tensor(w_lo[:, k], raw[:, k // 4, k % 4], w_hi[:, k].bitcast(F32),
                                            ALU.subtract).then_inc(lo_done, 1)
                if made and first(n):
                    for t in range(1, tiles):
                        made.dve_step(dve, t)
            if made:
                made.dve_start(dve)
                for i in range(made.first_step, 1):
                    made.dve_step(dve, i)
            repeat(dve, n_chunks, body)

        @block.tensor
        def _(pe):
            def body(n):
                for t in range(tiles):
                    if made and first(n):
                        if t == 5:
                            pe.wait_ge(z_out, copies(0, 1))
                        if t < T1:
                            made.turn(pe, t + 1)
                        pe.wait_ge(made.rows_lo_done, 2 * t + 2)
                    m, s = (n - 1, t) if t < 8 else (n, 4)
                    if t == 4 and tiles == 9:
                        s = 8
                    if not first(n) or t == 8:
                        need(pe, z_out, copies(m, s))
                    for k in range(KD):
                        if t == 0:
                            pe.wait_ge(lo_done, n * KD + k + 1)
                        ah, al = a_hi[:, k, t * P:t * P + P], a_lo[:, k, t * P:t * P + P]
                        o = g.ps[:, bank(t)]
                        nc.tensor.matmul(o, al, w_hi[:, k], start=(k == 0), stop=False)
                        nc.tensor.matmul(o, ah, w_hi[:, k], start=False, stop=False)
                        last = nc.tensor.matmul(o, ah, w_lo[:, k], start=False, stop=(k == KD - 1))
                        if t == T1:
                            last.then_inc(w_used, 1)
                    if t < T1:
                        last.then_inc(z_done, 1)
            if made:
                made.turn(pe, 0)
            if silu:
                for n in range(n_chunks):
                    body(n)
            else:
                repeat(pe, n_chunks, body)

        @block.gpsimd
        def _(pool):
            def body(n):
                for t in range(tiles):
                    pool.wait_ge(z_out, copies(n, t))
                    for dst, c0, c1 in outs(n, t):
                        pool.dma_start(dst, z[:, t % S, c0:c1]).then_inc(stored[t % S].sem, 16)
            if silu:
                for n in range(n_chunks):
                    body(n)
            else:
                repeat(pool, n_chunks, body)
            for s in range(S):
                stored[s].wait_all(pool, n_chunks * US * 16 * stores)
    g.close()


def columns(z, tiles):
    v = z.rearrange("(t p) (n c) -> n t p c", p=P, c=NC)

    def outs(n, t):
        return [(at(v[:, t], n), 0, NC)]
    return outs


def retention(g, z, t_in, cat, state_in, state_out, sample):
    nc = g.nc
    g.open("retention")
    R = NS if sample else P
    B = DB if sample else 1
    n_tiles = 1 if sample else PT
    U = 1 if sample else 2
    steps = n_tiles // U
    zq, zv, zg = g.sb("zq", [P, U, 2 * NQ]), g.sb("zv", [P, U, NV]), g.sb("zg", [P, U, NV])
    rope = g.sb("rope", [P, U, 64])
    zcos, zsin = g.sb("zcos", [P, 2 * NQ]), g.sb("zsin", [P, 2 * NQ])
    rot = g.sb("rot", [P, U, 2 * NQ])
    q_t, k_t = g.sb("q_t", [P, U, 3, R]), g.sb("k_t", [P, U, 3, R])
    qd, kd = g.sb("qd", [P, U, B, 3, R]), g.sb("kd", [P, U, B, H_RET, DK])
    inner = g.sb("inner", [P, H_RET, R])
    o = g.sb("o", [P, U, H_RET, DV])
    square = g.sb("square", [P, H_RET, DV])
    r = g.sb("r", [P, U, NV])
    st = g.sb("st", [P, U, 5, H_RET])
    S = g.sb("S", [P, B, 3, DV])
    dmask, qdec = g.sb("dmask", [P, H_RET, R]), g.sb("qdec", [P, B, 3, R])
    kdec, sdec = g.sb("kdec", [P, B, H_RET]), g.sb("sdec", [P, 3])
    eps = g.sb("eps", [P, 1])
    zq_in, zv_in, zg_in = ([g.sem(f"{x}_in{u}") for u in range(U)] for x in ("zq", "zv", "zg"))
    r_stored = [g.pool_sem(f"r_stored{u}") for u in range(U)]
    tables_in, s_stored = g.sem("tables_in"), g.pool_sem("s_stored")
    (s_set, cos_done, sin_done, rot_done, qk_turned, q_ready, k_ready, qd_done, kd_done, inner_in, inner_done,
     o_in, s_in, s_done, o_copied, mean_done, center_done, square_done, var_done, std_done, rstd_done, norm_done,
     r_done) = (g.sem(x) for x in (
         "s_set cos_done sin_done rot_done qk_turned q_ready k_ready qd_done kd_done inner_in inner_done o_in s_in "
         "s_done o_copied mean_done center_done square_done var_done std_done rstd_done norm_done r_done").split())
    inner_bank = lambda h: g.ps[0:R, 2 + h % 2, (h // 2) * R:(h // 2) * R + R]
    o_bank = lambda h: g.ps[0:R, 4 + h % 2, (h // 2) * DV:(h // 2) * DV + DV]
    heads = lambda x, f: x.rearrange("p (c f) r -> p f c r", f=2)[:, f]


    def loaded(t, u, n):
        return n * 16 // U * (t - u) + n * 16

    def walk(eng, tile):
        def body(i):
            for u in range(U):
                tile(i * U + u, u, last_of(i, steps) and u == U - 1)
        if steps == 1:
            body(0)
        else:
            repeat_ahead(eng, steps, body)

    with nc.Block() as block:
        @block.sync
        def _(sp):
            g.clear_old(sp)
            for dst, src in ((dmask[0:R], t_in["dmask"]), (qdec[:], t_in["qdec"]), (kdec[0:R], t_in["kdec"]),
                             (sdec[:], t_in["sdec"])):
                sp.dma_start(dst, src).then_inc(tables_in, 16)
            if sample:
                for half in range(2):
                    for c in range(3):
                        sp.dma_start(S[half * DK:half * DK + DK, :, c],
                                     state_in[:, 2 * c + half].rearrange("b d e -> d b e")).then_inc(tables_in, 16)

            def load(t, u, last):
                src = at(z, PT if sample else t)
                need(sp, rot_done, 2 * (t - U + 1))
                sp.dma_start(zq[:, u], src[:, 0:2 * NQ]).then_inc(zq_in[u], 16)
                sp.dma_start(rope[0:R, u], at(t_in["rope"], PT if sample else t)[0:R]).then_inc(zq_in[u], 16)
                need_all(sp, (s_in, (t - U + 1) * B), (o_in, t - U + 1))
                sp.dma_start(zv[:, u], src[:, Z_V:Z_G]).then_inc(zv_in[u], 16)
                need(sp, r_done, t - U + 1)
                sp.dma_start(zg[:, u], src[:, Z_G:Z_M]).then_inc(zg_in[u], 16)
            walk(sp, load)

        @block.scalar
        def _(act):
            act.wait_ge(s_set, 2)

            def operands(t, u):
                need(act, inner_in, t - U + 1)
                need(act, qd_done, t - U + 1)
                act.wait_ge(qk_turned, 2 * t + 1)
                nc.scalar.activation(q_t[:, u], g.ps[:, 0, 0:3 * R].rearrange("p (c r) -> p c r", c=3),
                                     ACT.Copy).then_inc(q_ready, 1)
                act.wait_ge(qk_turned, 2 * t + 2)
                nc.scalar.activation(k_t[:, u], g.ps[:, 1, 0:3 * R].rearrange("p (c r) -> p c r", c=3),
                                     ACT.Copy, scale=DK ** -0.5).then_inc(k_ready, 1)

            def std(t, u):
                act.wait_ge(var_done, t + 1)
                nc.scalar.activation(st[0:R, u, 3], st[0:R, u, 2], ACT.Sqrt, scale=1.0 / DV, bias=eps[0:R]).then_inc(
                    std_done, 1)

            def tile(t, u, last):
                if not first(t):
                    std(t - 1, (u - 1) % U)
                act.wait_ge(o_in, t + 1)
                need(act, norm_done, t - U + 1)
                for f in range(2):
                    copied = nc.scalar.activation(heads(o[0:R, u], f), g.ps[0:R, 4 + f, 0:3 * DV].rearrange(
                        "p (c e) -> p c e", c=3), ACT.Copy)
                copied.then_inc(o_copied, 1)
                if not last:
                    operands(t + 1, (u + 1) % U)
                act.wait_ge(center_done, t + 1)
                need(act, var_done, t)
                nc.scalar.activation(square[0:R], o[0:R, u], ACT.Square).then_inc(square_done, 1)
            operands(0, 0)
            walk(act, tile)
            std(n_tiles - 1, U - 1)

        @block.vector
        def _(dve):
            nc.vector.memset(eps[:], EPS).then_inc(s_set, 1)
            if sample:
                nc.vector.memset(inner[:], 0.0).then_inc(s_set, 1)
            else:
                nc.vector.memset(S[:], 0.0).then_inc(s_set, 1)
            dve.wait_ge(s_set, 2)
            dve.wait_ge(tables_in, 16 * (10 if sample else 4))

            def rotary(t, u):
                dve.wait_ge(zq_in[u], loaded(t, u, 2))
                qk = zq[0:R, u].rearrange("p (h d) -> p h d", d=32)
                C = zcos[0:R].rearrange("p (h f d) -> p h f d", f=2, d=32)
                Sn = zsin[0:R].rearrange("p (h f d) -> p h f d", f=2, d=32)
                need(dve, rot_done, 2 * t)
                nc.vector.tensor_tensor(zcos[0:R].rearrange("p (h d) -> p h d", d=32), qk,
                                        bc(rope[0:R, u, 0:32], 1, 24), ALU.mult).then_inc(cos_done, 1)
                nc.vector.tensor_tensor(zsin[0:R].rearrange("p (h d) -> p h d", d=32), qk,
                                        bc(rope[0:R, u, 32:64], 1, 24), ALU.mult).then_inc(sin_done, 1)
                dve.wait_ge(cos_done, t + 1)
                dve.wait_ge(sin_done, t + 1)
                need(dve, qk_turned, 2 * (t - U + 1))
                need(dve, kd_done, t - U + 1)
                rv = rot[0:R, u].rearrange("p (h f d) -> p h f d", f=2, d=32)
                nc.vector.tensor_tensor(rv[:, :, 0], C[:, :, 0], Sn[:, :, 1], ALU.subtract).then_inc(rot_done, 1)
                nc.vector.tensor_tensor(rv[:, :, 1], Sn[:, :, 0], C[:, :, 1], ALU.add).then_inc(rot_done, 1)
                dve.wait_ge(rot_done, 2 * t + 2)
                need(dve, s_in, (t - U + 1) * B)
                for b in range(B):
                    last = nc.vector.tensor_tensor(kd[0:R, u, b], rot[0:R, u, NQ:].rearrange("p (h d) -> p h d", d=DK),
                                                   bc(kdec[0:R, b], 2, DK), ALU.mult)
                last.then_inc(kd_done, 1)

            def decayed(t, u):
                dve.wait_ge(q_ready, t + 1)
                need(dve, o_in, t - U + 1)
                for b in range(B):
                    last = nc.vector.tensor_tensor(qd[:, u, b], q_t[:, u], qdec[:, b], ALU.mult)
                last.then_inc(qd_done, 1)

            def mask(t):
                dve.wait_ge(inner_in, t + 1)
                need(dve, o_in, t)
                for f in range(2):
                    last = nc.vector.tensor_tensor(
                        heads(inner[0:R], f), g.ps[0:R, 2 + f, 0:3 * R].rearrange("p (c r) -> p c r", c=3),
                        heads(dmask[0:R], f), ALU.mult)
                last.then_inc(inner_done, 1)

            def state(t):
                for b in range(B):
                    dve.wait_ge(s_in, t * B + b + 1)
                    if b == 0:
                        dve.wait_ge(o_in, t + 1)
                    for c in range(3):
                        last = nc.vector.scalar_tensor_tensor(
                            out=S[:, b, c], in0=S[:, b, c], scalar=sdec[:, c:c + 1],
                            in1=g.ps[:, 6 + b % 2, c * DV:c * DV + DV], op0=ALU.mult, op1=ALU.add)
                    last.then_inc(s_done, 1)

            def center(t, u):
                dve.wait_ge(o_copied, t + 1)
                need(dve, rstd_done, t - U + 1)
                need(dve, center_done, t - U + 1)
                nc.vector.tensor_reduce(st[0:R, u, 0], o[0:R, u], AX.X, ALU.add).then_inc(mean_done, 1)
                dve.wait_ge(mean_done, 2 * t + 1)
                nc.vector.tensor_scalar(st[0:R, u, 1], st[0:R, u, 0], -1.0 / DV, None, ALU.mult).then_inc(mean_done, 1)
                dve.wait_ge(mean_done, 2 * t + 2)
                nc.vector.tensor_tensor(o[0:R, u], o[0:R, u], bc(st[0:R, u, 1], 2, DV), ALU.add).then_inc(
                    center_done, 1)

            def finish(t, u):
                dve.wait_ge(square_done, t + 1)
                need(dve, std_done, t - U + 1)
                nc.vector.tensor_reduce(st[0:R, u, 2], square[0:R], AX.X, ALU.add).then_inc(var_done, 1)
                dve.wait_ge(std_done, t + 1)
                need(dve, norm_done, t - U + 1)
                nc.vector.reciprocal(st[0:R, u, 4], st[0:R, u, 3]).then_inc(rstd_done, 1)
                dve.wait_ge(rstd_done, t + 1)
                dve.wait_ge(center_done, t + 1)
                need(dve, r_stored[u], 16 // U * (t - u))
                nc.vector.tensor_tensor(r[0:R, u].rearrange("p (h e) -> p h e", h=H_RET), o[0:R, u],
                                        bc(st[0:R, u, 4], 2, DV), ALU.mult).then_inc(norm_done, 1)
                dve.wait_ge(norm_done, t + 1)
                dve.wait_ge(zg_in[u], loaded(t, u, 1))
                nc.vector.tensor_tensor(r[0:R, u], r[0:R, u], zg[0:R, u], ALU.mult).then_inc(r_done, 1)

            def tile(t, u, last):
                mask(t)
                if not last:
                    rotary(t + 1, (u + 1) % U)
                if not first(t):
                    finish(t - 1, (u - 1) % U)
                state(t)
                center(t, u)
                if not last:
                    decayed(t + 1, (u + 1) % U)
            rotary(0, 0)
            decayed(0, 0)
            walk(dve, tile)
            finish(n_tiles - 1, U - 1)

        @block.tensor
        def _(pe):
            pe.wait_ge(s_set, 2)
            if sample:
                pe.wait_ge(tables_in, 160)

            def turn(t, u):
                pe.wait_ge(rot_done, 2 * t + 2)
                need(pe, q_ready, t)
                need(pe, k_ready, t)
                for x in range(2):
                    for c in range(3):
                        last = nc.tensor.transpose(g.ps[:, x, c * R:c * R + R],
                                                   rot[0:R, u, x * NQ + c * P:x * NQ + c * P + P],
                                                   g.ident[0:R, 0:R])
                    last.then_inc(qk_turned, 1)

            def tile(t, u, last_tile):
                pe.wait_ge(q_ready, t + 1)
                pe.wait_ge(k_ready, t + 1)
                need(pe, inner_done, t)
                for h in range(H_RET):
                    half = slice((h % 2) * DK, (h % 2) * DK + DK)
                    last = nc.tensor.matmul(inner_bank(h), k_t[half, u, h // 2], q_t[half, u, h // 2],
                                            start=True, stop=True)
                last.then_inc(inner_in, 1)
                pe.wait_ge(kd_done, t + 1)
                pe.wait_ge(zv_in[u], loaded(t, u, 1))
                for b in range(B):
                    need(pe, s_done, t if B == 1 else b - 1)
                    for h in range(H_RET):
                        half = slice((h % 2) * DK, (h % 2) * DK + DK)
                        v = zv[0:R, u, h * DV:h * DV + DV]
                        last = nc.tensor.matmul(g.ps[half, 6 + b % 2, (h // 2) * DV:(h // 2) * DV + DV],
                                                kd[0:R, u, b, h], v, start=True, stop=True)
                    last.then_inc(s_in, 1)
                    if b == 0:
                        outputs(t, u)
                if not last_tile:
                    turn(t + 1, (u + 1) % U)

            def outputs(t, u):
                pe.wait_ge(inner_done, t + 1)
                pe.wait_ge(qd_done, t + 1)
                need(pe, s_done, t * B)
                need(pe, o_copied, t)
                for h in range(H_RET):
                    half = slice((h % 2) * DK, (h % 2) * DK + DK)
                    nc.tensor.matmul(o_bank(h), inner[:, h], zv[:, u, h * DV:h * DV + DV], start=True, stop=False)
                    for b in range(B):
                        last = nc.tensor.matmul(o_bank(h), qd[half, u, b, h // 2], S[half, b, h // 2], start=False,
                                                stop=(b == B - 1))
                last.then_inc(o_in, 1)
            turn(0, 0)
            walk(pe, tile)

        @block.gpsimd
        def _(pool):
            def body(i):
                for u in range(U):
                    t = i * U + u
                    pool.wait_ge(r_done, t + 1)
                    pool.dma_start(at(cat, PT if sample else t)[0:R, 0:NV], r[0:R, u]).then_inc(r_stored[u].sem, 16)
            repeat(pool, steps, body)
            pool.wait_ge(s_done, n_tiles * B)
            for half in range(2):
                for c in range(3):
                    pool.dma_start(state_out[:, 2 * c + half].rearrange("b d e -> d b e"),
                                   S[half * DK:half * DK + DK, :, c]).then_inc(s_stored.sem, 16)
            s_stored.wait_all(pool, 6 * 16)
            for u in range(U):
                r_stored[u].wait_all(pool, 16 * steps)
    g.close()


def mem_prompt(g, z, q0, mem_k, mem_v, cat):
    nc = g.nc
    g.open("mem_prompt")
    U = 2
    steps = PT // U
    mk = g.sb("mk", [P, MT, N_MEM])
    mv = g.sb("mv", [P, MT, N_MEM])
    mk_t = g.sb("mk_t", [P, 2, N_MEM])
    q = g.sb("q", [P, U, N_MEM])
    q_t = g.sb("q_t", [P, U, 2, P])
    p = g.sb("p", [P, U, H_MEM, N_MEM])
    p_t = g.sb("p_t", [P, H_MEM * MT, P])
    st = g.sb("st", [P, U, 3, H_MEM])
    o_t = g.sb("o_t", [P, 2, P])
    o = g.sb("o", [P, U, H_MEM, DH])
    q_in = [g.sem(f"q_in{u}") for u in range(U)]
    o_stored = [g.pool_sem(f"o_stored{u}") for u in range(U)]
    (mem_in, k_turned, k_ready, q_turned, q_ready, scores_in, max_done, exp_done, p_turned, p_ready, o_in, ot_ready,
     o_turned, rsum_done, o_done) = (g.sem(x) for x in (
         "mem_in k_turned k_ready q_turned q_ready scores_in max_done exp_done p_turned p_ready o_in ot_ready "
         "o_turned rsum_done o_done").split())

    def scores(u, h):
        return g.ps[:, 1 + 4 * u + h % 2, (h // 2) * N_MEM:(h // 2) * N_MEM + N_MEM]

    def walk(eng, tile):
        def body(i):
            for u in range(U):
                tile(i * U + u, u, last_of(i, steps) and u == U - 1)
        repeat_ahead(eng, steps, body)

    with nc.Block() as block:
        @block.sync
        def _(sp):
            g.clear_old(sp)
            sp.dma_start(mk[:], mem_k.rearrange("(m p) c -> p m c", p=P)).then_inc(mem_in, 16)
            sp.dma_start(mv[:], mem_v.rearrange("(m p) c -> p m c", p=P)).then_inc(mem_in, 16)

            def body(i):
                for u in range(U):
                    need(sp, q_turned, i * U + u - U + 1)
                    sp.dma_start(q[:, u], at(z, i * U + u)[:, q0:q0 + N_MEM]).then_inc(q_in[u], 16)
            repeat(sp, steps, body)

        @block.tensor
        def _(pe):
            pe.wait_ge(mem_in, 32)
            for c in range(2):
                for m in range(MT):
                    last = nc.tensor.transpose(g.ps[:, 0, (c * MT + m) * P:(c * MT + m) * P + P],
                                               mk[:, m, c * P:c * P + P], g.ident[:])
            last.then_inc(k_turned, 1)
            pe.wait_ge(k_ready, 1)

            def turn_q(t, u):
                pe.wait_ge(q_in[u], 16 // U * (t - u) + 16)
                need(pe, q_ready, t)
                need(pe, o_done, t - 2)
                for c in range(2):
                    last = nc.tensor.transpose(g.ps[:, 0, c * P:c * P + P], q[:, u, c * P:c * P + P], g.ident[:])
                last.then_inc(q_turned, 1)

            def score(t, u):
                pe.wait_ge(q_ready, t + 1)
                need(pe, exp_done, (t - 1) * H_MEM)
                for h in range(H_MEM):
                    half = slice((h % 2) * DH, (h % 2) * DH + DH)
                    last = nc.tensor.matmul(scores(u, h), q_t[half, u, h // 2], mk_t[half, h // 2], start=True,
                                            stop=True)
                last.then_inc(scores_in, 1)

            def turn_p(t, u):
                for j in range(2):
                    need(pe, p_ready, 2 * (t - 1) + j + 1)
                    for x in range(4):
                        h, m = (4 * j + x) // MT, x % MT
                        pe.wait_ge(exp_done, t * H_MEM + h + 1)
                        last = nc.tensor.transpose(g.ps[:, 3 + j, x * P:x * P + P], p[:, u, h, m * P:m * P + P],
                                                   g.ident[:])
                    last.then_inc(p_turned, 1)

            def weigh(t):
                need(pe, ot_ready, t)
                for h in range(H_MEM):
                    half = slice((h % 2) * DH, (h % 2) * DH + DH)
                    pe.wait_ge(p_ready, 2 * t + h // 2 + 1)
                    for m in range(MT):
                        last = nc.tensor.matmul(g.ps[half, 7, (h // 2) * P:(h // 2) * P + P],
                                                mv[:, m, h * DH:h * DH + DH], p_t[:, h * MT + m], start=(m == 0),
                                                stop=(m == MT - 1))
                last.then_inc(o_in, 1)

            def turn_o(t):
                pe.wait_ge(ot_ready, t + 1)
                for c in range(2):
                    last = nc.tensor.transpose(g.ps[:, 0, c * P:c * P + P], o_t[:, c], g.ident[:])
                last.then_inc(o_turned, 1)

            def tile(t, u, last):
                if not last:
                    turn_q(t + 1, (u + 1) % U)
                turn_p(t, u)
                if not last:
                    score(t + 1, (u + 1) % U)
                if not first(t):
                    turn_o(t - 1)
                weigh(t)
            turn_q(0, 0)
            score(0, 0)
            walk(pe, tile)
            turn_o(PT - 1)

        @block.scalar
        def _(act):
            act.wait_ge(k_turned, 1)
            nc.scalar.activation(mk_t[:], g.ps[:, 0, :].rearrange("p (c m) -> p c m", c=2), ACT.Copy).then_inc(
                k_ready, 1)

            def queries(t, u):
                act.wait_ge(q_turned, t + 1)
                need(act, scores_in, t - 1)
                nc.scalar.activation(q_t[:, u], g.ps[:, 0, 0:2 * P].rearrange("p (c m) -> p c m", c=2), ACT.Copy,
                                     scale=DH ** -0.5).then_inc(q_ready, 1)

            def probs(t, u):
                act.wait_ge(max_done, t + 1)
                need(act, p_turned, 2 * (t - 1))
                need(act, rsum_done, t - 1)
                for h in range(H_MEM):
                    nc.scalar.activation(p[:, u, h], scores(u, h), ACT.Exp, bias=st[:, u, 0, h:h + 1],
                                         accum_out=st[:, u, 1, h:h + 1]).then_inc(exp_done, 1)

            def tile(t, u, last):
                probs(t, u)
                if not last:
                    queries(t + 1, (u + 1) % U)
            queries(0, 0)
            walk(act, tile)

        @block.vector
        def _(dve):
            def row_max(t, u):
                dve.wait_ge(scores_in, t + 1)
                need(dve, exp_done, (t - 1) * H_MEM)
                nc.vector.tensor_reduce(st[:, u, 0].rearrange("p (c f) -> p f c", f=2),
                                        g.ps[:, 1 + 4 * u:3 + 4 * u, :].rearrange("p f (c m) -> p f c m", m=N_MEM),
                                        AX.X, ALU.max, negate=True).then_inc(max_done, 1)

            def operand(t):
                for j in range(2):
                    dve.wait_ge(p_turned, 2 * t + j + 1)
                    need(dve, o_in, t)
                    nc.vector.tensor_copy(p_t[:, 4 * j:4 * j + 4],
                                          g.ps[:, 3 + j, :].rearrange("p (x r) -> p x r", x=4)).then_inc(p_ready, 1)

            def keep(t):
                dve.wait_ge(o_in, t + 1)
                need(dve, o_turned, t)
                nc.vector.tensor_copy(o_t[:], g.ps[:, 7, 0:2 * P].rearrange("p (c r) -> p c r", c=2)).then_inc(
                    ot_ready, 1)

            def divide(t, u):
                dve.wait_ge(exp_done, t * H_MEM + H_MEM)
                need(dve, o_done, t - 1)
                nc.vector.reciprocal(st[:, u, 2], st[:, u, 1]).then_inc(rsum_done, 1)
                dve.wait_ge(rsum_done, t + 1)
                dve.wait_ge(o_turned, t + 1)
                need(dve, o_stored[u], 16 // U * (t - u))
                nc.vector.tensor_tensor(o[:, u], g.ps[:, 0, 0:N_MEM].rearrange("p (h d) -> p h d", d=DH),
                                        bc(st[:, u, 2], 2, DH), ALU.mult).then_inc(o_done, 1)

            def tile(t, u, last):
                operand(t)
                if not last:
                    row_max(t + 1, (u + 1) % U)
                if not first(t):
                    divide(t - 1, (u - 1) % U)
                keep(t)
            row_max(0, 0)
            walk(dve, tile)
            divide(PT - 1, U - 1)

        @block.gpsimd
        def _(pool):
            def body(i):
                for u in range(U):
                    pool.wait_ge(o_done, i * U + u + 1)
                    pool.dma_start(at(cat, i * U + u)[:, NV:D], o[:, u].rearrange("p h d -> p (h d)")).then_inc(
                        o_stored[u].sem, 16)
            repeat(pool, steps, body)
            for u in range(U):
                o_stored[u].wait_all(pool, 16 * steps)
    g.close()


def mem_sample(g, z, q0, mem_kt, mem_v, cat):
    nc = g.nc
    g.open("mem_sample")
    HT = H_MEM * DS
    mk_t = g.sb("mk_t", [P, DB, 2, N_MEM])
    mv = g.sb("mv", [P, DB, MT, N_MEM])
    q = g.sb("q", [P, N_MEM])
    qb = g.sb("qb", [P, 2, DB, H_MEM, DS])
    p = g.sb("p", [HT, 2, N_MEM])
    p_t = g.sb("p_t", [P, 2, MT, HT])
    st = g.sb("st", [HT, 2, 3])
    o = g.sb("o", [HT, DB, N_MEM])
    (mem_in, q_in, zeroed, q_turned, q_ready, scores_in, max_done, exp_done, p_turned, p_ready, o_in, rsum_done,
     o_done) = (g.sem(x) for x in (
         "mem_in q_in zeroed q_turned q_ready scores_in max_done exp_done p_turned p_ready o_in rsum_done "
         "o_done").split())
    o_stored = g.pool_sem("o_stored")
    with nc.Block() as block:
        @block.sync
        def _(sp):
            g.clear_old(sp)
            sp.dma_start(q[0:NS], at(z, PT)[0:NS, q0:q0 + N_MEM]).then_inc(q_in, 16)
            sp.dma_start(mk_t[:], mem_kt.rearrange("b p c m -> p b c m")).then_inc(mem_in, 16)
            sp.dma_start(mv[:], mem_v.rearrange("b (m p) c -> p b m c", p=P)).then_inc(mem_in, 16)

        @block.tensor
        def _(pe):
            pe.wait_ge(q_in, 16)
            for c in range(2):
                last = nc.tensor.transpose(g.ps[:, 0, c * NS:c * NS + NS], q[0:NS, c * P:c * P + P],
                                           g.ident[0:NS, 0:NS])
            last.then_inc(q_turned, 1)
            pe.wait_ge(q_ready, 1)
            pe.wait_ge(mem_in, 32)

            def scores(b):
                need(pe, exp_done, b - 1)
                for c in range(2):
                    last = nc.tensor.matmul(g.ps[0:HT, 1 + b % 2, 0:N_MEM], qb[:, c, b], mk_t[:, b, c],
                                            start=(c == 0), stop=(c == 1))
                last.then_inc(scores_in, 1)

            scores(0)
            for b in range(DB):
                if b + 1 < DB:
                    scores(b + 1)
                pe.wait_ge(exp_done, b + 1)
                need(pe, p_ready, b - 1)
                for m in range(MT):
                    last = nc.tensor.transpose(g.ps[:, 3 + b % 2, m * HT:m * HT + HT], p[:, b % 2, m * P:m * P + P],
                                               g.ident[0:HT, 0:HT])
                last.then_inc(p_turned, 1)
                pe.wait_ge(p_ready, b + 1)
                need(pe, o_done, b - 1)
                for m in range(MT):
                    last = nc.tensor.matmul(g.ps[0:HT, 5 + b % 2, 0:N_MEM], p_t[:, b % 2, m], mv[:, b, m],
                                            start=(m == 0), stop=(m == MT - 1))
                last.then_inc(o_in, 1)

        @block.scalar
        def _(act):
            act.wait_ge(q_turned, 1)
            act.wait_ge(zeroed, 1)
            for h in range(H_MEM):
                half = slice((h % 2) * DH, (h % 2) * DH + DH)
                last = nc.scalar.activation(
                    qb[half, h // 2, :, h], g.ps[half, 0, (h // 2) * NS:(h // 2) * NS + NS].rearrange(
                        "p (b t) -> p b t", b=DB), ACT.Copy, scale=DH ** -0.5)
            last.then_inc(q_ready, 1)
            for b in range(DB):
                act.wait_ge(max_done, b + 1)
                need(act, p_turned, b - 1)
                need(act, rsum_done, b - 1)
                nc.scalar.activation(p[:, b % 2], g.ps[0:HT, 1 + b % 2, 0:N_MEM], ACT.Exp, bias=st[:, b % 2, 0:1],
                                     accum_out=st[:, b % 2, 1:2]).then_inc(exp_done, 1)

        @block.vector
        def _(dve):
            nc.vector.memset(qb[:], 0.0).then_inc(zeroed, 1)

            def row_max(b):
                dve.wait_ge(scores_in, b + 1)
                need(dve, exp_done, b - 1)
                nc.vector.tensor_reduce(st[:, b % 2, 0:1], g.ps[0:HT, 1 + b % 2, 0:N_MEM], AX.X, ALU.max,
                                        negate=True).then_inc(max_done, 1)

            row_max(0)
            for b in range(DB):
                if b + 1 < DB:
                    row_max(b + 1)
                dve.wait_ge(p_turned, b + 1)
                need(dve, o_in, b - 1)
                nc.vector.tensor_copy(p_t[:, b % 2], g.ps[:, 3 + b % 2, 0:MT * HT].rearrange(
                    "p (m r) -> p m r", m=MT)).then_inc(p_ready, 1)
                dve.wait_ge(exp_done, b + 1)
                need(dve, o_done, b - 1)
                nc.vector.reciprocal(st[:, b % 2, 2:3], st[:, b % 2, 1:2]).then_inc(rsum_done, 1)
                dve.wait_ge(rsum_done, b + 1)
                dve.wait_ge(o_in, b + 1)
                nc.vector.tensor_scalar(o[:, b], g.ps[0:HT, 5 + b % 2, 0:N_MEM], st[:, b % 2, 2:3], None,
                                        ALU.mult).then_inc(o_done, 1)

        @block.gpsimd
        def _(pool):
            pool.wait_ge(o_done, DB)
            for h in range(H_MEM):
                pool.dma_start(at(cat, PT)[0:NS, NV + h * DH:NV + h * DH + DH].rearrange("(b t) d -> t b d", b=DB),
                               o[h * DS:h * DS + DS, :, h * DH:h * DH + DH]).then_inc(o_stored.sem, 16)
            o_stored.wait_all(pool, 16 * H_MEM)
    g.close()


def ffn_up(g, a, w_up, taps, state_in, y_t, state_out, rows):
    nc = g.nc
    g.open("ffn_up")
    U = 2
    steps = KF // U
    raw = g.sb("raw", [P, U, 2, KD * P])
    w_hi, w_lo = g.sb("w_hi", [P, U, 2, KD * P], F32R), g.sb("w_lo", [P, U, 2, KD * P], F32R)
    up = g.sb("up", [P, 2, SEQ + CW - 1])
    us = g.sb("us", [P, 2, DB, DS + CW - 1])
    cp = g.sb("cp", [P, 2, TOK])
    y = g.sb("y", [P, U, TOK])
    tp = g.sb("tp", [P, 2 * KF, 4])
    s_in = g.sb("s_in", [P, 2 * KF, DB, 2])
    s_new = g.sb("s_new", [P, 2 * KF, 2 + 2 * DB])
    a_hi, a_lo = a
    w_in = [g.sem(f"w_in{u}") for u in range(U)]
    y_stored = [g.pool_sem(f"y_stored{u}") for u in range(U)]
    (tables_in, zeroed, hi_done, lo_done, u_in, u_copied, state_set, tap0, tap1, tap2, gelu_done, y_done, state_kept,
     ) = (g.sem(x) for x in ("tables_in zeroed w_hi_done w_lo_done u_in u_copied state_set tap0 tap1 tap2 "
                                         "gelu_done y_done state_kept").split())
    state_stored = g.pool_sem("state_stored")
    SPANS = [(0, 364), (364, 364), (728, TOK - 728)]
    made = Rows(g, a, bank=lambda t, j: 6 + j, slots=4, **rows)
    SPAN_TILES = TILES // len(SPANS)
    sample = lambda x: x[:, SEQ:TOK].rearrange("p (b t) -> p b t", b=DB)

    with nc.Block() as block:
        @block.sync
        def _(sp):
            g.clear_old(sp)
            for t in range(2):
                made.load(sp, t)
            sp.dma_start(tp[:], taps).then_inc(tables_in, 16)
            sp.dma_start(s_in[:], state_in).then_inc(tables_in, 16)

            def body(i):
                for u in range(U):
                    need(sp, lo_done, i * U + u - U + 1)
                    sp.dma_start(raw[:, u], at(w_up, i * U + u)).then_inc(w_in[u], 16)
                    if first(i):
                        for t in ((2, 3), range(4, TILES))[u]:
                            made.load(sp, t)
            repeat(sp, steps, body)

        @block.scalar
        def _(act):
            act.wait_ge(zeroed, 1)

            def split(f, i, u):
                act.wait_ge(w_in[u], 16 * i + 16)
                need(act, u_in, 2 * (f - U) + 2)
                nc.scalar.activation(w_hi[:, u], raw[:, u], ACT.Copy).then_inc(hi_done, 1)

            def body(i):
                for u in range(U):
                    f = i * U + u
                    if not last_of(f, KF):
                        split(f + 1, i + u, 1 - u)
                    for x in range(2):
                        act.wait_ge(u_in, 2 * f + x + 1)
                        need(act, tap2, 4 * (f - 1) + 2 * x + 2)
                        need(act, state_kept, 4 * (f - 1) + 2 * x + 2)
                        for j, (c0, cn) in enumerate(SPANS):
                            cn = min(cn, SEQ - c0)
                            nc.scalar.activation(up[:, x, CW - 1 + c0:CW - 1 + c0 + cn],
                                                 g.ps[:, 3 * x + j, 0:cn], ACT.Copy).then_inc(u_copied, 1)
                        nc.scalar.activation(us[:, x, :, CW - 1:], g.ps[:, 3 * x + 2, cn:cn + NS].rearrange(
                            "p (b t) -> p b t", b=DB), ACT.Copy).then_inc(u_copied, 1)
                    act.wait_ge(tap2, 4 * f + 2)
                    nc.scalar.activation(cp[:, 0], cp[:, 0], ACT.Gelu_apprx_tanh).then_inc(gelu_done, 1)
            act.wait_ge(made.eps_set, 1)
            for t in range(made.first_step, TILES):
                made.act_step(act, t)
                if t == 0:
                    split(0, 0, 0)
            repeat_ahead(act, steps, body)
            made.stored(act)

        @block.vector
        def _(dve):
            nc.vector.memset(up[:, :, 0:CW - 1], 0.0).then_inc(zeroed, 1)
            made.dve_start(dve)

            def split(f, u):
                dve.wait_ge(hi_done, f + 1)
                nc.vector.tensor_tensor(w_lo[:, u], raw[:, u], w_hi[:, u].bitcast(F32), ALU.subtract).then_inc(
                    lo_done, 1)

            def body(i):
                for u in range(U):
                    f = i * U + u
                    if not last_of(f, KF):
                        split(f + 1, 1 - u)
                    for x in range(2):
                        ch = f + x * KF
                        tap = lambda j: tp[:, bass.ds(ch, 1), j]
                        dve.wait_ge(u_copied, 8 * f + 4 * x + 4)
                        dve.wait_ge(state_set, 2 * f + x + 1)
                        if x == 0:
                            need(dve, y_done, f)
                        parts = ((cp[:, x, 0:SEQ], lambda j: up[:, x, j:j + SEQ]),
                                 (sample(cp[:, x]), lambda j: us[:, x, :, j:j + DS]))
                        for out, src in parts:
                            nc.vector.tensor_scalar(out, src(0), tap(0), tap(3), ALU.mult, ALU.add).then_inc(tap0, 1)
                        for j, prev, done in ((1, tap0, tap1), (2, tap1, tap2)):
                            for s, (out, src) in enumerate(parts):
                                dve.wait_ge(prev, 4 * f + 2 * x + s + 1)
                                nc.vector.scalar_tensor_tensor(out=out, in0=src(j), scalar=tap(j), in1=out,
                                                               op0=ALU.mult, op1=ALU.add).then_inc(done, 1)
                    dve.wait_ge(gelu_done, f + 1)
                    dve.wait_ge(tap2, 4 * f + 4)
                    need(dve, y_stored[u], 16 * i)
                    nc.vector.tensor_tensor(y[:, u], cp[:, 0], cp[:, 1], ALU.mult).then_inc(y_done, 1)
            for t in range(made.first_step, TILES):
                made.dve_step(dve, t)
                if t == 0:
                    split(0, 0)
            dve.wait_ge(zeroed, 1)
            dve.wait_ge(tables_in, 32)
            repeat_ahead(dve, steps, body)

        @block.tensor
        def _(pe):
            def products(u, x, k, spans):
                wh, wl = (w[:, u, x, k * P:k * P + P] for w in (w_hi, w_lo))
                for n, (w, m) in enumerate(((wh, a_lo), (wh, a_hi), (wl, a_hi))):
                    for j in spans:
                        c0, cn = SPANS[j]
                        last = nc.tensor.matmul(g.ps[:, 3 * x + j, 0:cn], w, m[:, k, c0:c0 + cn],
                                                start=(k == 0 and n == 0), stop=(k == KD - 1 and n == 2))
                return last

            def chunk(f, u):
                pe.wait_ge(lo_done, f + 1)
                for x in range(2):
                    need(pe, u_copied, 8 * (f - 1) + 4 * x + 4)
                    for k in range(KD):
                        last = products(u, x, k, range(len(SPANS)))
                    last.then_inc(u_in, 1)

            def first_chunk():
                for t in range(SPAN_TILES):
                    made.turn(pe, t)
                for j in range(len(SPANS)):
                    for t in range(j * SPAN_TILES + 1, (j + 1) * SPAN_TILES if j else 0):
                        made.turn(pe, t)
                    pe.wait_ge(made.rows_lo_done, 2 * (j + 1) * SPAN_TILES)
                    pe.wait_ge(lo_done, 1)
                    for x in range(2):
                        for k in range(KD):
                            last = products(0, x, k, [j])
                        if j == len(SPANS) - 1:
                            last.then_inc(u_in, 1)
                        elif x == 0:
                            made.turn(pe, (j + 1) * SPAN_TILES)

            def body(i):
                for u in range(U):
                    if first(i) and u == 0:
                        first_chunk()
                    else:
                        chunk(i * U + u, u)
            repeat(pe, steps, body)

        @block.gpsimd
        def _(pool):
            pool.wait_ge(tables_in, 32)

            def body(i):
                for u in range(U):
                    f = i * U + u
                    for x in range(2):
                        ch = bass.ds(f + x * KF, 1)
                        need(pool, tap2, 4 * (f - 1) + 2 * x + 2)
                        need(pool, state_kept, 4 * (f - 1) + 2 * x + 2)
                        nc.gpsimd.tensor_copy(us[:, x, :, 0:2],
                                              s_in[:, ch].rearrange("p o b j -> p (o b) j")).then_inc(state_set, 1)
                    for x in range(2):
                        ch = bass.ds(f + x * KF, 1)
                        pool.wait_ge(u_copied, 8 * f + 4 * x + 4)
                        nc.gpsimd.tensor_copy(s_new[:, ch, 0:2].rearrange("p o j -> p (o j)"),
                                              up[:, x, SEQ:SEQ + 2]).then_inc(state_kept, 1)
                        nc.gpsimd.tensor_copy(s_new[:, ch, 2:].rearrange("p o (b j) -> p (o b) j", j=2),
                                              us[:, x, :, DS:DS + 2]).then_inc(state_kept, 1)
                    pool.wait_ge(y_done, f + 1)
                    pool.dma_start(at(y_t, f)[:, 0:TOK], y[:, u]).then_inc(y_stored[u].sem, 16)
            repeat(pool, steps, body)
            pool.wait_ge(state_kept, 4 * KF)
            pool.dma_start(state_out, s_new[:]).then_inc(state_stored.sem, 16)
            state_stored.wait_all(pool, 16)
            for u in range(U):
                y_stored[u].wait_all(pool, 16 * steps)
    g.close()


def ffn_down(g, y_t, w_down, outs):
    nc = g.nc
    g.open("ffn_down")
    N = D // NC
    K2 = 2
    W = KF // K2
    WS = 4
    raw = g.sb("raw", [P, WS, K2, NC])
    w_hi, w_lo = g.sb("w_hi", [P, KF, NC], F32R), g.sb("w_lo", [P, KF, NC], F32R)
    yr = g.sb("yr", [P, 2, KF, P])
    y_hi, y_lo = g.sb("y_hi", [P, 2, KF, P], F32R), g.sb("y_lo", [P, 2, KF, P], F32R)
    z = g.sb("z", [P, 2, NC])
    w_in = [g.sem(f"w_in{s}") for s in range(WS)]
    y_in = [g.sem(f"y_in{s}") for s in range(2)]
    stored = [g.pool_sem(f"stored{s}") for s in range(2)]
    w_hi_done, w_lo_done, w_used = g.sem("w_hi_done"), g.sem("w_lo_done"), g.sem("w_used")
    y_hi_done, y_lo_done, z_done, z_out = g.sem("y_hi_done"), g.sem("y_lo_done"), g.sem("z_done"), g.sem("z_copied")
    T1 = TILES - 1
    FIRST, REST = range(KF // 2 + 1), range(KF // 2 + 1, KF)
    items = [(n, t) for n in range(N) for t in range(TILES)]

    def used(x):
        n, t = items[x]
        return (z_done, n * T1 + t + 1) if t < T1 else (w_used, (n + 1) * KF)

    with nc.Block() as block:
        @block.sync
        def _(sp):
            g.clear_old(sp)

            def load_w(n, js):
                for j in js:
                    x = n * W + j
                    if x >= WS:
                        sp.wait_ge(w_lo_done, (x - WS + 1) * K2)
                    sp.dma_start(raw[:, x % WS], w_down[n, :, j * K2:j * K2 + K2, :]).then_inc(w_in[x % WS], 16)

            def load_y(x):
                if x >= 2:
                    sp.wait_ge(y_lo_done, x - 1)
                sp.dma_start(yr[:, x % 2], y_t[:, :, items[x][1] * P:items[x][1] * P + P].rearrange(
                    "k p c -> p k c")).then_inc(y_in[x % 2], 16)

            for x, (n, t) in enumerate(items):
                early = WS if t == 0 and n > 0 else 0
                load_w(n, range(early))
                load_y(x)
                if t == 0:
                    load_w(n, range(early, W // 2 + 1))
                if t == 1:
                    load_w(n, range(W // 2 + 1, W))

        @block.scalar
        def _(act):
            def split_w(n, ks):
                for k in ks:
                    x = n * W + k // K2
                    act.wait_ge(w_in[x % WS], 16 * (x // WS + 1))
                    need(act, w_used, (n - 1) * KF + k + 1)
                    nc.scalar.activation(w_hi[:, k], raw[:, x % WS, k % K2], ACT.Copy).then_inc(w_hi_done, 1)

            def split_y(x):
                act.wait_ge(y_in[x % 2], 16 * (x // 2 + 1))
                if x >= 2:
                    act.wait_ge(*used(x - 2))
                nc.scalar.activation(y_hi[:, x % 2], yr[:, x % 2], ACT.Copy).then_inc(y_hi_done, 1)

            def evac(x):
                act.wait_ge(*used(x))
                need(act, stored[x % 2], 16 * (x // 2))
                nc.scalar.activation(z[:, x % 2], g.ps[:, x % 8], ACT.Copy).then_inc(z_out, 1)

            for x, (n, t) in enumerate(items):
                split_y(x)
                if t == 0:
                    split_w(n, FIRST)
                if t == 1:
                    split_w(n, REST)
                if x > 0:
                    evac(x - 1)
            evac(len(items) - 1)

        @block.vector
        def _(dve):
            def split_w(n, ks):
                for k in ks:
                    x = n * W + k // K2
                    dve.wait_ge(w_hi_done, n * KF + k + 1)
                    nc.vector.tensor_tensor(w_lo[:, k], raw[:, x % WS, k % K2], w_hi[:, k].bitcast(F32),
                                            ALU.subtract).then_inc(w_lo_done, 1)

            def split_y(x):
                dve.wait_ge(y_hi_done, x + 1)
                nc.vector.tensor_tensor(y_lo[:, x % 2], yr[:, x % 2], y_hi[:, x % 2].bitcast(F32),
                                        ALU.subtract).then_inc(y_lo_done, 1)

            for x, (n, t) in enumerate(items):
                split_y(x)
                if t == 0:
                    split_w(n, FIRST)
                if t == 1:
                    split_w(n, REST)

        @block.tensor
        def _(pe):
            for x, (n, t) in enumerate(items):
                pe.wait_ge(y_lo_done, x + 1)
                need(pe, z_out, x - 7)
                for k in range(KF):
                    if t == 0:
                        pe.wait_ge(w_lo_done, n * KF + k + 1)
                    o = g.ps[:, x % 8]
                    yh, yl = y_hi[:, x % 2, k], y_lo[:, x % 2, k]
                    nc.tensor.matmul(o, yl, w_hi[:, k], start=(k == 0), stop=False)
                    nc.tensor.matmul(o, yh, w_hi[:, k], start=False, stop=False)
                    last = nc.tensor.matmul(o, yh, w_lo[:, k], start=False, stop=(k == KF - 1))
                    if t == T1:
                        last.then_inc(w_used, 1)
                if t < T1:
                    last.then_inc(z_done, 1)

        @block.gpsimd
        def _(pool):
            for x, (n, t) in enumerate(items):
                pool.wait_ge(z_out, x + 1)
                pool.dma_start(outs(n, t)[0][0], z[:, x % 2]).then_inc(stored[x % 2].sem, 16)
            for s in range(2):
                stored[s].wait_all(pool, 16 * len(items) // 2)
    g.close()


def gates(g, a, w_f, b_f, logf_out, fgt):
    nc = g.nc
    g.open("gates")
    a_hi, a_lo = a
    wf = g.sb("wf", [P, KD, H_FOX])
    wh, wl = g.sb("wh", [P, KD, H_FOX], F32R), g.sb("wl", [P, KD, H_FOX], F32R)
    bias = g.sb("bias", [P, H_FOX])
    W = ROWS // 3
    zt = g.sb("zt", [H_FOX, ROWS])
    x, ax, e, up, ln, d, one, q, mn, lf, tot = (g.sb(n, [P, TILES, H_FOX]) for n in (
        "x", "ax", "e", "up", "ln", "d", "one", "q", "mn", "lf", "tot"))
    rest = g.sb("rest", [P, PT, H_FOX])
    (w_in, hi_done, lo_done, zt_in, zt_done, z_done, x_done, abs_done, exp_done, up_done, ln_done, step, lf_done,
     sums_in, tot_done, rest_done) = (g.sem(s) for s in (
         "w_in hi_done lo_done zt_in zt_done z_done x_done abs_done exp_done up_done ln_done dve_step lf_done "
         "sums_in tot_done rest_done").split())
    stored = g.pool_sem("stored")
    with nc.Block() as block:
        @block.sync
        def _(sp):
            g.clear_old(sp)
            sp.dma_start(wf[:], w_f).then_inc(w_in, 16)
            sp.dma_start(bias[:], b_f).then_inc(w_in, 16)

        @block.scalar
        def _(act):
            act.wait_ge(w_in, 32)
            nc.scalar.activation(wh[:], wf[:], ACT.Copy).then_inc(hi_done, 1)
            for s in range(3):
                act.wait_ge(zt_in, s + 1)
                nc.scalar.activation(zt[:, s * W:s * W + W], g.ps[0:H_FOX, 4 + s, 0:W], ACT.Copy).then_inc(zt_done, 1)
            act.wait_ge(x_done, 1)
            nc.scalar.activation(ax[:], x[:], ACT.Abs).then_inc(abs_done, 1)
            act.wait_ge(abs_done, 1)
            nc.scalar.activation(e[:], ax[:], ACT.Exp, scale=-1.0).then_inc(exp_done, 1)
            act.wait_ge(up_done, 1)
            nc.scalar.activation(ln[:], up[:], ACT.Ln).then_inc(ln_done, 1)

        @block.tensor
        def _(pe):
            pe.wait_ge(lo_done, 1)
            for s in range(3):
                for k in range(KD):
                    ah, al = a_hi[:, k, s * W:s * W + W], a_lo[:, k, s * W:s * W + W]
                    o = g.ps[0:H_FOX, 4 + s, 0:W]
                    nc.tensor.matmul(o, wh[:, k], al, start=(k == 0), stop=False)
                    nc.tensor.matmul(o, wh[:, k], ah, start=False, stop=False)
                    last = nc.tensor.matmul(o, wl[:, k], ah, start=False, stop=(k == KD - 1))
                last.then_inc(zt_in, 1)
            pe.wait_ge(zt_done, 3)
            for t in range(TILES):
                last = nc.tensor.transpose(g.ps[:, 0, t * H_FOX:t * H_FOX + H_FOX], zt[:, t * P:t * P + P],
                                           g.ident[0:H_FOX, 0:H_FOX])
            last.then_inc(z_done, 1)
            pe.wait_ge(lf_done, 1)
            flat = lf[:, 0:PT].rearrange("p t h -> p (t h)")
            nc.tensor.matmul(g.ps[:, 1, 0:PT * H_FOX], g.later[:], flat, start=True, stop=True).then_inc(sums_in, 1)
            nc.tensor.matmul(g.ps[:, 2, 0:PT * H_FOX], g.ones[:], flat, start=True, stop=True).then_inc(sums_in, 1)

        @block.vector
        def _(dve):
            V = nc.vector
            dve.wait_ge(hi_done, 1)
            V.tensor_tensor(wl[:], wf[:], wh[:].bitcast(F32), ALU.subtract).then_inc(lo_done, 1)
            dve.wait_ge(z_done, 1)
            V.tensor_tensor(x[:], g.ps[:, 0, 0:TILES * H_FOX].rearrange("p (t h) -> p t h", h=H_FOX),
                            bc(bias[:], 1, TILES), ALU.add).then_inc(x_done, 1)
            dve.wait_ge(exp_done, 1)
            V.tensor_scalar(up[:], e[:], 1.0, None, ALU.add).then_inc(up_done, 1)
            dve.wait_ge(up_done, 1)
            V.tensor_scalar(d[:], up[:], -1.0, 1e-30, ALU.add, ALU.max).then_inc(step, 1)
            V.tensor_scalar(one[:], up[:], 1.0, None, ALU.is_equal).then_inc(step, 1)
            V.tensor_scalar(mn[:], x[:], 0.0, None, ALU.min).then_inc(step, 1)
            dve.wait_ge(step, 3)
            V.reciprocal(q[:], d[:]).then_inc(step, 1)
            dve.wait_ge(ln_done, 1)
            dve.wait_ge(step, 4)
            V.tensor_tensor(q[:], q[:], ln[:], ALU.mult).then_inc(step, 1)
            dve.wait_ge(step, 5)
            V.tensor_tensor(q[:], q[:], one[:], ALU.add).then_inc(step, 1)
            dve.wait_ge(step, 6)
            V.tensor_tensor(q[:], q[:], e[:], ALU.mult).then_inc(step, 1)
            dve.wait_ge(step, 7)
            V.tensor_tensor(lf[:], mn[:], q[:], ALU.subtract).then_inc(lf_done, 1)
            dve.wait_ge(sums_in, 2)
            V.tensor_copy(tot[:, 0:PT], g.ps[:, 2, 0:PT * H_FOX].rearrange("p (t h) -> p t h", h=H_FOX)).then_inc(
                tot_done, 1)
            V.memset(rest[:, PT - 1], 0.0).then_inc(rest_done, 1)
            dve.wait_ge(tot_done, 1)
            for t in range(PT - 2, -1, -1):
                dve.wait_ge(rest_done, PT - 1 - t)
                V.tensor_tensor(rest[:, t], rest[:, t + 1], tot[:, t + 1], ALU.add).then_inc(rest_done, 1)
            dve.wait_ge(rest_done, PT)
            V.tensor_tensor(fgt[:], g.ps[:, 1, 0:PT * H_FOX].rearrange("p (t h) -> p t h", h=H_FOX), rest[:],
                            ALU.add).then_inc(step, 1)

        @block.gpsimd
        def _(pool):
            pool.wait_ge(lf_done, 1)
            pool.dma_start(logf_out.rearrange("(t p) h -> p t h", p=P), lf[:]).then_inc(stored.sem, 16)
            stored.wait_all(pool, 16)
    g.close()


def fox_prompt(g, z, kv, fgt, cat):
    nc = g.nc
    g.open("fox_prompt")
    E = DH + 2
    q, k, v = (g.sb(n, [P, 2, PT, P]) for n in "qkv")
    qa, ka = g.sb("qa", [P, 2, PT, E]), g.sb("ka", [P, 2, PT, E])
    q_t, k_t = g.sb("q_t", [E, 2, SEQ]), g.sb("k_t", [E, 2, SEQ])
    mask = g.causal
    p = g.sb("p", [P, 2, SEQ])
    p_t = g.sb("p_t", [P, 2, PT, P])
    neg_max = g.sb("neg_max", [P, 2, 1])
    sums, rsum = g.sb("sums", [P, 2, PT]), g.sb("rsum", [P, 2, PT])
    o_t = g.sb("o_t", [DH, 2, PT, P])
    o = g.sb("o", [P, 2, PT, DH])
    qkv_in = [g.sem(f"qkv_in{s}") for s in range(2)]
    o_stored = [g.pool_sem(f"o_stored{s}") for s in range(2)]
    (ones_set, aug_done, turned, t_ready, scores_in, masked, max_done, exp_done, p_turned, p_ready, o_in, ot_ready,
     o_turned, rsum_done, o_done) = (g.sem(x) for x in (
         "ones_set aug_done turned t_ready scores_in masked max_done exp_done p_turned p_ready o_in ot_ready "
         "o_turned rsum_done o_done").split())
    groups = [(i + 4) // 4 for i in range(PT)]
    before = [sum(groups[:i]) for i in range(PT)]
    G8 = sum(groups)
    CP = 2
    steps = HP // CP
    LAST = (H_FOX * PT - 1, PT - 1, 1, H_FOX - 1, HP - 1, (HP - 1) % CP)

    with nc.Block() as block:
        @block.sync
        def _(sp):
            g.clear_old(sp)

            def body(i):
                for cc in range(CP):
                    c = i * CP + cc
                    need(sp, o_in, (c - CP + 1) * 2 * PT)
                    for dst, src, c0 in ((q, z, 0), (k, kv, 0), (v, kv, NF)):
                        sp.dma_start(dst[:, cc], at(src[0:SEQ, c0:c0 + NF].rearrange(
                            "(t p) (c d) -> c p t d", p=P, d=P), c)).then_inc(qkv_in[cc], 16)
            repeat(sp, steps, body)

        def setup_pe(pe, h, s, r):
            pe.wait_ge(aug_done, 2 * h + r // 2 + 1)
            need(pe, t_ready, 4 * h + r)
            if r == 0:
                need(pe, o_done, h - 1)
            rows = (qa, ka)[r // 2]
            for x in range(4):
                last = nc.tensor.transpose(g.ps[0:E, 0, x * P:x * P + P], rows[:, s, 4 * (r % 2) + x], g.ident[:])
            last.then_inc(turned, 1)

        def before_that(n, b, s, h, c, cc):
            return (n - 1, b - 1, s, h, c, cc) if b else (n - 1, PT - 1, 1 - s, h - 1, c if s else c - 1,
                                                          cc if s else 1 - cc)

        def turned_at(b, h):
            return (h * G8 if b >= 0 else (h - 1) * G8) + before[b % PT] + groups[b % PT]

        def walk(eng, body_of_item, ahead, at_mid=None, at_start=None, late=None):
            def body(i):
                for cc in range(CP):
                    for s in range(2):
                        h = (i * CP + cc) * 2 + s
                        for b in range(PT):
                            n = h * PT + b
                            if b == 1 and at_start and not last_of(h, H_FOX):
                                at_start(h + 1, 1 - s, i + (cc + s) // 2, (cc + s) % 2)
                            if b == 2 and late and not first(h):
                                late(h - 1, 1 - s, i * CP + cc - (1 - s))
                            if b in range(3, 7) and at_mid and not last_of(h, H_FOX):
                                at_mid(h + 1, 1 - s, b - 3)
                            if not last_of(n, H_FOX * PT):
                                ahead(n + 1, (b + 1) % PT, *((s, h) if b + 1 < PT else (1 - s, h + 1)))
                            body_of_item(n, b, s, h, i * CP + cc, cc)
            repeat_ahead(eng, steps, body)

        @block.tensor
        def _(pe):
            for r in range(4):
                setup_pe(pe, 0, 0, r)

            def scores(n, b, s, h):
                pe.wait_ge(t_ready, 4 * h + 4)
                need(pe, exp_done, n - 1)
                w = (b + 1) * P
                for c0 in range(0, w, 512):
                    c1 = min(w, c0 + 512)
                    last = nc.tensor.matmul(g.ps[:, 2 + 2 * (b % 2) + c0 // 512, 0:c1 - c0], q_t[:, s, b * P:b * P + P],
                                            k_t[:, s, c0:c1], start=True, stop=True)
                last.then_inc(scores_in, 1)

            scores(0, 0, 0, 0)

            def item(n, b, s, h, c, cc):
                pe.wait_ge(exp_done, n + 1)
                gr = h * G8 + before[b]
                for r in range(groups[b]):
                    need(pe, p_ready, gr + r - 1)
                    bank = 6 + (before[b] + r) % 2
                    for x in range(min(4, b + 1 - 4 * r)):
                        j = 4 * r + x
                        last = nc.tensor.transpose(g.ps[:, bank, x * P:x * P + P], p[:, b % 2, j * P:j * P + P],
                                                   g.ident[:])
                    last.then_inc(p_turned, 1)
                if not first(n):
                    weigh(*before_that(n, b, s, h, c, cc))

            def weigh(n, b, s, h, c, cc):
                need(pe, ot_ready, n)
                for j in range(b + 1):
                    if j % 4 == 0:
                        pe.wait_ge(p_ready, h * G8 + before[b] + j // 4 + 1)
                    last = nc.tensor.matmul(g.ps[0:DH, 1, 0:P], v[:, cc, j, s * DH:s * DH + DH],
                                            p_t[:, b % 2, j], start=(j == 0), stop=(j == b))
                last.then_inc(o_in, 1)

            def turn_o(h, s, c):
                pe.wait_ge(ot_ready, h * PT + PT)
                if not last_of(h, H_FOX):
                    pe.wait_ge(t_ready, 4 * h + 8)
                for b in range(PT):
                    last = nc.tensor.transpose(g.ps[:, 0, b * DH:b * DH + DH], o_t[:, s, b], g.ident[0:DH, 0:DH])
                last.then_inc(o_turned, 1)

            walk(pe, item, scores, at_mid=lambda h, s, r: setup_pe(pe, h, s, r), late=turn_o)
            weigh(*LAST)
            turn_o(H_FOX - 1, 1, HP - 1)

        @block.scalar
        def _(act):
            act.wait_ge(ones_set, 2)

            def augment(h, s, i, cc):
                need_all(act, (qkv_in[cc], 48 * i + 48), (turned, 4 * (h - 1)))
                half = slice(s * DH, s * DH + DH)
                f = fgt[:, :, bass.ds(h, 1)].rearrange("p t o -> p (t o)")
                nc.scalar.activation(qa[:, s, :, 0:DH], q[:, cc, :, half], ACT.Copy, scale=DH ** -0.5)
                nc.scalar.activation(qa[:, s, :, DH + 1], f, ACT.Copy, scale=-1.0).then_inc(aug_done, 1)
                nc.scalar.activation(ka[:, s, :, 0:DH], k[:, cc, :, half], ACT.Copy)
                nc.scalar.activation(ka[:, s, :, DH], f, ACT.Copy).then_inc(aug_done, 1)

            def setup(h, s, r):
                act.wait_ge(turned, 4 * h + r + 1)
                if r == 0:
                    need(act, scores_in, (h - 1) * PT)
                dst = (q_t, k_t)[r // 2]
                nc.scalar.activation(dst[:, s, (r % 2) * 512:(r % 2) * 512 + 512], g.ps[0:E, 0, :],
                                     ACT.Copy).then_inc(t_ready, 1)

            augment(0, 0, 0, 0)
            for r in range(4):
                setup(0, 0, r)

            def item(n, b, s, h, c, cc):
                act.wait_ge(max_done, n + 1)
                need(act, p_turned, turned_at(b - 2, h))
                if b == 0:
                    need(act, rsum_done, h - 1)
                nc.scalar.activation(p[:, b % 2, 0:(b + 1) * P], g.ps[:, 2 + 2 * (b % 2):4 + 2 * (b % 2), :].rearrange(
                    "p a c -> p (a c)")[:, 0:(b + 1) * P], ACT.Exp, bias=neg_max[:, b % 2],
                                     accum_out=sums[:, s, b:b + 1]).then_inc(exp_done, 1)
            walk(act, item, lambda *_: None, setup, augment)

        @block.vector
        def _(dve):
            nc.vector.memset(qa[:, :, :, DH], 1.0).then_inc(ones_set, 1)
            nc.vector.memset(ka[:, :, :, DH + 1], 1.0).then_inc(ones_set, 1)

            def row_max(n, b, s, h):
                dve.wait_ge(scores_in, n + 1)
                flat = g.ps[:, 2 + 2 * (b % 2):4 + 2 * (b % 2), :].rearrange("p a c -> p (a c)")
                diag = flat[:, b * P:b * P + P]
                nc.vector.tensor_tensor(diag, diag, mask[:], ALU.add).then_inc(masked, 1)
                dve.wait_ge(masked, n + 1)
                need(dve, exp_done, n - 1)
                nc.vector.tensor_reduce(neg_max[:, b % 2], flat[:, 0:(b + 1) * P], AX.X, ALU.max,
                                        negate=True).then_inc(max_done, 1)

            row_max(0, 0, 0, 0)

            def item(n, b, s, h, c, cc):
                gr = h * G8 + before[b]
                for r in range(groups[b]):
                    dve.wait_ge(p_turned, gr + r + 1)
                    need(dve, o_in, n - 1)
                    m = min(4, b + 1 - 4 * r)
                    bank = 6 + (before[b] + r) % 2
                    nc.vector.tensor_copy(p_t[:, b % 2, 4 * r:4 * r + m], g.ps[:, bank, 0:m * P].rearrange(
                        "p (x r) -> p x r", x=m)).then_inc(p_ready, 1)
                if not first(n):
                    keep(*before_that(n, b, s, h, c, cc))

            def keep(n, b, s, h, c, cc):
                dve.wait_ge(o_in, n + 1)
                if b == 0:
                    need(dve, o_turned, h - 1)
                nc.vector.tensor_copy(o_t[:, s, b], g.ps[0:DH, 1, 0:P]).then_inc(ot_ready, 1)

            def divide(h, s, c):
                dve.wait_ge(exp_done, h * PT + PT)
                nc.vector.reciprocal(rsum[:, s], sums[:, s]).then_inc(rsum_done, 1)
                dve.wait_ge(rsum_done, h + 1)
                dve.wait_ge(o_turned, h + 1)
                need(dve, o_stored[s], 16 * c)
                nc.vector.tensor_tensor(o[:, s], g.ps[:, 0, :].rearrange("p (t d) -> p t d", t=PT),
                                        bc(rsum[:, s], 2, DH), ALU.mult).then_inc(o_done, 1)
            walk(dve, item, row_max, late=divide)
            keep(*LAST)
            divide(H_FOX - 1, 1, HP - 1)

        @block.gpsimd
        def _(pool):
            def body(i):
                for cc in range(CP):
                    for s in range(2):
                        h = (i * CP + cc) * 2 + s
                        if not first(h):
                            store(pool, h - 1, 1 - s)

            def store(pool, h, s):
                pool.wait_ge(o_done, h + 1)
                pool.dma_start(at(cat[0:SEQ, 0:NF].rearrange("(t p) (h d) -> h p t d", p=P, d=DH), h),
                               o[:, s]).then_inc(o_stored[s].sem, 16)
            repeat(pool, steps, body)
            store(pool, H_FOX - 1, 1)
            for s in range(2):
                o_stored[s].wait_all(pool, 16 * HP)
    g.close()


def page_gates(g, pages, cache_f, logf, t_in, fg_out):
    nc = g.nc
    g.open("page_gates")
    NP = cache_f.shape[1]
    R = DB * PAGES
    ids, idf = g.sb("ids", [P, R], I32), g.sb("idf", [P, R])
    phys = g.sb("phys", [P, NP])
    lp = g.sb("lp", [P, NP, PAGE * H_FOX])
    hot = g.sb("hot", [P, NP, R])
    pp, pt, off = g.sb("pp", [P, NP, H_FOX]), g.sb("pt", [P, 2, H_FOX]), g.sb("off", [P, 2, H_FOX])
    lf, fg = g.sb("lf", [P, H_FOX, R]), g.sb("fg", [P, 2, H_FOX, PAGE])
    lfs = g.sb("lfs", [NS, H_FOX])
    later_pages, batch_sel = g.sb("later_pages", [P, P]), g.sb("batch_sel", [NS, 2, P])
    (ids_in, tables_in, pages_in, f_done, hot_done, pp_done, pt_in, pt_done, off_in, off_done, lf_in, lf_done, fg_in,
     fg_done, stored) = (g.sem(n) for n in (
         "ids_in tables_in pages_in f_done hot_done pp_done pt_in pt_done off_in off_done lf_in lf_done fg_in "
         "fg_done stored").split())

    with nc.Block() as block:
        @block.sync
        def _(sp):
            g.clear_old(sp)
            sp.dma_start(ids[:], pages.broadcast_to([P, R])).then_inc(ids_in, 16)
            for dst, src in ((phys, t_in["phys"]), (later_pages, t_in["later_pages"]), (batch_sel, t_in["batch_sel"]),
                             (lfs, logf[SEQ:SEQ + NS])):
                sp.dma_start(dst[:], src).then_inc(tables_in, 16)
            sp.dma_start(lp[:], cache_f).then_inc(pages_in, 16)
            for x in range(2):
                sp.wait_ge(fg_done, 2 * H_FOX - 1 + x)
                sp.dma_start(fg_out.rearrange("h (x b) (g k) -> x (b g) h k", x=2, k=PAGE)[x], fg[:, x]).then_inc(
                    stored, 16)
            sp.wait_ge(stored, 32)

        @block.vector
        def _(dve):
            V = nc.vector
            dve.wait_ge(ids_in, 16)
            V.tensor_copy(idf[:], ids[:]).then_inc(f_done, 1)
            dve.wait_ge(f_done, 1)
            dve.wait_ge(tables_in, 64)
            for x in range(NP):
                V.tensor_scalar(hot[:, x], idf[:], phys[:, x:x + 1], None, ALU.is_equal).then_inc(hot_done, 1)
            dve.wait_ge(pages_in, 16)
            for x in range(NP):
                V.tensor_reduce(pp[:, x], lp[:, x].rearrange("p (k h) -> p h k", h=H_FOX), AX.X,
                                ALU.add).then_inc(pp_done, 1)
            dve.wait_ge(pt_in, 1)
            V.tensor_copy(pt[:], g.ps[:, 0, 0:2 * H_FOX].rearrange("p (a h) -> p a h", a=2)).then_inc(pt_done, 1)
            dve.wait_ge(off_in, 1)
            V.tensor_copy(off[:], g.ps[:, 1, 0:2 * H_FOX].rearrange("p (a h) -> p a h", a=2)).then_inc(off_done, 1)
            dve.wait_ge(off_done, 1)
            for h in range(H_FOX):
                dve.wait_ge(fg_in, h + 1)
                for half in range(2):
                    V.tensor_scalar(fg[:, half, h], g.ps[:, 6 + h % 2, half * P:half * P + P], off[:, half, h:h + 1],
                                    None, ALU.add).then_inc(fg_done, 1)

        @block.scalar
        def _(act):
            for h in range(H_FOX):
                act.wait_ge(lf_in, h + 1)
                nc.scalar.activation(lf[:, h], g.ps[:, 2 + h % 4, 0:R], ACT.Copy).then_inc(lf_done, 1)

        @block.tensor
        def _(pe):
            pe.wait_ge(hot_done, NP)
            pe.wait_ge(pp_done, NP)
            for half in range(2):
                for x in range(NP):
                    last = nc.tensor.matmul(g.ps[:, 0, half * H_FOX:half * H_FOX + H_FOX],
                                            hot[:, x, half * P:half * P + P], pp[:, x], start=(x == 0),
                                            stop=(x == NP - 1))
            last.then_inc(pt_in, 1)

            def gather(h):
                need(pe, lf_done, h - 3)
                for x in range(NP):
                    last = nc.tensor.matmul(g.ps[:, 2 + h % 4, 0:R],
                                            lp[:, x].rearrange("p (k h) -> p h k", h=H_FOX)[:, h], hot[:, x],
                                            start=(x == 0), stop=(x == NP - 1))
                last.then_inc(lf_in, 1)
            gather(0)
            pe.wait_ge(pt_done, 1)
            for half in range(2):
                nc.tensor.matmul(g.ps[:, 1, half * H_FOX:half * H_FOX + H_FOX], later_pages[:], pt[:, half],
                                 start=True, stop=False)
                last = nc.tensor.matmul(g.ps[:, 1, half * H_FOX:half * H_FOX + H_FOX], batch_sel[:, half], lfs[:],
                                        start=False, stop=True)
            last.then_inc(off_in, 1)
            for h in range(H_FOX):
                if h + 1 < H_FOX:
                    gather(h + 1)
                pe.wait_ge(lf_done, h + 1)
                need(pe, fg_done, 2 * (h - 1))
                for half in range(2):
                    last = nc.tensor.matmul(g.ps[:, 6 + h % 2, half * P:half * P + P], lf[:, h, half * P:half * P + P],
                                            g.later[:], start=True, stop=True)
                last.then_inc(fg_in, 1)
    g.close()


def fox_sample(g, z, kv, logf, pages, cache_k, cache_v, fg_in_dram, t_in, cat):
    nc = g.nc
    g.open("fox_sample")
    HT = H_FOX * DS
    KS = 16
    GP = 4
    NG = PAGES // GP
    W = GP * PAGE
    KEYS = PAGES * PAGE
    QW = HT + 2 * DS
    PIECES = ((0, 1), (1, 4), (4, NG))
    ids = g.sb("ids", [1, DB * PAGES], I32)
    kr, vr = g.sb("kr", [P, KS, HP, PAGE]), g.sb("vr", [P, KS, NF])
    fg = g.sb("fg", [HT, 2, KEYS // 2])
    qk = g.sb("qk", [NS, 2 * NF])
    qb = g.sb("qb", [P, DB, HP, 2, DS])
    kn = g.sb("kn", [P, HP, DB, DS])
    vn = g.sb("vn", [DS, DB, NF])
    lfn, lfw = g.sb("lfn", [NS, H_FOX]), g.sb("lfw", [NS, H_FOX, DS])
    later_new, new_mask = g.sb("later_new", [NS, NS]), g.sb("new_mask", [HT, DS])
    fn = g.sb("fn", [HT, DB, DS])
    own, fold = g.sb("own", [HT, NF]), g.sb("fold", [HT, DS])
    qc, kc, vc = g.sb("qc", [P, HP * QW]), g.sb("kc", [P, HP, DS]), g.sb("vc", [DS, NF])
    sc = g.sb("sc", [HT, KEYS + DS])
    gm, nm = g.sb("gm", [HT, NG + 1]), g.sb("nm", [HT, 1])
    sums, sm, rs = g.sb("sums", [HT, len(PIECES)]), g.sb("sm", [HT, 1]), g.sb("rs", [HT, 1])
    pt = g.sb("pt", [P, 2, GP + 1, HT])
    om = g.sb("om", [HT, NF])
    kin = [g.sem(f"k_in{s}") for s in range(KS)]
    vin = [g.sem(f"v_in{s}") for s in range(KS)]
    (ids_in, ids_done, tables_in, rows_in, fg_in0, fg_in1, zeroed, turned, q_set, lfw_done, fn_in, fn_done, qk_set,
     v_set, k_used, v_used, new_in, scores_out, new_out, group_max, max_done, exp_done, sm_done, rs_done, p_turned,
     p_ready, o_in, o_done, folded, back) = (g.sem(n) for n in (
         "ids_in ids_done tables_in rows_in fg_in0 fg_in1 zeroed turned q_set lfw_done fn_in fn_done qk_set v_set "
         "k_used v_used new_in scores_out new_out group_max max_done exp_done sm_done rs_done p_turned p_ready o_in "
         "o_done folded back").split())

    fg_sems = (fg_in0, fg_in1)
    stored = g.pool_sem("stored")

    def slot(j):
        return j % KS

    def fills(b, j):
        return b * (PAGES // KS) + j // KS + 1

    def piece_of(x):
        return [x < j1 for _, j1 in PIECES].index(True)

    with nc.Block() as block:
        @block.sync
        def _(sp):
            g.clear_old(sp)
            sp.dma_start(ids[:], pages).then_inc(ids_in, 16)
            sp.dma_start(qk[:, 0:NF], at(z, PT)[0:NS, 0:NF]).then_inc(rows_in, 16)
            sp.dma_start(qk[:, NF:], at(kv, PT)[0:NS, 0:NF]).then_inc(rows_in, 16)
            sp.dma_start(vn[:], at(kv, PT)[0:NS, NF:].rearrange("(b t) c -> t b c", b=DB)).then_inc(rows_in, 16)
            for dst, src in ((lfn, logf[SEQ:SEQ + NS]), (later_new, t_in["later_new"]), (new_mask, t_in["new_mask"]),
                             (own, t_in["own_head"]), (fold, t_in["fold"])):
                sp.dma_start(dst[:], src).then_inc(tables_in, 16)

            def load_fg(b, x):
                need(sp, scores_out, (b - 1) * NG + (x + 1) * NG // 2)
                sp.dma_start(fg[:, x], bc(at(fg_in_dram.rearrange("h b n -> b h n"), b)[
                    :, x * KEYS // 2:(x + 1) * KEYS // 2], 1, DS)).then_inc(fg_sems[x], 16)

            def load(ring, arrived, free, value, cache, b, j):
                page = nc.values_load(ids[0:1, bass.ds(b * PAGES + j, 1)], engines=[sp.engine], min_val=0,
                                      max_val=cache.shape[0] - 1,
                                      skip_runtime_bounds_check_because="DVE has clamped the page numbers")
                need(sp, free, value)
                sp.dma_start(ring[:, slot(j)], at_page(cache, page)).then_inc(arrived[slot(j)], 16)

            def load_k(b, j):
                load(kr, kin, k_used, b * NG + (j - KS) // GP + 1, cache_k, b, j)

            def load_v(b, j):
                load(vr, vin, v_used, b * PAGES + j - KS + 1, cache_v, b, j)

            def body(b):
                for x in range(NG):
                    if not last_of(b, DB):
                        if x % (NG // 2) == 0:
                            load_fg(b + 1, x // (NG // 2))
                        for j in range(x * GP, x * GP + GP):
                            load_k(b + 1, j)
                    for j in range(x * GP, x * GP + GP):
                        load_v(b, j)
            sp.wait_ge(ids_done, 1)
            for x in range(2):
                load_fg(0, x)
            for j in range(PAGES):
                load_k(0, j)
            repeat_ahead(sp, DB, body)

        @block.gpsimd
        def _(pool):
            nc.gpsimd.memset(qc[:], 0.0).then_inc(zeroed, 1)
            nc.gpsimd.memset(qb[:], 0.0).then_inc(zeroed, 1)
            pool.wait_ge(zeroed, 2)
            pool.wait_ge(q_set, 2)
            pool.wait_ge(rows_in, 48)

            def queries(b):
                need(pool, new_in, b)
                nc.gpsimd.tensor_copy(qc[:].rearrange("p (c w) -> p c w", w=QW)[:, :, 0:2 * DS],
                                      qb[:, bass.ds(b, 1)].rearrange("p o c f t -> p (o c) (f t)"))
                nc.gpsimd.tensor_copy(kc[:], kn[:, :, bass.ds(b, 1)].rearrange("p c o t -> p c (o t)")).then_inc(
                    qk_set, 1)

            def body(b):
                need(pool, o_in, b)
                nc.gpsimd.tensor_copy(vc[:], vn[:, bass.ds(b, 1)].rearrange("p o c -> p (o c)")).then_inc(v_set, 1)
                if not last_of(b, DB):
                    queries(b + 1)
            queries(0)
            repeat_ahead(pool, DB, body)
            pool.wait_ge(back, 2 * DB)
            pool.dma_start(at(cat, PT)[0:NS, 0:NF].rearrange("(b t) c -> t b c", b=DB), vn[:]).then_inc(stored.sem, 16)
            stored.wait_all(pool, 16)

        @block.tensor
        def _(pe):
            pe.wait_ge(rows_in, 48)
            for x in range(2):
                for c in range(HP):
                    last = nc.tensor.transpose(g.ps[:, x, c * NS:c * NS + NS], qk[:, x * NF + c * P:x * NF + c * P + P],
                                               g.ident[0:NS, 0:NS])
                last.then_inc(turned, 1)
            pe.wait_ge(lfw_done, 1)
            nc.tensor.matmul(g.ps[0:HT, 6, 0:NS], lfw[:].rearrange("p h t -> p (h t)"), later_new[:], start=True,
                             stop=True).then_inc(fn_in, 1)
            pe.wait_ge(q_set, 2)

            def own_queries(c):
                return qc[:, c * HT:c * HT + HT]

            def score(b, x):
                need(pe, scores_out, b * NG + x - 1)
                for j in range(x * GP, x * GP + GP):
                    pe.wait_ge(kin[slot(j)], 16 * fills(b, j))
                s0 = slot(x * GP)
                for c in range(HP):
                    last = nc.tensor.matmul(g.ps[0:HT, x % 2, :], own_queries(c), kr[:, s0:s0 + GP, c], start=(c == 0),
                                            stop=(c == HP - 1))
                last.then_inc(k_used, 1)

            def score_new(b):
                need(pe, back, 2 * (b - 1))
                if first(b):
                    pe.wait_ge(fn_done, 1)
                for c in range(HP):
                    last = nc.tensor.matmul(g.ps[0:HT, 6, 0:DS], own_queries(c), kc[:, c], start=(c == 0),
                                            stop=(c == HP - 1))
                last.then_inc(new_in, 1)

            def turn(b, x):
                pe.wait_ge(exp_done, len(PIECES) * b + piece_of(x) + 1)
                need(pe, p_ready, b * NG + x - 1)
                for y in range(GP):
                    last = nc.tensor.transpose(g.ps[:, 2 + x % 2, y * HT:y * HT + HT],
                                               sc[:, x * W + y * PAGE:x * W + (y + 1) * PAGE], g.ident[0:HT, 0:HT])
                if x == NG - 1:
                    last = nc.tensor.transpose(g.ps[0:DS, 2 + x % 2, GP * HT:(GP + 1) * HT], sc[:, KEYS:],
                                               g.ident[0:HT, 0:HT])
                last.then_inc(p_turned, 1)

            def weigh(b, x):
                pe.wait_ge(p_ready, b * NG + x + 1)
                if x == 0:
                    need(pe, o_done, 2 * b)
                for y in range(GP):
                    j = x * GP + y
                    pe.wait_ge(vin[slot(j)], 16 * fills(b, j))
                    for bank, c0, c1 in ((4, 0, 512), (5, 512, NF)):
                        last = nc.tensor.matmul(g.ps[0:HT, bank, 0:c1 - c0], pt[:, x % 2, y], vr[:, slot(j), c0:c1],
                                                start=(j == 0), stop=False)
                    last.then_inc(v_used, 1)
                if x == NG - 1:
                    pe.wait_ge(v_set, b + 1)
                    for bank, c0, c1 in ((4, 0, 512), (5, 512, NF)):
                        last = nc.tensor.matmul(g.ps[0:HT, bank, 0:c1 - c0], pt[0:DS, x % 2, GP], vc[:, c0:c1],
                                                start=False, stop=True)
                    last.then_inc(o_in, 1)

            def fold_o(b):
                pe.wait_ge(o_done, 2 * b + 2)
                for bank, c0, c1 in ((6, 0, 512), (7, 512, NF)):
                    last = nc.tensor.matmul(g.ps[0:DS, bank, 0:c1 - c0], fold[:], om[:, c0:c1], start=True, stop=True)
                last.then_inc(folded, 1)

            pe.wait_ge(tables_in, 80)
            pe.wait_ge(qk_set, 1)
            for x in range(NG):
                score(0, x)
            score_new(0)

            def body(b):
                if not last_of(b, DB):
                    pe.wait_ge(qk_set, b + 2)
                for x in range(NG):
                    if not last_of(b, DB):
                        score(b + 1, x)
                    turn(b, x)
                    if x == 0 and not first(b):
                        pe.wait_ge(new_out, b + 1)
                        fold_o(b - 1)
                    if x > 0:
                        weigh(b, x - 1)
                if not last_of(b, DB):
                    score_new(b + 1)
                weigh(b, NG - 1)
            repeat_ahead(pe, DB, body)
            fold_o(DB - 1)

        @block.scalar
        def _(act):
            act.wait_ge(turned, 1)
            act.wait_ge(zeroed, 2)
            for h in range(H_FOX):
                half = slice((h % 2) * DH, (h % 2) * DH + DH)
                last = nc.scalar.activation(
                    qb[half, :, h // 2, h % 2], g.ps[half, 0, (h // 2) * NS:(h // 2) * NS + NS].rearrange(
                        "p (b t) -> p b t", b=DB), ACT.Copy, scale=DH ** -0.5)
            last.then_inc(q_set, 1)
            act.wait_ge(turned, 2)
            nc.scalar.activation(kn[:].rearrange("p c b t -> p c (b t)"), g.ps[:, 1, 0:HP * NS].rearrange(
                "p (c r) -> p c r", c=HP), ACT.Copy).then_inc(q_set, 1)

            def body(b):
                act.wait_ge(max_done, b + 1)
                need(act, sm_done, b)
                for i, (x0, x1) in enumerate(PIECES):
                    cols = sc[:, x0 * W:x1 * W if x1 < NG else KEYS + DS]
                    nc.scalar.activation(cols, cols, ACT.Exp, bias=nm[:], accum_out=sums[:, i:i + 1]).then_inc(
                        exp_done, 1)
                for x in range(NG):
                    act.wait_ge(p_turned, b * NG + x + 1)
                    need(act, v_used, b * PAGES + (x - 1) * GP)
                    if x == 1:
                        need(act, o_in, b)
                    if x == NG - 1:
                        nc.scalar.activation(pt[0:DS, x % 2, GP], g.ps[0:DS, 2 + x % 2, GP * HT:(GP + 1) * HT],
                                             ACT.Copy)
                    nc.scalar.activation(pt[:, x % 2, 0:GP].rearrange("p y r -> p (y r)"),
                                         g.ps[:, 2 + x % 2, 0:GP * HT], ACT.Copy).then_inc(p_ready, 1)
                    if x == 0 and not first(b):
                        output(b - 1)

            def output(b):
                act.wait_ge(folded, b + 1)
                act.wait_ge(v_set, b + 1)
                for bank, c0, c1 in ((6, 0, 512), (7, 512, NF)):
                    nc.scalar.activation(vn[:, bass.ds(b, 1), c0:c1].rearrange("p o c -> p (o c)"),
                                         g.ps[0:DS, bank, 0:c1 - c0], ACT.Copy).then_inc(back, 1)
            repeat(act, DB, body)
            output(DB - 1)

        @block.vector
        def _(dve):
            V = nc.vector
            dve.wait_ge(ids_in, 16)
            V.tensor_scalar(ids[:], ids[:], 0, cache_k.shape[0] - 1, ALU.max, ALU.min).then_inc(ids_done, 1)
            dve.wait_ge(tables_in, 80)
            V.tensor_copy(lfw[:], bc(lfn[:], 2, DS)).then_inc(lfw_done, 1)
            dve.wait_ge(fn_in, 1)
            V.tensor_tensor(fn[:], g.ps[0:HT, 6, 0:NS].rearrange("p (b t) -> p b t", b=DB), bc(new_mask[:], 1, DB),
                            ALU.add).then_inc(fn_done, 1)
            dve.wait_ge(fn_done, 1)

            def softmax(b):
                need(dve, max_done, b)
                for x in range(NG):
                    cols = sc[:, x * W:x * W + W]
                    dve.wait_ge(k_used, b * NG + x + 1)
                    need(dve, p_turned, (b - 1) * NG + x + 1)
                    if x % (NG // 2) == 0:
                        dve.wait_ge(fg_sems[x // (NG // 2)], 16 * b + 16)
                    V.tensor_tensor(cols, g.ps[0:HT, x % 2, :],
                                    fg[:, x // (NG // 2), (x % (NG // 2)) * W:(x % (NG // 2)) * W + W],
                                    ALU.add).then_inc(scores_out, 1)
                    dve.wait_ge(scores_out, b * NG + x + 1)
                    V.tensor_reduce(gm[:, x:x + 1], cols, AX.X, ALU.max).then_inc(group_max, 1)
                dve.wait_ge(new_in, b + 1)
                V.tensor_tensor(sc[:, KEYS:], g.ps[0:HT, 6, 0:DS], fn[:, bass.ds(b, 1)].rearrange("p o t -> p (o t)"),
                                ALU.add).then_inc(new_out, 1)
                dve.wait_ge(new_out, b + 1)
                V.tensor_reduce(gm[:, NG:], sc[:, KEYS:], AX.X, ALU.max).then_inc(group_max, 1)
                dve.wait_ge(group_max, (b + 1) * (NG + 1))
                V.tensor_reduce(nm[:], gm[:], AX.X, ALU.max, negate=True).then_inc(max_done, 1)
                if not first(b):
                    divide(b - 1)
                dve.wait_ge(exp_done, len(PIECES) * (b + 1))
                V.tensor_reduce(sm[:], sums[:], AX.X, ALU.add).then_inc(sm_done, 1)
                dve.wait_ge(sm_done, b + 1)
                need(dve, o_done, 2 * b)
                V.reciprocal(rs[:], sm[:]).then_inc(rs_done, 1)

            def divide(b):
                dve.wait_ge(rs_done, b + 1)
                dve.wait_ge(o_in, b + 1)
                need(dve, folded, b)
                for bank, c0, c1 in ((4, 0, 512), (5, 512, NF)):
                    V.scalar_tensor_tensor(om[:, c0:c1], g.ps[0:HT, bank, 0:c1 - c0], rs[:], own[:, c0:c1], ALU.mult,
                                           ALU.mult).then_inc(o_done, 1)
            repeat(dve, DB, softmax)
            divide(DB - 1)
    g.close()


def at_page(cache, page):
    return cache[bass.ds(page, 1)].rearrange("o p n -> (o p) n")


def build(nc, d):
    def scratch(name, shape):
        return nc.dram_tensor(name, shape, F32, kind="Internal").ap()

    def tiles(ap):
        return ap.rearrange("(t p) c -> t p c", p=P)

    h1, h2, h3 = (tiles(scratch(f"h{i}", [ROWS, D])) for i in (1, 2, 3))
    z_a, z_b = scratch("z_a", [ROWS, NZ]), scratch("z_b", [ROWS, D])
    cat, o, f = scratch("cat", [ROWS, D]), scratch("o", [ROWS, D]), scratch("f", [ROWS, D])
    y_t = scratch("y_t", [KF, P, ROWS])
    with ExitStack() as ctx:
        g = Program(nc, ctx)
        for name in ("ident", "later", "ones", "causal"):
            t = ctx.enter_context(nc.sbuf_tensor(name, [P, P], F32))
            if name == "ident":
                g.ident = t
            elif name == "later":
                g.later = t
            elif name == "ones":
                g.ones = t
            else:
                g.causal = t
        fgt = ctx.enter_context(nc.sbuf_tensor("fgt", [P, PT, H_FOX], F32))

        def operands():
            m = ExitStack()
            a = tuple(m.enter_context(nc.sbuf_tensor(f"a_{x}{g.n}", [P, KD, ROWS], F32R)) for x in ("hi", "lo"))
            return m, a

        m, a = operands()
        g.open("setup")
        mem_t, zero = g.sb("mem_t", [P, KD, N_MEM]), g.sb("zero", [P, D])
        const_in, mem_in, hi_done, lo_done, zeroed, zero_out = (g.sem(s) for s in (
            "const_in mem_in hi_done lo_done zeroed zero_out").split())
        with nc.Block() as block:
            @block.sync
            def _(sp):
                for t, name in ((g.ident, "ident"), (g.later, "later"), (g.ones, "ones"), (g.causal, "causal")):
                    sp.dma_start(t[:], d[name]).then_inc(const_in, 16)
                sp.dma_start(mem_t[:], d["mem_t"]).then_inc(mem_in, 16)
                sp.wait_ge(zeroed, 1)
                sp.dma_start(cat[TOK:], zero[0:ROWS - TOK]).then_inc(zero_out, 16)
                for k in range(KF):
                    sp.dma_start(y_t[k, :, TOK:], zero[:, 0:ROWS - TOK]).then_inc(zero_out, 16)
                sp.wait_ge(zero_out, 16 * (KF + 1))
                sp.wait_ge(const_in, 64)

            @block.vector
            def _(dve):
                nc.vector.memset(zero[:], 0.0).then_inc(zeroed, 1)
                dve.wait_ge(hi_done, 1)
                nc.vector.tensor_tensor(a[1][:, :, 0:N_MEM], mem_t[:], a[0][:, :, 0:N_MEM].bitcast(F32),
                                        ALU.subtract).then_inc(lo_done, 1)

            @block.scalar
            def _(act):
                act.wait_ge(mem_in, 16)
                nc.scalar.activation(a[0][:, :, 0:N_MEM], mem_t[:], ACT.Copy).then_inc(hi_done, 1)
        g.close()
        mk, mv = d["mem_k"], d["mem_v"]

        def mem_outs(n, t):
            return [(at(mk, n)[t * P:t * P + P], 0, N_MEM), (at(mv, n)[t * P:t * P + P], N_MEM, NC)]
        project(g, a, d["w_mem"], DEPTH, MT, mem_outs)

        project(g, a, d["w_in_a"], NZ // NC, TILES, columns(z_a, TILES), silu=(0, 0, 0, NC, NC // 2),
                rows=dict(src=tiles(d["x"]), gain=d["g_pre"][0]))
        m.close()
        prompt = {n: d[f"p_{n}"] for n in ("dmask", "qdec", "kdec", "sdec")}
        sample = {n: d[f"s_{n}"] for n in ("dmask", "qdec", "kdec", "sdec")}
        prompt["rope"] = sample["rope"] = tiles(d["rope"])
        retention(g, tiles(z_a), prompt, tiles(cat), None, d["ret_p"], False)
        retention(g, tiles(z_a), sample, tiles(cat), d["state_ret"], d["ret_s"], True)
        mem_prompt(g, tiles(z_a), Z_M, mk[0], mv[0], tiles(cat))
        mem_sample(g, tiles(z_a), Z_M, d["cache_mem_kt"][0], d["cache_mem_v"][0], tiles(cat))
        m, a = operands()
        project(g, a, d["w_out_a"], D // NC, TILES, columns(o, TILES), rows=dict(src=tiles(cat), plain=True))

        def ffn(layer, h_in, h_mid, m, a):
            ffn_up(g, a, d["w_up"][layer], d["taps"][layer], d["state_conv"][layer], y_t, d["conv"][layer],
                   rows=dict(src=h_in, gain=d["g_pre"][2 + layer], residual=(tiles(o), d["g_mix_post"][layer]),
                             h_out=h_mid))
            m.close()
            ffn_down(g, y_t, d["w_down"][layer], columns(f, TILES))
        ffn(0, tiles(d["x"]), h1, m, a)

        m, a = operands()
        project(g, a, d["w_kv"], 2 * NF // NC, TILES, columns(d["kv"], TILES),
                rows=dict(src=h1, gain=d["g_pre"][4], residual=(tiles(f), d["g_ffn_post"][0]), h_out=h2))
        gates(g, a, d["w_f"], d["b_f"], d["logf"], fgt)
        project(g, a, d["w_in_b"], D // NC, TILES, columns(z_b, TILES), rows=dict(src=h2, gain=d["g_pre"][1]))
        m.close()
        fg = scratch("fg", [H_FOX, DB, PAGES * PAGE])
        page_gates(g, d["page_table"], d["cache_logf"], d["logf"], d, fg)
        fox_prompt(g, z_b, d["kv"], fgt, cat)
        mem_prompt(g, tiles(z_b), NF, mk[1], mv[1], tiles(cat))
        mem_sample(g, tiles(z_b), NF, d["cache_mem_kt"][1], d["cache_mem_v"][1], tiles(cat))
        fox_sample(g, tiles(z_b), tiles(d["kv"]), d["logf"], d["page_table"], d["cache_kt"], d["cache_v"], fg, d,
                   tiles(cat))
        m, a = operands()
        project(g, a, d["w_out_b"], D // NC, TILES, columns(o, TILES), rows=dict(src=tiles(cat), plain=True))
        ffn(1, h2, h3, m, a)
        normalise(g, None, h3, residual=(tiles(f), d["g_ffn_post"][1]), h_out=tiles(d["y"]))


def tables():
    import numpy as np
    f = np.float32
    t = {}
    i = np.arange(P)
    t["ident"] = np.eye(P, dtype=f)
    t["later"] = (i[:, None] > i[None, :]).astype(f)
    t["ones"] = np.ones((P, P), f)
    t["causal"] = np.where(i[None, :] <= i[:, None], 0.0, NEG).astype(f)
    inv = (f(10000.0) ** (-np.arange(32, dtype=f) / f(32))).astype(f)
    pos = np.concatenate([np.arange(SEQ), np.tile(PAGES * PAGE + np.arange(DS), DB), np.zeros(ROWS - TOK)]).astype(f)
    ang = (pos[:, None] * inv[None]).astype(f)
    t["rope"] = np.concatenate([np.cos(ang), np.sin(ang)], axis=1).astype(f)
    lg = np.log1p(-(2.0 ** (-5.0 - np.arange(H_RET))))

    def decay(name, C, B):
        R = C * B
        n, b = np.arange(R) % C, np.arange(R) // C
        same = b[:, None] == b[None, :]
        rel = n[None, :] - n[:, None]
        t[f"{name}_dmask"] = np.stack([np.where(same & (rel >= 0), np.exp(x * np.maximum(rel, 0)), 0.0) for x in lg],
                                      axis=1).astype(f)
        qd = np.zeros((P, B, 3, R))
        kd = np.zeros((R, B, H_RET))
        for h in range(H_RET):
            for x in range(B):
                rows = slice((h % 2) * DK, (h % 2) * DK + DK)
                qd[rows, x, h // 2] = np.where(b == x, np.exp(lg[h] * (n + 1.0)), 0.0)[None]
                kd[:, x, h] = np.where(b == x, np.exp(lg[h] * (C - 1.0 - n)), 0.0) * DK ** -0.5
        t[f"{name}_qdec"], t[f"{name}_kdec"] = qd.astype(f), kd.astype(f)
        t[f"{name}_sdec"] = np.exp(lg.reshape(3, 2)[:, np.arange(P) // DK].T * C).astype(f)
    decay("p", P, 1)
    decay("s", DS, DB)
    b4, pg = i // PAGES, i % PAGES
    t["later_pages"] = ((b4[:, None] == b4[None]) & (pg[:, None] > pg[None])).astype(f)
    t["batch_sel"] = np.stack([(np.arange(NS) // DS)[:, None] == (4 * x + b4)[None] for x in range(2)],
                              axis=1).astype(f)
    rows = np.arange(H_FOX * DS)
    new = np.arange(NS)
    t["later_new"] = ((new[:, None] // DS == new[None] // DS) & (new[:, None] > new[None])).astype(f)
    t["new_mask"] = np.where(np.arange(DS)[None] <= rows[:, None] % DS, 0.0, NEG).astype(f)
    t["own_head"] = (np.arange(NF)[None] // DH == rows[:, None] // DS).astype(f)
    t["fold"] = (np.arange(DS)[None] == rows[:, None] % DS).astype(f)
    return {k: np.ascontiguousarray(v) for k, v in t.items()}


def kernel(x_prompt, x_sample, mem_prompt, cache_k, cache_v, cache_logf, page_table, cache_mem_k, cache_mem_v,
           state_ret, state_conv, g_mix_pre, g_mix_post, g_ffn_pre, g_ffn_post, w_in_a, w_out_a, w_in_b, w_out_b,
           w_mem_kv, g_kv, w_kv_shared, b_f, w_ffn_up, conv_w, conv_b, w_ffn_down):
    import numpy as np
    import concourse.bacc as bacc
    from concourse.bass_utils import run_bass_kernel_spmd as run

    def chunks(w, n=NC):
        return w.reshape(-1, P, w.shape[1] // n, n).transpose(2, 1, 0, 3)

    ins = tables()
    ins["x"] = np.concatenate([x_prompt.reshape(SEQ, D), x_sample.reshape(NS, D),
                               np.zeros((ROWS - TOK, D), x_prompt.dtype)])
    ins["mem_t"] = mem_prompt[0].reshape(N_MEM, KD, P).transpose(2, 1, 0)
    n_phys = cache_k.shape[0]
    ins["cache_kt"] = cache_k.reshape(n_phys, PAGE, HP, P).transpose(0, 3, 2, 1).reshape(n_phys, P, HP * PAGE)
    ins["cache_v"] = cache_v.reshape(n_phys, PAGE, NF)
    phys = -(-n_phys // P)
    padded = np.concatenate([cache_logf.reshape(n_phys, PAGE * H_FOX),
                             np.zeros((phys * P - n_phys, PAGE * H_FOX), cache_logf.dtype)])
    ins["cache_logf"] = padded.reshape(phys, P, PAGE * H_FOX).transpose(1, 0, 2)
    ins["phys"] = (np.arange(P)[:, None] + P * np.arange(phys)[None]).astype(np.float32)
    ins["page_table"] = page_table.reshape(1, DB * PAGES)
    ins["cache_mem_kt"] = cache_mem_k.reshape(DEPTH, DB, N_MEM, 2, P).transpose(0, 1, 4, 3, 2)
    ins["cache_mem_v"] = cache_mem_v.reshape(DEPTH, DB, N_MEM, N_MEM)
    ins["state_ret"] = state_ret[0]
    ins["state_conv"] = state_conv.reshape(DEPTH, DB, 2, 2 * KF, P).transpose(0, 4, 3, 1, 2)
    for name, gain in (("g_mix_post", g_mix_post), ("g_ffn_post", g_ffn_post),
                       ("g_pre", np.concatenate([g_mix_pre, g_ffn_pre, g_kv[None]]))):
        ins[name] = gain[:, None]
    ins["w_in_a"], ins["w_out_a"] = chunks(w_in_a[0]), chunks(w_out_a[0])
    ins["w_in_b"], ins["w_out_b"] = chunks(w_in_b[0]), chunks(w_out_b[0])
    ins["w_mem"] = w_mem_kv.reshape(DEPTH, KD, P, NC).transpose(0, 2, 1, 3)
    ins["w_kv"] = chunks(w_kv_shared[:, :2 * NF])
    ins["w_f"] = w_kv_shared[:, 2 * NF:].reshape(KD, P, H_FOX).transpose(1, 0, 2)
    ins["b_f"] = np.broadcast_to(b_f[None], (P, H_FOX))
    ins["w_up"] = w_ffn_up.reshape(DEPTH, KD, P, 2, KF, P).transpose(0, 4, 2, 3, 1, 5).reshape(
        DEPTH, KF, P, 2, KD * P)
    ins["taps"] = np.concatenate([conv_w, conv_b[:, None]], axis=1).reshape(DEPTH, 4, 2 * KF, P).transpose(0, 3, 2, 1)
    ins["w_down"] = np.stack([chunks(w) for w in w_ffn_down])
    outs = {"y": (ROWS, D), "kv": (ROWS, 2 * NF), "logf": (ROWS, H_FOX), "mem_k": (DEPTH, N_MEM, N_MEM),
            "mem_v": (DEPTH, N_MEM, N_MEM), "ret_p": (1, H_RET, DK, DV), "ret_s": (DB, H_RET, DK, DV),
            "conv": (DEPTH, P, 2 * KF, 2 + 2 * DB)}

    nc = bacc.Bacc("TRN2", target_bir_lowering=False, num_devices=1)
    d, arrays = {}, {}
    for name, v in ins.items():
        arrays[f"in_{name}"] = np.ascontiguousarray(v)
        d[name] = nc.dram_tensor(f"in_{name}", v.shape, mybir.dt.from_np(v.dtype), kind="ExternalInput").ap()
    for name, shape in outs.items():
        d[name] = nc.dram_tensor(f"out_{name}", shape, F32, kind="ExternalOutput").ap()
    build(nc, d)
    r = run(nc, [arrays], core_ids=[0]).results[0]
    r = {name: r[f"out_{name}"] for name in outs}

    def heads(x, c0, *shape):
        return x[:, c0:c0 + NF].reshape(*shape, H_FOX, DH)
    k_p, v_p = (heads(r["kv"][:SEQ], c, 1, SEQ) for c in (0, NF))
    k_s, v_s = (heads(r["kv"][SEQ:TOK], c, DB, DS) for c in (0, NF))
    conv = r["conv"].transpose(0, 3, 2, 1).reshape(DEPTH, 2 + 2 * DB, 2 * DFF)
    return (r["y"][:SEQ].reshape(1, SEQ, D), r["y"][SEQ:TOK].reshape(DB, DS, D), k_p, v_p,
            r["logf"][:SEQ].reshape(1, SEQ, H_FOX), k_s, v_s, r["logf"][SEQ:TOK].reshape(DB, DS, H_FOX),
            r["mem_k"].reshape(DEPTH, 1, N_MEM, H_MEM, DH), r["mem_v"].reshape(DEPTH, 1, N_MEM, H_MEM, DH),
            r["ret_p"].reshape(1, 1, H_RET, DK, DV), r["ret_s"].reshape(1, DB, H_RET, DK, DV),
            conv[:, :2].reshape(DEPTH, 1, 2, 2 * DFF), conv[:, 2:].reshape(DEPTH, DB, 2, 2 * DFF))
```
